# Optimizing a Trainium2 kernel written in Bass

```python
import jax
import jax.numpy as jnp
from jax import lax
import numpy as np

D_MODEL = 1024
BATCH = 1
SEQ = 1024
DEPTH = 1

HEAD_DIM = 64
N_HEADS = D_MODEL // HEAD_DIM
N_HEADS_SB = N_HEADS // 2
N_HEADS_DIL = N_HEADS - N_HEADS_SB
D_SB = N_HEADS_SB * HEAD_DIM
D_DIL = N_HEADS_DIL * HEAD_DIM
D_IN = 3 * D_SB + 3 * D_DIL
D_FF = 2816
DILATED_PATTERNS = ((128, 1), (512, 4), (2048, 16))
BLOCK = 128
ROPE_THETA = 10000.0
RMS_EPS = 1e-6
HALF_STEP = 0.5

kernel_name = 'hybrid_stickbreak_dilated_macaron'

def rmsnorm(x, gain):
    xf = x.astype(jnp.float32)
    y = xf * lax.rsqrt(jnp.mean(xf * xf, axis=-1, keepdims=True) + RMS_EPS)
    return (y * gain.astype(jnp.float32)).astype(x.dtype)

def swiglu(x, w_gate, w_up, w_down):
    return (jax.nn.silu(x @ w_gate) * (x @ w_up)) @ w_down

def rotary(t, positions):
    half = t.shape[-1] // 2
    inv_freq = ROPE_THETA ** (-jnp.arange(half, dtype=jnp.float32) / half)
    ang = positions.astype(jnp.float32)[:, None] * inv_freq[None, :]
    cos, sin = jnp.cos(ang), jnp.sin(ang)
    tf = t.astype(jnp.float32)
    t1, t2 = tf[..., :half], tf[..., half:]
    return jnp.concatenate([t1 * cos - t2 * sin, t2 * cos + t1 * sin], axis=-1).astype(t.dtype)

def split_heads(t, n_heads):
    b, s, _ = t.shape
    return t.reshape(b, s, n_heads, HEAD_DIM).transpose(0, 2, 1, 3)

def merge_heads(t):
    b, h, s, d = t.shape
    return t.transpose(0, 2, 1, 3).reshape(b, s, h * d)

def stick_breaking_attention(q, k, v):
    b, h, s, d = q.shape
    nb = s // BLOCK
    scale = d ** -0.5
    qb = q.reshape(b, h, nb, BLOCK, d).transpose(2, 0, 1, 3, 4)
    key_pos = jnp.arange(s)

    def one_block(args):
        q_blk, blk = args
        q_pos = blk * BLOCK + jnp.arange(BLOCK)
        z = jnp.einsum('bhqd,bhkd->bhqk', q_blk, k, preferred_element_type=jnp.float32) * scale
        mask = key_pos[None, :] < q_pos[:, None]
        log_beta = jax.nn.log_sigmoid(z)
        log_stay = jnp.where(mask, jax.nn.log_sigmoid(-z), 0.0)
        later = lax.cumsum(log_stay, axis=3, reverse=True) - log_stay
        weights = jnp.where(mask, jnp.exp(log_beta + later), 0.0)
        return jnp.einsum('bhqk,bhkd->bhqd', weights.astype(v.dtype), v)

    out = lax.map(one_block, (qb, jnp.arange(nb)))
    return out.transpose(1, 2, 0, 3, 4).reshape(b, h, s, d)

def _dilated_pattern(q, k, v, window, dilation):
    b, h, s, d = q.shape
    span = window // dilation
    n_comp = s // dilation
    nb = n_comp // BLOCK

    def to_blocks(t):
        t = t.reshape(b, h, n_comp, dilation, d).transpose(0, 1, 3, 2, 4)
        return t.reshape(b, h, dilation, nb, BLOCK, d)

    def with_previous(t):
        prev = jnp.pad(t, ((0, 0), (0, 0), (0, 0), (1, 0), (0, 0), (0, 0)))[:, :, :, :-1]
        return jnp.concatenate([prev, t], axis=4)

    qb = to_blocks(q)
    kb = with_previous(to_blocks(k))
    vb = with_previous(to_blocks(v))
    z = jnp.einsum('bhcnqd,bhcnkd->bhcnqk', qb, kb, preferred_element_type=jnp.float32) * (d ** -0.5)
    q_idx = jnp.arange(BLOCK)[:, None] + BLOCK
    k_idx = jnp.arange(2 * BLOCK)[None, :]
    dist = q_idx - k_idx
    band = (dist >= 0) & (dist <= span)
    has_prev = (jnp.arange(nb) > 0)[:, None, None] | (k_idx >= BLOCK)[None]
    valid = band[None] & has_prev
    z = jnp.where(valid, z, -jnp.inf)
    m = jnp.max(z, axis=-1, keepdims=True)
    p = jnp.exp(z - m)
    denom = jnp.sum(p, axis=-1, keepdims=True)
    o = jnp.einsum('bhcnqk,bhcnkd->bhcnqd', p, vb.astype(jnp.float32)) / denom
    lse = m + jnp.log(denom)

    def from_blocks(t):
        e = t.shape[-1]
        t = t.reshape(b, h, dilation, n_comp, e).transpose(0, 1, 3, 2, 4)
        return t.reshape(b, h, s, e)

    return from_blocks(o), from_blocks(lse)

def dilated_mixture_attention(q, k, v):
    s = q.shape[2]
    outs, lses = [], []
    for window, dilation in DILATED_PATTERNS:
        unit = BLOCK * dilation
        s_pad = -(-s // unit) * unit
        pad = ((0, 0), (0, 0), (0, s_pad - s), (0, 0))
        o, lse = _dilated_pattern(jnp.pad(q, pad), jnp.pad(k, pad), jnp.pad(v, pad), window, dilation)
        outs.append(o[:, :, :s])
        lses.append(lse[:, :, :s])
    alpha = jax.nn.softmax(jnp.stack(lses), axis=0)
    return jnp.sum(alpha * jnp.stack(outs), axis=0).astype(q.dtype)

def token_mixer(h, w_in, sb_out_norm, dil_out_norm, w_out):
    seq = h.shape[1]
    proj = h @ w_in
    cuts = [D_SB, 2 * D_SB, 3 * D_SB, 3 * D_SB + D_DIL, 3 * D_SB + 2 * D_DIL]
    q_sb, k_sb, v_sb, q_dl, k_dl, v_dl = jnp.split(proj, cuts, axis=-1)
    positions = jnp.arange(seq)
    o_sb = stick_breaking_attention(split_heads(q_sb, N_HEADS_SB), split_heads(k_sb, N_HEADS_SB),
                                    split_heads(v_sb, N_HEADS_SB))
    o_dl = dilated_mixture_attention(rotary(split_heads(q_dl, N_HEADS_DIL), positions),
                                     rotary(split_heads(k_dl, N_HEADS_DIL), positions),
                                     split_heads(v_dl, N_HEADS_DIL))
    merged = jnp.concatenate([rmsnorm(merge_heads(o_sb), sb_out_norm),
                              rmsnorm(merge_heads(o_dl), dil_out_norm)], axis=-1)
    return merged @ w_out

def setup_inputs(seed: int = 0) -> dict:
    key = jax.random.key(seed)
    ks = jax.random.split(key, 16)

    def normal(k, shape, scale):
        return jax.random.normal(k, shape, jnp.float32) * scale

    def gain(k, shape):
        return 1.0 + 0.02 * jax.random.normal(k, shape, jnp.float32)

    dm, df = D_MODEL ** -0.5, D_FF ** -0.5
    return {
        'x': normal(ks[0], (BATCH, SEQ, D_MODEL), 1.0),
        'ffn1_norm': gain(ks[1], (DEPTH, D_MODEL)),
        'ffn1_w_gate': normal(ks[2], (DEPTH, D_MODEL, D_FF), dm),
        'ffn1_w_up': normal(ks[3], (DEPTH, D_MODEL, D_FF), dm),
        'ffn1_w_down': normal(ks[4], (DEPTH, D_FF, D_MODEL), df),
        'mix_norm': gain(ks[5], (DEPTH, D_MODEL)),
        'w_in': normal(ks[6], (DEPTH, D_MODEL, D_IN), dm),
        'sb_out_norm': gain(ks[7], (DEPTH, D_SB)),
        'dil_out_norm': gain(ks[8], (DEPTH, D_DIL)),
        'w_out': normal(ks[9], (DEPTH, D_MODEL, D_MODEL), dm),
        'ffn2_norm': gain(ks[10], (DEPTH, D_MODEL)),
        'ffn2_w_gate': normal(ks[11], (DEPTH, D_MODEL, D_FF), dm),
        'ffn2_w_up': normal(ks[12], (DEPTH, D_MODEL, D_FF), dm),
        'ffn2_w_down': normal(ks[13], (DEPTH, D_FF, D_MODEL), df),
        'final_norm': gain(ks[14], (D_MODEL,)),
    }

def reference(x, ffn1_norm, ffn1_w_gate, ffn1_w_up, ffn1_w_down, mix_norm, w_in, sb_out_norm,
              dil_out_norm, w_out, ffn2_norm, ffn2_w_gate, ffn2_w_up, ffn2_w_down, final_norm):
    for layer in range(DEPTH):
        x = x + HALF_STEP * swiglu(rmsnorm(x, ffn1_norm[layer]), ffn1_w_gate[layer],
                                   ffn1_w_up[layer], ffn1_w_down[layer])
        x = x + token_mixer(rmsnorm(x, mix_norm[layer]), w_in[layer], sb_out_norm[layer],
                            dil_out_norm[layer], w_out[layer])
        x = x + HALF_STEP * swiglu(rmsnorm(x, ffn2_norm[layer]), ffn2_w_gate[layer],
                                   ffn2_w_up[layer], ffn2_w_down[layer])
    return rmsnorm(x, final_norm)


_drawn_inputs = setup_inputs


def setup_inputs(seed=0):
    import zlib

    import numpy as np

    out = dict(_drawn_inputs(seed))
    spreads = {}
    factors = {'ffn1_norm': 5.052,
     'sb_out_norm': 5.703,
     'dil_out_norm': 5.956,
     'ffn2_norm': 8.0,
     'final_norm': 2.873}
    for name, (base, spread) in spreads.items():
        noise = np.random.default_rng([zlib.crc32(name.encode()), seed]).standard_normal(out[name].shape)
        drawn = base * np.exp(spread * noise) if base else spread * noise
        out[name] = jnp.asarray(drawn.astype(out[name].dtype))
    for name, factor in factors.items():
        out[name] = (out[name] * factor).astype(out[name].dtype)
    return out
```

```python
from contextlib import ExitStack

import numpy as np

import concourse.bass as bass
from concourse import mybir

F32 = mybir.dt.float32
F32R = mybir.dt.float32r
ALU = mybir.AluOpType
ACT = mybir.ActivationFunctionType

P = 128
SEQ = 1024
D = 1024
DFF = 2816
HEAD = 64
HALF = 512
TT = SEQ // P
KT = D // P
CH = 2
NCH = DFF // (CH * P)
PAIRS = 4
GROUP = D // 2
EPS = 1e-6
SCALE = HEAD ** -0.5
NEG = -1e30



class NormSems:
    def __init__(self, sem, tag):
        self.square = sem(f"{tag}_sum_of_squares")
        self.root = sem(f"{tag}_root")
        self.rstd = sem(f"{tag}_rstd")
        self.scaled = sem(f"{tag}_scaled")
        self.turned = sem(f"{tag}_turned")
        self.hi = sem(f"{tag}_hi_split")
        self.lo = sem(f"{tag}_lo_split")


def norm_scalar(act, s, b, x_loaded):
    for half in range(2):
        for i in range(4):
            t = 4 * half + i
            if x_loaded is not None:
                act.wait_ge(x_loaded[t], 16)
            if half == 1 and i == 0:
                act.wait_ge(s.turned, KT)
            act.activation(b.scaled[:, i, :], b.x[:, t, :], ACT.Square,
                           accum_out=b.sumsq[:, t:t + 1]).then_inc(s.square, 1)
        act.wait_ge(s.square, 4 * half + 4)
        act.activation(b.root[:, 4 * half:4 * half + 4], b.sumsq[:, 4 * half:4 * half + 4], ACT.Sqrt,
                       scale=1.0 / D, bias=b.eps[:, 0:1]).then_inc(s.root, 1)
        for j in range(KT):
            act.wait_ge(s.turned, KT * half + j + 1)
            act.activation(b.xn_hi[:, j, half * HALF:(half + 1) * HALF], b.ps[:, j, :], ACT.Copy,
                           scale=b.gain[:, j:j + 1]).then_inc(s.hi, 1)


def norm_vector(dve, s, b):
    for half in range(2):
        dve.wait_ge(s.root, half + 1)
        dve.reciprocal(b.rstd[:, 4 * half:4 * half + 4], b.root[:, 4 * half:4 * half + 4]).then_inc(s.rstd, 1)
        dve.wait_ge(s.rstd, half + 1)
        for i in range(4):
            t = 4 * half + i
            dve.tensor_scalar(b.scaled[:, i, :], b.x[:, t, :], b.rstd[:, t:t + 1], None,
                              ALU.mult).then_inc(s.scaled, 1)
        for j in range(KT):
            dve.wait_ge(s.hi, KT * half + j + 1)
            dve.scalar_tensor_tensor(out=b.xn_lo[:, j, half * HALF:(half + 1) * HALF], in0=b.ps[:, j, :],
                                     scalar=b.gain[:, j:j + 1],
                                     in1=b.xn_hi[:, j, half * HALF:(half + 1) * HALF].bitcast(F32),
                                     op0=ALU.mult, op1=ALU.subtract).then_inc(s.lo, 1)


def norm_tensor(pe, s, b):
    for half in range(2):
        for j in range(KT):
            for i in range(4):
                if j == 0:
                    pe.wait_ge(s.scaled, 4 * half + i + 1)
                if half == 1 and i == 0:
                    pe.wait_ge(s.lo, j + 1)
                last = pe.transpose(b.ps[:, j, i * P:(i + 1) * P], b.scaled[:, i, j * P:(j + 1) * P],
                                    b.ident[:, :])
            last.then_inc(s.turned, 1)


def address(eng, value):
    return value if isinstance(value, int) else eng.snap(value)



def ffn_block(nc, b, sem, tag, w_gate, w_up, w_down, x_dram, x_loaded_from, x_store, final):
    with ExitStack() as ctx:
        def sb(name, shape, dt=F32):
            return ctx.enter_context(nc.sbuf_tensor(f"{tag}_{name}", shape, dt))

        gate_raw = sb("gate_raw", [P, KT, CH * P])
        up_raw = sb("up_raw", [P, KT, CH * P])
        down_raw = sb("down_raw", [P, CH, D])
        gate_hi = [sb(f"gate_hi{t}", [P, KT, P], F32R) for t in range(CH)]
        gate_lo = [sb(f"gate_lo{t}", [P, KT, P], F32R) for t in range(CH)]
        up_hi = [sb(f"up_hi{t}", [P, KT, P], F32R) for t in range(CH)]
        up_lo = [sb(f"up_lo{t}", [P, KT, P], F32R) for t in range(CH)]
        down_hi = sb("down_hi", [P, CH, D], F32R)
        down_lo = sb("down_lo", [P, CH, D], F32R)
        h_hi = [sb(f"h_hi{k}", [P, CH, SEQ], F32R) for k in range(2)]
        h_lo = [sb(f"h_lo{k}", [P, CH, SEQ], F32R) for k in range(2)]
        b.scaled = sb("scaled", [P, 4, D])
        gate_act = [b.scaled[:, 0, h * HALF:(h + 1) * HALF] for h in range(2)]
        h_full = [b.scaled[:, 1, h * HALF:(h + 1) * HALF] for h in range(2)]
        norm = NormSems(sem, tag)
        x_loaded = [sem(f"{tag}_x_loaded{t}") for t in range(TT)]
        gate_loaded = sem(f"{tag}_gate_loaded")
        up_loaded = sem(f"{tag}_up_loaded")
        down_loaded = sem(f"{tag}_down_loaded")
        gate_hi_done = sem(f"{tag}_gate_hi_done")
        up_hi_done = sem(f"{tag}_up_hi_done")
        down_hi_done = sem(f"{tag}_down_hi_done")
        gate_split = sem(f"{tag}_gate_split")
        up_split = sem(f"{tag}_up_split")
        down_split = sem(f"{tag}_down_split")
        gate_ready = sem(f"{tag}_gate_ready")
        up_ready = sem(f"{tag}_up_ready")
        silu_done = sem(f"{tag}_silu_done")
        h_done = sem(f"{tag}_h_done")
        h_hi_done = sem(f"{tag}_h_hi_done")
        h_split = sem(f"{tag}_h_split")
        y_ready = sem(f"{tag}_y_ready")
        y_added = sem(f"{tag}_y_added")
        stored = sem(f"{tag}_stored")
        fin_sq, fin_root, fin_rstd, fin_scaled, fin_done = (sem(f"{tag}_fin{i}") for i in range(5))
        block = ctx.enter_context(nc.Block())

        BANK_Y = 4

        @block.sync
        def _(sp):
            if x_loaded_from is not None:
                for t in range(TT):
                    sp.dma_start(b.x[:, t, :], x_loaded_from[t * P:(t + 1) * P, :]).then_inc(x_loaded[t], 16)

            def load_columns(raw, w, first, loaded):
                sp.dma_start(raw[:, :, :], w[bass.ds(first, P), :].rearrange("p (k f) -> p k f", k=KT)
                             ).then_inc(loaded, 16)

            def load_down(first):
                sp.dma_start(down_raw[:, :, :], w_down[bass.ds(first, CH * P), :].rearrange(
                    "(t p) d -> p t d", p=P)).then_inc(down_loaded, 16)

            def chunk(c, first=False, last=False):
                here, ahead = address(sp, c * CH * P), address(sp, (c + 1) * P)
                if not first:
                    sp.wait_ge(down_split, CH * c)
                load_down(here)
                if not last:
                    sp.wait_ge(gate_split, CH * (c + 1))
                    load_columns(gate_raw, w_gate, ahead, gate_loaded)
                    sp.wait_ge(up_split, CH * (c + 1))
                    load_columns(up_raw, w_up, ahead, up_loaded)

            load_columns(gate_raw, w_gate, 0, gate_loaded)
            load_columns(up_raw, w_up, 0, up_loaded)
            chunk(0, first=True)
            with sp.Fori(0, (NCH - 3) // 2) as i:
                chunk(2 * i + 1)
                chunk(2 * i + 2)
            chunk(NCH - 2)
            chunk(NCH - 1, last=True)
            for t in range(TT):
                if final:
                    sp.wait_ge(fin_done, t + 1)
                else:
                    sp.wait_ge(y_added, 4 + 16 * (NCH - 1) + 2 * t + 2)
                sp.dma_start(x_store[t * P:(t + 1) * P, :], b.x[:, t, :]).then_inc(stored, 16)
            sp.wait_ge(stored, 16 * TT)

        @block.scalar
        def _(act):
            def split_columns(c, t):
                act.wait_ge(gate_loaded, 16 * (c + 1))
                act.activation(gate_hi[t][:, :, :], gate_raw[:, :, t * P:(t + 1) * P], ACT.Copy
                               ).then_inc(gate_hi_done, 1)
                act.wait_ge(up_loaded, 16 * (c + 1))
                act.activation(up_hi[t][:, :, :], up_raw[:, :, t * P:(t + 1) * P], ACT.Copy
                               ).then_inc(up_hi_done, 1)

            def split_down(c):
                act.wait_ge(y_ready, 16 * c + 1)
                act.wait_ge(down_loaded, 16 * (c + 1))
                for t in range(CH):
                    act.activation(down_hi[:, t, :], down_raw[:, t, :], ACT.Copy).then_inc(down_hi_done, 1)

            def chunk(c, k, first=False, last=False):
                if not first:
                    split_down(c - 1)
                for t in range(CH):
                    for half in range(2):
                        n = 2 * CH * c + 2 * t + half
                        cols = slice(half * HALF, (half + 1) * HALF)
                        act.wait_ge(gate_ready, n + 1)
                        if not (first and t == 0):
                            act.wait_ge(h_done, n - 1)
                        act.activation(gate_act[half], b.ps[:, half, :], ACT.Silu).then_inc(silu_done, 1)
                        act.wait_ge(h_done, n + 1)
                        act.activation(h_hi[k][:, t, cols], h_full[half], ACT.Copy).then_inc(h_hi_done, 1)
                    if not last:
                        split_columns(c + 1, t)

            norm_scalar(act, norm, b, x_loaded if x_loaded_from is not None else None)
            for t in range(CH):
                split_columns(0, t)
            chunk(0, 0, first=True)
            with act.Fori(0, (NCH - 3) // 2) as i:
                chunk(2 * i + 1, 1)
                chunk(2 * i + 2, 0)
            chunk(NCH - 2, (NCH - 2) % 2)
            chunk(NCH - 1, (NCH - 1) % 2, last=True)
            split_down(NCH - 1)
            if final:
                for t in range(TT):
                    act.wait_ge(y_added, 4 + 16 * (NCH - 1) + 2 * t + 2)
                    if t >= 2:
                        act.wait_ge(fin_done, t - 1)
                    act.activation(b.scaled[:, 2 + t % 2, :], b.x[:, t, :], ACT.Square,
                                   accum_out=b.sumsq[:, t:t + 1]).then_inc(fin_sq, 1)
                    act.wait_ge(fin_sq, t + 1)
                    act.activation(b.root[:, t:t + 1], b.sumsq[:, t:t + 1], ACT.Sqrt, scale=1.0 / D,
                                   bias=b.eps[:, 0:1]).then_inc(fin_root, 1)

        @block.vector
        def _(dve):
            def split_columns(c, t):
                dve.wait_ge(gate_hi_done, CH * c + t + 1)
                dve.tensor_tensor(gate_lo[t][:, :, :], gate_raw[:, :, t * P:(t + 1) * P],
                                  gate_hi[t][:, :, :].bitcast(F32), ALU.subtract).then_inc(gate_split, 1)
                dve.wait_ge(up_hi_done, CH * c + t + 1)
                dve.tensor_tensor(up_lo[t][:, :, :], up_raw[:, :, t * P:(t + 1) * P],
                                  up_hi[t][:, :, :].bitcast(F32), ALU.subtract).then_inc(up_split, 1)

            def split_down(c):
                for t in range(CH):
                    dve.wait_ge(down_hi_done, CH * c + t + 1)
                    dve.tensor_tensor(down_lo[:, t, :], down_raw[:, t, :], down_hi[:, t, :].bitcast(F32),
                                      ALU.subtract).then_inc(down_split, 1)

            def add_down(c):
                for t in range(TT):
                    for half in range(2):
                        g = 2 * t + half
                        dve.wait_ge(y_ready, 1 + 16 * c + g + 1)
                        cols = slice(half * HALF, (half + 1) * HALF)
                        dve.scalar_tensor_tensor(out=b.x[:, t, cols], in0=b.ps[:, BANK_Y + g % 4, :], scalar=0.5,
                                                 in1=b.x[:, t, cols], op0=ALU.mult, op1=ALU.add
                                                 ).then_inc(y_added, 1)

            def chunk(c, k, first=False, last=False):
                if not first:
                    split_down(c - 1)
                for t in range(CH):
                    for half in range(2):
                        n = 2 * CH * c + 2 * t + half
                        cols = slice(half * HALF, (half + 1) * HALF)
                        dve.wait_ge(silu_done, n + 1)
                        dve.wait_ge(up_ready, n + 1)
                        if not (first and t == 0):
                            dve.wait_ge(h_split, n - 1)
                        dve.tensor_tensor(h_full[half], b.ps[:, 2 + half, :], gate_act[half], ALU.mult
                                          ).then_inc(h_done, 1)
                        dve.wait_ge(h_hi_done, n + 1)
                        dve.tensor_tensor(h_lo[k][:, t, cols], h_full[half], h_hi[k][:, t, cols].bitcast(F32),
                                          ALU.subtract).then_inc(h_split, 1)
                    if not last:
                        split_columns(c + 1, t)
                if not first:
                    add_down(c - 1)

            norm_vector(dve, norm, b)
            for t in range(CH):
                split_columns(0, t)
            chunk(0, 0, first=True)
            with dve.Fori(0, (NCH - 3) // 2) as i:
                chunk(2 * i + 1, 1)
                chunk(2 * i + 2, 0)
            chunk(NCH - 2, (NCH - 2) % 2)
            chunk(NCH - 1, (NCH - 1) % 2, last=True)
            split_down(NCH - 1)
            add_down(NCH - 1)
            if final:
                for t in range(TT):
                    dve.wait_ge(fin_root, t + 1)
                    dve.reciprocal(b.rstd[:, t:t + 1], b.root[:, t:t + 1]).then_inc(fin_rstd, 1)
                    dve.wait_ge(fin_rstd, t + 1)
                    dve.tensor_scalar(b.scaled[:, 2 + t % 2, :], b.x[:, t, :], b.rstd[:, t:t + 1], None,
                                      ALU.mult).then_inc(fin_scaled, 1)
                    dve.wait_ge(fin_scaled, t + 1)
                    dve.tensor_tensor(b.x[:, t, :], b.scaled[:, 2 + t % 2, :], b.final_gain[:, :], ALU.mult
                                      ).then_inc(fin_done, 1)

        @block.tensor
        def _(pe):
            def product(bank, hi, lo, half):
                cols = slice(half * HALF, (half + 1) * HALF)
                for k in range(KT):
                    pe.matmul(b.ps[:, bank, :], hi[:, k, :], b.xn_hi[:, k, cols], start=(k == 0), stop=False)
                    pe.matmul(b.ps[:, bank, :], hi[:, k, :], b.xn_lo[:, k, cols], start=False, stop=False)
                    last = pe.matmul(b.ps[:, bank, :], lo[:, k, :], b.xn_hi[:, k, cols], start=False,
                                     stop=(k == KT - 1))
                return last

            def up_products(c, t, first=False):
                pe.wait_ge(gate_split, CH * c + t + 1)
                pe.wait_ge(up_split, CH * c + t + 1)
                for half in range(2):
                    n = 2 * CH * c + 2 * t + half
                    if not first:
                        pe.wait_ge(silu_done, n - 1)
                    product(half, gate_hi[t], gate_lo[t], half).then_inc(gate_ready, 1)
                    if not first:
                        pe.wait_ge(h_done, n - 1)
                    product(2 + half, up_hi[t], up_lo[t], half).then_inc(up_ready, 1)

            def down_products(c, k):
                pe.wait_ge(h_split, 2 * CH * (c + 1))
                pe.wait_ge(down_split, CH * (c + 1))
                for t in range(TT):
                    for half in range(2):
                        g = 2 * t + half
                        pe.wait_ge(y_added, 16 * c + g + 1)
                        tok, cols = slice(t * P, (t + 1) * P), slice(half * HALF, (half + 1) * HALF)
                        for f in range(CH):
                            out = b.ps[:, BANK_Y + g % 4, :]
                            pe.matmul(out, h_hi[k][:, f, tok], down_hi[:, f, cols], start=(f == 0), stop=False)
                            pe.matmul(out, h_hi[k][:, f, tok], down_lo[:, f, cols], start=False, stop=False)
                            last = pe.matmul(out, h_lo[k][:, f, tok], down_hi[:, f, cols], start=False,
                                             stop=(f == CH - 1))
                        last.then_inc(y_ready, 1)

            def chunk(c, k, first=False):
                for t in range(CH):
                    up_products(c, t, first and t == 0)
                if not first:
                    down_products(c - 1, 1 - k)

            norm_tensor(pe, norm, b)
            pe.sem_inc(y_added, 4)
            pe.sem_inc(y_ready, 1)
            pe.wait_ge(norm.lo, 2 * KT)
            chunk(0, 0, first=True)
            with pe.Fori(0, (NCH - 3) // 2) as i:
                chunk(2 * i + 1, 1)
                chunk(2 * i + 2, 0)
            chunk(NCH - 2, (NCH - 2) % 2)
            chunk(NCH - 1, (NCH - 1) % 2)
            down_products(NCH - 1, (NCH - 1) % 2)



STEPS = 8
QG = 256
SB_KIND, DIL_KIND = 0, 1
HALVES = 6
V, Q, K = 0, 1, 2
PRODUCTS = ((V, 0), (V, 1), (Q, 0), (K, 0), (Q, 1), (K, 1))
UNITS = (4, 4, 8, 8, 4, 4, 8, 8)
UNIT_START = (0, 4, 8, 16, 24, 28, 32, 40)
ENDS = {1: 0, 2: 1, 3: 2, 5: 3, 6: 4, 7: 5}
V_TURN = {2: 0, 3: 1}
TURNS = 22


def turn_index(s, j, v_turn):
    n = sum(u % 4 + 1 for u in range(s)) + j
    if v_turn:
        n += sum(1 for u in V_TURN if u < s) + (s in V_TURN)
    return n


def units_between(s, j):
    banks = s % 4 + 1
    first, rest = UNITS[s] * j // (banks + 1), UNITS[s] * (j + 1) // (banks + 1)
    return UNIT_START[s] + first, UNIT_START[s] + rest


def mixer_norm_block(nc, b, sem):
    with ExitStack() as ctx:
        b.scaled = ctx.enter_context(nc.sbuf_tensor("mix_scaled", [P, 4, D], F32))
        norm = NormSems(sem, "mix")
        block = ctx.enter_context(nc.Block())

        @block.scalar
        def _(act):
            norm_scalar(act, norm, b, None)

        @block.vector
        def _(dve):
            norm_vector(dve, norm, b)

        @block.tensor
        def _(pe):
            norm_tensor(pe, norm, b)


def heads_block(nc, b, sem, w_in, ident, neg_mask, log_count, cos, sin, o_dram):
    with ExitStack() as ctx:
        def sb(name, shape, dt=F32):
            return ctx.enter_context(nc.sbuf_tensor(f"heads_{name}", shape, dt))

        w_raw = [sb(f"w_raw{i}", [P, KT, P]) for i in range(2)]
        w_hi = [sb(f"w_hi{i}", [P, KT, P], F32R) for i in range(2)]
        w_lo = [sb(f"w_lo{i}", [P, KT, P], F32R) for i in range(2)]
        qk_hi = [[sb(f"{n}_hi{kind}", [P, SEQ], F32R) for n in "qk"] for kind in range(2)]
        qk_lo = [[sb(f"{n}_lo{kind}", [P, SEQ], F32R) for n in "qk"] for kind in range(2)]
        v_hi = [sb(f"v_hi{kind}", [P, TT, P], F32R) for kind in range(2)]
        v_lo = [sb(f"v_lo{kind}", [P, TT, P], F32R) for kind in range(2)]
        v_turned = sb("v_feature_major", [P, HALF])
        weight = [[sb(f"weight{s}{a}", [P, SEQ]) for a in range(2)] for s in range(2)]
        stay = [[sb(f"stay{s}{a}", [P, SEQ + 1]) for a in range(2)] for s in range(2)]
        wt_hi = sb("wt_hi", [P, TT, QG], F32R)
        wt_lo = sb("wt_lo", [P, TT, QG], F32R)
        o_stage = sb("o_stage", [P, SEQ])
        cos_sb, sin_sb = sb("cos", [P, SEQ]), sb("sin", [P, SEQ])
        log_count_sb = sb("log_count", [P, SEQ])
        rot_in, rot_swap, rot_out = sb("rot_in", [P, HALF]), sb("rot_swap", [P, HALF]), sb("rot_out", [P, HALF])
        neg_f = sb("neg_f", [P, P])
        neg_r, ident_r = sb("neg_r", [P, P], F32R), sb("ident_r", [P, P], F32R)
        row_max, neg_max, row_sum, row_inv = (sb(n, [P, 4]) for n in ("row_max", "neg_max", "row_sum", "row_inv"))

        tables_loaded = sem("tables_loaded")
        tables_ready = sem("tables_ready")
        w_loaded = [sem(f"w_loaded{i}") for i in range(2)]
        w_hi_done, w_split = sem("w_hi_done"), sem("w_split")
        proj_ready, proj_free = sem("proj_ready"), sem("proj_free")
        sb_hi_done = sem("sb_qk_hi_done")
        rot_swapped, rot_cos, rot_sin, rot_sum = (sem(f"rot_{n}") for n in ("swapped", "cos", "sin", "sum"))
        rot_hi_done, rot_split = sem("rot_hi_done"), sem("rot_split")
        z_ready = sem("z_ready")
        gates_ready, products_ready, sb_weights = sem("gates_ready"), sem("products_ready"), sem("sb_weights")
        dil_max, dil_negmax, dil_exp, dil_inv, dil_weights = (
            sem(f"dil_{n}") for n in ("max", "negmax", "exp", "inv", "weights"))
        scores_seen = sem("dil_scores_seen")
        turned, turn_hi_done, turn_split = sem("turned"), sem("turn_hi_done"), sem("turn_split")
        pv_ready, o_copied = sem("pv_ready"), sem("o_copied")
        o_stored = [sem(f"o_stored{h}") for h in range(2)]
        block = ctx.enter_context(nc.Block())

        BANK_PV, BANK_TURN, BANK_PROJ = 4, 5, 7
        z = [b.ps[:, 2 * a:2 * a + 2, :].rearrange("p a c -> p (a c)") for a in range(2)]

        def pair_of(it, kind, ahead):
            k = kind + ahead
            return it + k // 2, k % 2

        def run(it, kind):
            return 2 * it + kind

        @block.sync
        def _(sp):
            def load_weights(it, kind, piece):
                n = 3 * kind + piece
                slot = n % 2
                first = address(sp, (6 * it + n) * P)
                sp.wait_ge(w_split, 2 + 6 * it + n - 1)
                sp.dma_start(w_raw[slot][:, :, :], w_in[bass.ds(first, P), :].rearrange(
                    "p (k c) -> p k c", k=KT)).then_inc(w_loaded[slot], 16)

            def store_head(it, kind, head):
                rows = slice(head * HEAD, (head + 1) * HEAD)
                first = address(sp, kind * GROUP + it * P + head * HEAD)
                sp.wait_ge(o_copied, 1 + STEPS * run(it, kind) + 4 * head + 4)
                sp.dma_start(o_dram[bass.ds(first, HEAD), :], o_stage[rows, :]
                             ).then_inc(o_stored[head], 16)

            def one_run(it, kind, project=True, more=True):
                it1, kind1 = pair_of(it, kind, 1)
                it2, kind2 = pair_of(it, kind, 2)
                if project:
                    load_weights(it1, kind1, K)
                if more:
                    load_weights(it2, kind2, V)
                store_head(it, kind, 0)
                if more:
                    load_weights(it2, kind2, Q)
                store_head(it, kind, 1)

            sp.sem_inc(w_split, 2)
            for dst, src in ((neg_f, neg_mask), (log_count_sb, log_count), (cos_sb, cos), (sin_sb, sin)):
                sp.dma_start(dst[:, :], src[:, :]).then_inc(tables_loaded, 16)
            load_weights(0, 0, V)
            load_weights(0, 0, Q)
            load_weights(0, 0, K)
            load_weights(0, 1, V)
            load_weights(0, 1, Q)
            sp.sem_inc(o_stored[0], 16)
            sp.sem_inc(o_stored[1], 16)
            with sp.Fori(0, PAIRS - 1) as it:
                one_run(it, SB_KIND)
                one_run(it, DIL_KIND)
            one_run(PAIRS - 1, SB_KIND, more=False)
            one_run(PAIRS - 1, DIL_KIND, project=False, more=False)
            for h in range(2):
                sp.wait_ge(o_stored[h], 16 * (2 * PAIRS + 1))

        @block.gpsimd
        def _(pool):
            def products(it, s):
                for a in range(2):
                    nk = P * (2 * (s % 4) + a + 1)
                    beta = weight[s % 2][a][:, SEQ - nk:SEQ]
                    pool.wait_ge(products_ready, 2 * STEPS * it + 2 * s + a + 1)
                    pool.tensor_tensor(beta, beta, stay[s % 2][a][:, SEQ - nk + 1:SEQ + 1], ALU.mult
                                       ).then_inc(sb_weights, 1)

            def rotate_cos(it, j):
                half = PRODUCTS[j][1]
                n = 4 * it + j - 2
                pool.wait_ge(proj_free, 1 + HALVES * run(it, DIL_KIND) + j + 1)
                pool.wait_ge(rot_split, 1 + n)
                pool.tensor_tensor(rot_out[:, :], rot_in[:, :], cos_sb[:, half * HALF:(half + 1) * HALF],
                                   ALU.mult).then_inc(rot_cos, 1)

            def step(it, kind, s, project=True, last=False):
                it1, kind1 = pair_of(it, kind, 1)
                if s < STEPS - 1:
                    if kind == SB_KIND:
                        products(it, s + 1)
                elif not last and kind1 == SB_KIND:
                    products(it1, 0)
                if project and kind1 == DIL_KIND and ENDS.get(s, 0) >= 2:
                    rotate_cos(it1, ENDS[s])

            def one_run(it, kind, project=True, last=False):
                for s in range(STEPS):
                    step(it, kind, s, project, last)

            pool.wait_ge(tables_ready, 1)
            products(0, 0)
            with pool.Fori(0, PAIRS - 1) as it:
                one_run(it, SB_KIND)
                one_run(it, DIL_KIND)
            one_run(PAIRS - 1, SB_KIND)
            one_run(PAIRS - 1, DIL_KIND, project=False, last=True)

        @block.scalar
        def _(act):
            def split_weights(it, kind, piece):
                n = 3 * kind + piece
                slot = n % 2
                act.wait_ge(w_loaded[slot], 16 * (3 * it + n // 2 + 1))
                done = {Q: 0, K: 2, V: -1}[piece]
                if not (piece == V and isinstance(it, int) and run(it, kind) == 0):
                    act.wait_ge(proj_ready, 1 + HALVES * run(it, kind) + done)
                act.activation(w_hi[slot][:, :, :], w_raw[slot][:, :, :], ACT.Copy).then_inc(w_hi_done, 1)

            def gates(it, s, a):
                nk = P * (2 * (s % 4) + a + 1)
                keys = slice(SEQ - nk, SEQ)
                act.wait_ge(z_ready, 1 + 2 * STEPS * run(it, SB_KIND) + 2 * s + a + 1)
                if not (isinstance(it, int) and it == 0 and s == 0):
                    act.wait_ge(turned, stage_free(it, SB_KIND, s))
                act.activation(weight[s % 2][a][:, keys], z[a][:, 0:nk], ACT.Sigmoid, scale=SCALE)
                act.activation(stay[s % 2][a][:, keys], z[a][:, 0:nk], ACT.Sigmoid, scale=-SCALE
                               ).then_inc(gates_ready, 1)

            def exponentials(it, s, a):
                nk = P * (2 * (s % 4) + a + 1)
                keys = slice(SEQ - nk, SEQ)
                c = 2 * (s % 2) + a
                act.wait_ge(dil_negmax, 2 * STEPS * it + 2 * s + a + 1)
                act.activation(weight[s % 2][a][:, keys], weight[s % 2][a][:, keys], ACT.Exp, scale=SCALE,
                               bias=neg_max[:, c:c + 1], accum_out=row_sum[:, c:c + 1]).then_inc(dil_exp, 1)

            def elementwise(it, kind, s, a):
                if kind == SB_KIND:
                    gates(it, s, a)
                else:
                    exponentials(it, s, a)

            def weights_hi(it, kind, s, j, v_turn):
                n = 2 + TURNS * run(it, kind) + turn_index(s, j, v_turn)
                bank = BANK_TURN + turn_index(s, j, v_turn) % 2
                if j == 0:
                    act.wait_ge(pv_ready, 1 + STEPS * run(it, kind) + s)
                act.wait_ge(turned, n + 1)
                for dst, cols in turn_parts(wt_hi, s, j):
                    last = act.activation(dst, b.ps[:, bank, cols], ACT.Copy)
                last.then_inc(turn_hi_done, 1)

            def v_hi_part(it, kind, half, n, bank):
                act.wait_ge(turned, n + 1)
                act.activation(v_hi[kind][:, 4 * half:4 * half + 4, :],
                               b.ps[:, bank, :].rearrange("p (t c) -> p t c", c=P), ACT.Copy
                               ).then_inc(turn_hi_done, 1)

            def projected(it, kind, j):
                piece, half = PRODUCTS[j]
                cols = slice(half * HALF, (half + 1) * HALF)
                act.wait_ge(proj_ready, 1 + HALVES * run(it, kind) + j + 1)
                if piece == V:
                    act.activation(v_turned[:, :], b.ps[:, BANK_PROJ, :], ACT.Copy).then_inc(proj_free, 1)
                elif kind == SB_KIND:
                    act.activation(qk_hi[kind][piece - 1][:, cols], b.ps[:, BANK_PROJ, :], ACT.Copy
                                   ).then_inc(sb_hi_done, 1)
                else:
                    act.wait_ge(rot_split, 1 + 4 * it + j - 2)
                    act.activation(rot_in[:, :], b.ps[:, BANK_PROJ, :], ACT.Copy).then_inc(proj_free, 1)
                    act.wait_ge(proj_free, 1 + HALVES * run(it, kind) + j + 1)
                    for head in range(2):
                        for part in range(2):
                            src = head * HEAD + part * 32
                            dst = head * HEAD + (1 - part) * 32
                            act.dma_start(rot_swap[dst:dst + 32, :], rot_in[src:src + 32, :]
                                          ).then_inc(rot_swapped, 16)

            def rotated_hi(it, j):
                piece, half = PRODUCTS[j]
                act.wait_ge(rot_sum, 4 * it + j - 2 + 1)
                act.activation(qk_hi[DIL_KIND][piece - 1][:, half * HALF:(half + 1) * HALF], rot_out[:, :],
                               ACT.Copy).then_inc(rot_hi_done, 1)

            def pv_out(it, kind, s):
                head, g = s // 4, s % 4
                rows = slice(head * HEAD, (head + 1) * HEAD)
                act.wait_ge(pv_ready, 1 + STEPS * run(it, kind) + s + 1)
                if g == 0:
                    act.wait_ge(o_stored[head], 16 * (run(it, kind) + 1))
                act.activation(o_stage[rows, g * QG:(g + 1) * QG], b.ps[rows, BANK_PV, 0:QG], ACT.Copy
                               ).then_inc(o_copied, 1)

            def step(it, kind, s, project=True, last=False):
                it1, kind1 = pair_of(it, kind, 1)
                it2, kind2 = pair_of(it, kind, 2)
                nit, nkind, ns = (it, kind, s + 1) if s < STEPS - 1 else (it1, kind1, 0)
                ahead = not (last and s == STEPS - 1)
                if ahead:
                    elementwise(nit, nkind, ns, 0)
                if project and s in V_TURN:
                    i = turn_index(s, -1, True)
                    v_hi_part(it1, kind1, V_TURN[s], 2 + TURNS * run(it, kind) + i, BANK_TURN + i % 2)
                for j in range(s % 4 + 1):
                    weights_hi(it, kind, s, j, project)
                    if j == 0 and ahead:
                        elementwise(nit, nkind, ns, 1)
                if s == 0 and kind == DIL_KIND:
                    rotated_hi(it, 5)
                if project and kind1 == DIL_KIND and s > 0 and ENDS.get(s - 1, 0) >= 2:
                    rotated_hi(it1, ENDS[s - 1])
                if project and s == 0:
                    split_weights(it1, kind1, Q)
                if project and s == 3:
                    split_weights(it1, kind1, K)
                if project and s in ENDS:
                    projected(it1, kind1, ENDS[s])
                if s == 7 and project and not (isinstance(it, int) and it == PAIRS - 1):
                    split_weights(it2, kind2, V)
                pv_out(it, kind, s)

            def one_run(it, kind, project=True, last=False):
                for s in range(STEPS):
                    step(it, kind, s, project, last)

            split_weights(0, 0, V)
            split_weights(0, 0, Q)
            for j in range(HALVES):
                projected(0, 0, j)
                if j < 2:
                    v_hi_part(0, 0, j, j, BANK_TURN + j)
                if j == 1:
                    split_weights(0, 0, K)
                if j == 4:
                    split_weights(0, 1, V)
            elementwise(0, SB_KIND, 0, 0)
            elementwise(0, SB_KIND, 0, 1)
            with act.Fori(0, PAIRS - 1) as it:
                one_run(it, SB_KIND)
                one_run(it, DIL_KIND)
            one_run(PAIRS - 1, SB_KIND)
            one_run(PAIRS - 1, DIL_KIND, project=False, last=True)

        @block.vector
        def _(dve):
            def split_weights(it, kind, piece):
                n = 3 * kind + piece
                slot = n % 2
                dve.wait_ge(w_hi_done, 6 * it + n + 1)
                dve.tensor_tensor(w_lo[slot][:, :, :], w_raw[slot][:, :, :], w_hi[slot][:, :, :].bitcast(F32),
                                  ALU.subtract).then_inc(w_split, 1)

            def scan(it, s, a):
                nk = P * (2 * (s % 4) + a + 1)
                dve.wait_ge(gates_ready, 2 * STEPS * it + 2 * s + a + 1)
                back = stay[s % 2][a][:, SEQ - nk:SEQ][:, ::-1]
                dve.tensor_tensor_scan(back, back, back, 1.0, ALU.mult, ALU.min).then_inc(products_ready, 1)

            def masked_max(it, s, a):
                i = 2 * (s % 4) + a
                nk = P * (i + 1)
                keys = slice(SEQ - nk, SEQ)
                c = 2 * (s % 2) + a
                dve.wait_ge(z_ready, 1 + 2 * STEPS * run(it, DIL_KIND) + 2 * s + a + 1)
                dve.wait_ge(turned, stage_free(it, DIL_KIND, s))
                dve.wait_ge(tables_loaded, 16 * 4)
                dve.sem_inc(scores_seen, 1)
                dve.tensor_tensor_reduce(weight[s % 2][a][:, keys], z[a][:, 0:nk], log_count_sb[:, keys], 1.0,
                                         -3e38, ALU.add, ALU.max, row_max[:, c:c + 1]).then_inc(dil_max, 1)
                dve.wait_ge(dil_max, 2 * STEPS * it + 2 * s + a + 1)
                dve.tensor_scalar(neg_max[:, c:c + 1], row_max[:, c:c + 1], -SCALE, None, ALU.mult
                                  ).then_inc(dil_negmax, 1)

            def normalize(it, s, a):
                nk = P * (2 * (s % 4) + a + 1)
                keys = slice(SEQ - nk, SEQ)
                c = 2 * (s % 2) + a
                n = 2 * STEPS * it + 2 * s + a + 1
                dve.wait_ge(dil_exp, n)
                dve.reciprocal(row_inv[:, c:c + 1], row_sum[:, c:c + 1]).then_inc(dil_inv, 1)
                dve.wait_ge(dil_inv, n)
                dve.tensor_scalar(weight[s % 2][a][:, keys], weight[s % 2][a][:, keys], row_inv[:, c:c + 1], None,
                                  ALU.mult).then_inc(dil_weights, 1)

            def elementwise(it, kind, s, a):
                if kind == SB_KIND:
                    scan(it, s, a)
                else:
                    masked_max(it, s, a)

            def weights_lo(it, kind, s, j, v_turn):
                n = 2 + TURNS * run(it, kind) + turn_index(s, j, v_turn)
                bank = BANK_TURN + turn_index(s, j, v_turn) % 2
                dve.wait_ge(turn_hi_done, n + 1)
                for (dst, cols), (hi, _) in zip(turn_parts(wt_lo, s, j), turn_parts(wt_hi, s, j)):
                    last = dve.tensor_tensor(dst, b.ps[:, bank, cols], hi.bitcast(F32), ALU.subtract)
                last.then_inc(turn_split, 1)

            def v_lo_part(it, kind, half, n, bank):
                dve.wait_ge(turn_hi_done, n + 1)
                part = slice(4 * half, 4 * half + 4)
                dve.tensor_tensor(v_lo[kind][:, part, :], b.ps[:, bank, :].rearrange("p (t c) -> p t c", c=P),
                                  v_hi[kind][:, part, :].bitcast(F32), ALU.subtract).then_inc(turn_split, 1)

            def projected_lo(it, j):
                piece, half = PRODUCTS[j]
                cols = slice(half * HALF, (half + 1) * HALF)
                dve.wait_ge(sb_hi_done, 4 * it + j - 2 + 1)
                dve.tensor_tensor(qk_lo[SB_KIND][piece - 1][:, cols], b.ps[:, BANK_PROJ, :],
                                  qk_hi[SB_KIND][piece - 1][:, cols].bitcast(F32), ALU.subtract
                                  ).then_inc(proj_free, 1)

            def rotate(it, j):
                half = PRODUCTS[j][1]
                cols = slice(half * HALF, (half + 1) * HALF)
                n = 4 * it + j - 2
                dve.wait_ge(rot_swapped, 64 * (n + 1))
                dve.tensor_tensor(rot_swap[:, :], rot_swap[:, :], sin_sb[:, cols], ALU.mult).then_inc(rot_sin, 1)
                dve.wait_ge(rot_sin, n + 1)
                dve.wait_ge(rot_cos, n + 1)
                dve.tensor_tensor(rot_out[:, :], rot_out[:, :], rot_swap[:, :], ALU.add).then_inc(rot_sum, 1)

            def rotated_lo(it, j):
                piece, half = PRODUCTS[j]
                cols = slice(half * HALF, (half + 1) * HALF)
                dve.wait_ge(rot_hi_done, 4 * it + j - 2 + 1)
                dve.tensor_tensor(qk_lo[DIL_KIND][piece - 1][:, cols], rot_out[:, :],
                                  qk_hi[DIL_KIND][piece - 1][:, cols].bitcast(F32), ALU.subtract
                                  ).then_inc(rot_split, 1)

            def step(it, kind, s, project=True, last=False):
                it1, kind1 = pair_of(it, kind, 1)
                it2, kind2 = pair_of(it, kind, 2)
                nit, nkind, ns = (it, kind, s + 1) if s < STEPS - 1 else (it1, kind1, 0)
                ahead = not (last and s == STEPS - 1)
                rot = None
                if s == 0 and kind == DIL_KIND:
                    rot = (it, 5)
                if project and kind1 == DIL_KIND and s > 0 and ENDS.get(s - 1, 0) >= 2:
                    rot = (it1, ENDS[s - 1])
                if ahead:
                    elementwise(nit, nkind, ns, 0)
                if project and s in V_TURN:
                    i = turn_index(s, -1, True)
                    v_lo_part(it1, kind1, V_TURN[s], 2 + TURNS * run(it, kind) + i, BANK_TURN + i % 2)
                for j in range(s % 4 + 1):
                    weights_lo(it, kind, s, j, project)
                    if j == 0 and ahead:
                        elementwise(nit, nkind, ns, 1)
                if ahead and nkind == DIL_KIND:
                    normalize(nit, ns, 0)
                if rot:
                    rotate(*rot)
                if ahead and nkind == DIL_KIND:
                    normalize(nit, ns, 1)
                if rot:
                    rotated_lo(*rot)
                if project and s == 0:
                    split_weights(it1, kind1, Q)
                if project and s == 3:
                    split_weights(it1, kind1, K)
                if project and kind1 == SB_KIND and ENDS.get(s, 0) >= 2:
                    projected_lo(it1, ENDS[s])
                if s == 7 and project and not (isinstance(it, int) and it == PAIRS - 1):
                    split_weights(it2, kind2, V)

            def one_run(it, kind, project=True, last=False):
                for s in range(STEPS):
                    step(it, kind, s, project, last)

            dve.wait_ge(tables_loaded, 16 * 4)
            dve.tensor_copy(neg_r[:, :], neg_f[:, :])
            dve.tensor_copy(ident_r[:, :], b.ident[:, :])
            for s in range(2):
                for a in range(2):
                    ones = dve.memset(stay[s][a][:, SEQ:SEQ + 1], 1.0)
            ones.then_inc(tables_ready, 1)
            split_weights(0, 0, V)
            split_weights(0, 0, Q)
            for j in range(HALVES):
                if j < 2:
                    v_lo_part(0, 0, j, j, BANK_TURN + j)
                else:
                    projected_lo(0, j)
                if j == 1:
                    split_weights(0, 0, K)
                if j == 4:
                    split_weights(0, 1, V)
            elementwise(0, SB_KIND, 0, 0)
            elementwise(0, SB_KIND, 0, 1)
            with dve.Fori(0, PAIRS - 1) as it:
                one_run(it, SB_KIND)
                one_run(it, DIL_KIND)
            one_run(PAIRS - 1, SB_KIND)
            one_run(PAIRS - 1, DIL_KIND, project=False, last=True)

        @block.tensor
        def _(pe):
            def project(it, kind, u0, u1):
                for u in range(u0, u1):
                    j, k = u // KT, u % KT
                    piece, half = PRODUCTS[j]
                    n = 3 * kind + piece
                    hi, lo = w_hi[n % 2], w_lo[n % 2]
                    cols = slice(half * HALF, (half + 1) * HALF)
                    out = b.ps[:, BANK_PROJ, :]
                    if k == 0:
                        pe.wait_ge(w_split, 2 + 6 * it + n + 1)
                        pe.wait_ge(proj_free, 1 + HALVES * run(it, kind) + j)
                    pe.matmul(out, hi[:, k, :], b.xn_hi[:, k, cols], start=(k == 0), stop=False)
                    pe.matmul(out, hi[:, k, :], b.xn_lo[:, k, cols], start=False, stop=False)
                    last = pe.matmul(out, lo[:, k, :], b.xn_hi[:, k, cols], start=False, stop=(k == KT - 1))
                    if k == KT - 1:
                        last.then_inc(proj_ready, 1)

            def scores(it, kind, s):
                head, g = s // 4, s % 4
                rows = slice(head * HEAD, (head + 1) * HEAD)
                (q_hi, k_hi), (q_lo, k_lo) = qk_hi[kind], qk_lo[kind]
                if s in (0, 2):
                    if kind == SB_KIND:
                        pe.wait_ge(proj_free, 1 + HALVES * run(it, kind) + (4 if s == 0 else 6))
                    else:
                        pe.wait_ge(rot_split, 1 + 4 * it + (2 if s == 0 else 4))
                for a in range(2):
                    i = 2 * g + a
                    nk = P * (i + 1)
                    if s > 0 or kind == DIL_KIND:
                        before = (it, kind, s - 1) if s > 0 else (it, SB_KIND, STEPS - 1)
                        if before[1] == SB_KIND:
                            pe.wait_ge(gates_ready, 2 * STEPS * before[0] + 2 * before[2] + a + 1)
                        else:
                            pe.wait_ge(dil_max, 2 * STEPS * before[0] + 2 * before[2] + a + 1)
                    elif not (isinstance(it, int) and it == 0):
                        pe.wait_ge(dil_max, 2 * STEPS * it - 2 + a + 1)
                    qt = slice(i * P, (i + 1) * P)
                    for c0 in range(0, nk, HALF):
                        c1 = min(nk, c0 + HALF)
                        out = z[a][:, c0:c1]
                        pe.matmul(out, q_hi[rows, qt], k_hi[rows, c0:c1], start=True, stop=False)
                        if kind == SB_KIND and c1 == nk:
                            pe.matmul(z[a][:, nk - P:nk], ident_r[:, :], neg_r[:, :], start=False, stop=False)
                        pe.matmul(out, q_hi[rows, qt], k_lo[rows, c0:c1], start=False, stop=False)
                        last = pe.matmul(out, q_lo[rows, qt], k_hi[rows, c0:c1], start=False, stop=True)
                    last.then_inc(z_ready, 1)

            def turn_weights(it, kind, s, j, v_turn):
                g = s % 4
                n = turn_index(s, j, v_turn)
                if j == 0:
                    if kind == SB_KIND:
                        pe.wait_ge(sb_weights, 2 * STEPS * it + 2 * s + 2)
                    else:
                        pe.wait_ge(dil_weights, 2 * STEPS * it + 2 * s + 2)
                pe.wait_ge(turn_split, 2 + TURNS * run(it, kind) + n - 1)
                for kk in range(2):
                    for a in range(2):
                        key, i = 2 * j + kk, 2 * g + a
                        if key > i:
                            continue
                        col = SEQ - P * (i + 1) + key * P
                        c = (2 * kk + a) * P
                        last = pe.transpose(b.ps[:, BANK_TURN + n % 2, c:c + P],
                                            weight[s % 2][a][:, col:col + P], b.ident[:, :])
                last.then_inc(turned, 1)

            def turn_v(it, kind, half, bank, before):
                pe.wait_ge(proj_free, 1 + HALVES * run(it, kind) + half + 1)
                if before is not None:
                    pe.wait_ge(turn_split, before)
                for t in range(4):
                    last = pe.transpose(b.ps[:, bank, t * P:(t + 1) * P], v_turned[:, t * P:(t + 1) * P],
                                        b.ident[:, :])
                last.then_inc(turned, 1)

            def weighted_values(it, kind, s, v_turn):
                g = s % 4
                pe.wait_ge(turn_split, 2 + TURNS * run(it, kind) + turn_index(s, g, v_turn) + 1)
                pe.wait_ge(o_copied, 1 + STEPS * run(it, kind) + s)
                for k in range(2 * g + 2):
                    cols = slice(P, QG) if k == 2 * g + 1 else slice(0, QG)
                    out = b.ps[:, BANK_PV, cols]
                    end = k == 2 * g + 1
                    pe.matmul(out, v_hi[kind][:, k, :], wt_hi[:, k, cols], start=(k == 0), stop=False)
                    pe.matmul(out, v_hi[kind][:, k, :], wt_lo[:, k, cols], start=False, stop=False)
                    last = pe.matmul(out, v_lo[kind][:, k, :], wt_hi[:, k, cols], start=False, stop=end)
                last.then_inc(pv_ready, 1)

            def step(it, kind, s, proj=True, last=False):
                it1, kind1 = pair_of(it, kind, 1)
                nit, nkind, ns = (it, kind, s + 1) if s < STEPS - 1 else (it1, kind1, 0)
                if not (last and s == STEPS - 1):
                    scores(nit, nkind, ns)
                if proj and s in V_TURN:
                    i = turn_index(s, -1, True)
                    turn_v(it1, kind1, V_TURN[s], BANK_TURN + i % 2, 2 + TURNS * run(it, kind) + i - 1)
                for j in range(s % 4 + 1):
                    if proj:
                        project(it1, kind1, *units_between(s, j))
                    turn_weights(it, kind, s, j, proj)
                if proj:
                    project(it1, kind1, *units_between(s, s % 4 + 1))
                weighted_values(it, kind, s, proj)

            def one_run(it, kind, proj=True, last=False):
                for s in range(STEPS):
                    step(it, kind, s, proj, last)

            pe.sem_inc(proj_free, 1)
            pe.sem_inc(proj_ready, 1)
            pe.sem_inc(pv_ready, 1)
            pe.sem_inc(o_copied, 1)
            pe.sem_inc(rot_split, 1)
            pe.sem_inc(z_ready, 1)
            pe.wait_ge(tables_ready, 1)
            for j in range(HALVES):
                project(0, 0, KT * j, KT * (j + 1))
                if j < 2:
                    turn_v(0, 0, j, BANK_TURN + j, None)
            scores(0, SB_KIND, 0)
            with pe.Fori(0, PAIRS - 1) as it:
                one_run(it, SB_KIND)
                one_run(it, DIL_KIND)
            one_run(PAIRS - 1, SB_KIND)
            one_run(PAIRS - 1, DIL_KIND, proj=False, last=True)


def stage_free(it, kind, s):
    v_turn = not (isinstance(it, int) and it == PAIRS - 1 and kind == DIL_KIND)
    if s < 2:
        n = turn_index(s + STEPS - 2, (s - 2) % 4, True) + 1 - TURNS
    else:
        n = turn_index(s - 2, (s - 2) % 4, v_turn) + 1
    return 2 + TURNS * (2 * it + kind) + n


def turn_parts(dst, s, j):
    if j < s % 4:
        return [(dst[:, 2 * j:2 * j + 2, :], slice(0, 2 * QG))]
    return [(dst[:, 2 * j, :], slice(0, QG)), (dst[:, 2 * j + 1, P:QG], slice(QG + P, 2 * QG))]



def output_block(nc, b, sem, o_dram, x_dram, w_out, group_gain):
    with ExitStack() as ctx:
        def sb(name, shape, dt=F32):
            return ctx.enter_context(nc.sbuf_tensor(f"out_{name}", shape, dt))

        o_raw = [sb(f"o_raw{i}", [P, SEQ]) for i in range(3)]
        o_sq = [sb(f"o_sq{i}", [P, SEQ]) for i in range(2)]
        w_raw = [sb(f"w_raw{i}", [P, D]) for i in range(3)]
        w_hi, w_lo = sb("w_hi", [P, KT, D], F32R), sb("w_lo", [P, KT, D], F32R)
        ones = sb("ones", [P, 1])
        root, rstd = sb("root", [P, 2 * TT]), sb("rstd", [P, 2 * TT])
        o_loaded = [sem(f"out_o_loaded{i}") for i in range(3)]
        w_loaded = [sem(f"out_w_loaded{i}") for i in range(3)]
        x_loaded = [sem(f"out_x_loaded{t}") for t in range(TT)]
        o_hi_done, o_split, o_squared = sem("out_o_hi_done"), sem("out_o_split"), sem("out_o_squared")
        w_hi_done, w_split = sem("out_w_hi_done"), sem("out_w_split")
        ones_set, sums_ready, root_done, rstd_done = (sem(f"out_{n}") for n in ("ones", "sums", "root", "rstd"))
        y_ready, y_added = sem("out_y_ready"), sem("out_y_added")
        block = ctx.enter_context(nc.Block())
        BANK_SUM = 6

        @block.sync
        def _(sp):
            for f in range(KT):
                if f >= 3:
                    sp.wait_ge(o_split, f - 2)
                    sp.wait_ge(o_squared, f - 2)
                sp.dma_start(o_raw[f % 3][:, :], o_dram[f * P:(f + 1) * P, :]).then_inc(o_loaded[f % 3], 16)
                if f >= 3:
                    sp.wait_ge(w_split, f - 2)
                sp.dma_start(w_raw[f % 3][:, :], w_out[f * P:(f + 1) * P, :]).then_inc(w_loaded[f % 3], 16)
            for t in range(TT):
                sp.dma_start(b.x[:, t, :], x_dram[t * P:(t + 1) * P, :]).then_inc(x_loaded[t], 16)

        @block.scalar
        def _(act):
            for f in range(KT):
                act.wait_ge(o_loaded[f % 3], 16 * (f // 3 + 1))
                act.activation(b.xn_hi[:, f, :], o_raw[f % 3][:, :], ACT.Copy, scale=group_gain[:, f:f + 1]
                               ).then_inc(o_hi_done, 1)
                if f >= 2:
                    act.wait_ge(sums_ready, f - 1)
                act.activation(o_sq[f % 2][:, :], o_raw[f % 3][:, :], ACT.Square).then_inc(o_squared, 1)
                act.wait_ge(w_loaded[f % 3], 16 * (f // 3 + 1))
                act.activation(w_hi[:, f, :], w_raw[f % 3][:, :], ACT.Copy).then_inc(w_hi_done, 1)
            act.wait_ge(sums_ready, KT)
            act.activation(root[:, :], b.ps[:, BANK_SUM, 0:2 * TT], ACT.Sqrt, scale=1.0 / GROUP,
                           bias=b.eps[:, 0:1]).then_inc(root_done, 1)

        @block.vector
        def _(dve):
            dve.memset(ones[:, :], 1.0).then_inc(ones_set, 1)
            for f in range(KT):
                dve.wait_ge(o_hi_done, f + 1)
                dve.scalar_tensor_tensor(out=b.xn_lo[:, f, :], in0=o_raw[f % 3][:, :],
                                         scalar=group_gain[:, f:f + 1], in1=b.xn_hi[:, f, :].bitcast(F32),
                                         op0=ALU.mult, op1=ALU.subtract).then_inc(o_split, 1)
                dve.wait_ge(w_hi_done, f + 1)
                dve.tensor_tensor(w_lo[:, f, :], w_raw[f % 3][:, :], w_hi[:, f, :].bitcast(F32), ALU.subtract
                                  ).then_inc(w_split, 1)
            dve.wait_ge(root_done, 1)
            dve.reciprocal(rstd[:, :], root[:, :]).then_inc(rstd_done, 1)
            dve.wait_ge(rstd_done, 1)
            for t in range(TT):
                dve.wait_ge(x_loaded[t], 16)
                for half in range(2):
                    g = 2 * t + half
                    cols = slice(half * HALF, (half + 1) * HALF)
                    for group in range(2):
                        dve.wait_ge(y_ready, 2 * g + group + 1)
                        if group == 1:
                            dve.wait_ge(y_added, 2 * g + 1)
                        dve.scalar_tensor_tensor(out=b.x[:, t, cols], in0=b.ps[:, (2 * g + group) % 6, :],
                                                 scalar=rstd[:, group * TT + t:group * TT + t + 1],
                                                 in1=b.x[:, t, cols], op0=ALU.mult, op1=ALU.add
                                                 ).then_inc(y_added, 1)

        @block.tensor
        def _(pe):
            pe.wait_ge(ones_set, 1)
            for f in range(KT):
                pe.wait_ge(o_squared, f + 1)
                for t in range(TT):
                    c = (f // (KT // 2)) * TT + t
                    last = pe.matmul(b.ps[:, BANK_SUM, c:c + 1], o_sq[f % 2][:, t * P:(t + 1) * P], ones[:, :],
                                     start=(f == 0 and t == 0), stop=(f % (KT // 2) == KT // 2 - 1),
                                     skip_group_check=True)
                last.then_inc(sums_ready, 1)
            for t in range(TT):
                tok = slice(t * P, (t + 1) * P)
                for half in range(2):
                    cols = slice(half * HALF, (half + 1) * HALF)
                    for group in range(2):
                        m = 4 * t + 2 * half + group
                        out = b.ps[:, m % 6, :]
                        if m >= 6:
                            pe.wait_ge(y_added, m - 5)
                        for i in range(KT // 2):
                            f = group * (KT // 2) + i
                            if t == 0 and half == 0:
                                pe.wait_ge(o_split, f + 1)
                                pe.wait_ge(w_split, f + 1)
                            pe.matmul(out, b.xn_hi[:, f, tok], w_hi[:, f, cols], start=(i == 0), stop=False)
                            pe.matmul(out, b.xn_hi[:, f, tok], w_lo[:, f, cols], start=False, stop=False)
                            last = pe.matmul(out, b.xn_lo[:, f, tok], w_hi[:, f, cols], start=False,
                                             stop=(i == KT // 2 - 1))
                        last.then_inc(y_ready, 1)



class Buffers:
    pass


def constants():
    half = HEAD // 2
    inv_freq = np.float32(10000.0) ** (-np.arange(half, dtype=np.float32) / np.float32(half))
    ang = (np.arange(SEQ, dtype=np.float32)[None, :] * inv_freq[:, None]).astype(np.float32).astype(np.float64)
    cos, sin = np.cos(ang).astype(np.float32), np.sin(ang).astype(np.float32)
    cos_rows = np.concatenate([cos] * 4)
    sin_rows = np.concatenate([-sin, sin] * 2)
    ident = np.eye(P, dtype=np.float32)
    neg = np.where(np.arange(P)[None, :] < np.arange(P)[:, None], 0.0, NEG).astype(np.float32)
    dist = (SEQ - P) + np.arange(P)[:, None] - np.arange(SEQ)[None, :]
    count = np.zeros((P, SEQ))
    for window, dilation in ((128, 1), (512, 4), (2048, 16)):
        count += (dist >= 0) & (dist <= window) & (dist % dilation == 0)
    log_count = np.where(count > 0, np.log(np.maximum(count, 1.0)) / SCALE, NEG).astype(np.float32)
    return {"ident_c": ident, "neg_c": neg, "log_count_c": log_count, "cos_c": cos_rows, "sin_c": sin_rows}


def build(nc, a, out):
    x_dram = nc.dram_tensor("x_between", [SEQ, D], F32, kind="Internal").ap()
    o_dram = nc.dram_tensor("o_between", [D, SEQ], F32, kind="Internal").ap()
    with ExitStack() as ctx:
        def sem(name):
            return ctx.enter_context(nc.semaphore(name))

        def sb(name, shape, dt=F32):
            return ctx.enter_context(nc.sbuf_tensor(name, shape, dt))

        b = Buffers()
        b.ps = ctx.enter_context(nc.psum_tensor("banks", [P, 8, HALF], F32))
        b.ident = sb("ident_sb", [P, P])
        gains = sb("gains_sb", [P, 4, KT])
        b.eps, b.sumsq, b.root, b.rstd = sb("eps", [P, 1]), sb("sumsq", [P, TT]), sb("root", [P, TT]), sb("rstd", [P, TT])
        b.xn_hi, b.xn_lo = sb("xn_hi", [P, KT, SEQ], F32R), sb("xn_lo", [P, KT, SEQ], F32R)
        loaded, eps_set = sem("constants_loaded"), sem("eps_set")
        with nc.Block() as block:
            @block.sync
            def _(sp):
                sp.dma_start(b.ident[:, :], a["ident_c"]).then_inc(loaded, 16)
                for i, name in enumerate(("ffn1_norm", "mix_norm", "group_norm", "ffn2_norm")):
                    sp.dma_start(gains[:, i, :], a[name]).then_inc(loaded, 16)
                sp.wait_ge(loaded, 16 * 5)

            @block.vector
            def _(dve):
                dve.memset(b.eps[:, :], EPS).then_inc(eps_set, 1)

        with nc.sbuf_tensor("x_first", [P, TT, D], F32) as x_first:
            b.x = x_first
            b.gain = gains[:, 0, :]
            ffn_block(nc, b, sem, "ffn1", a["ffn1_w_gate"], a["ffn1_w_up"], a["ffn1_w_down"], None, a["x"],
                      x_dram, False)
            b.gain = gains[:, 1, :]
            mixer_norm_block(nc, b, sem)
        heads_block(nc, b, sem, a["w_in"], None, a["neg_c"], a["log_count_c"], a["cos_c"], a["sin_c"], o_dram)
        with (nc.sbuf_tensor("x_second", [P, TT, D], F32) as x_second,
              nc.sbuf_tensor("final_gain_sb", [P, D], F32) as final_gain):
            b.x = x_second
            output_block(nc, b, sem, o_dram, x_dram, a["w_out"], gains[:, 2, :])
            b.gain = gains[:, 3, :]
            b.final_gain = final_gain
            with nc.Block() as block:
                @block.sync
                def _(sp):
                    sp.dma_start(b.final_gain[:, :], a["final_norm"].to_broadcast([P, D])).then_inc(loaded, 16)
                    sp.wait_ge(loaded, 16 * 6)
            ffn_block(nc, b, sem, "ffn2", a["ffn2_w_gate"], a["ffn2_w_up"], a["ffn2_w_down"], None, None, out, True)


def kernel(**inputs):
    import concourse.bacc as bacc
    from concourse.bass_utils import run_bass_kernel_spmd as run

    nc = bacc.Bacc("TRN2", target_bir_lowering=False, num_devices=1, dynamic_dma_scratch_size=1024)

    def feature_tiles(v):
        return np.ascontiguousarray(v.reshape(-1, P).T)

    def column_blocks(w, width):
        return w.reshape(KT, P, -1, width).transpose(2, 1, 0, 3).reshape(-1, KT * width)

    i = {k: np.asarray(v) for k, v in inputs.items()}
    arrays = {
        "x": i["x"].reshape(SEQ, D),
        "ffn1_norm": feature_tiles(i["ffn1_norm"]),
        "mix_norm": feature_tiles(i["mix_norm"]),
        "group_norm": feature_tiles(np.concatenate([i["sb_out_norm"][0], i["dil_out_norm"][0]])),
        "ffn2_norm": feature_tiles(i["ffn2_norm"]),
        "final_norm": i["final_norm"].reshape(1, D),
        **constants(),
    }
    for name in ("ffn1_w_down", "w_out", "ffn2_w_down"):
        arrays[name] = i[name][0]
    for name in ("ffn1_w_gate", "ffn1_w_up", "ffn2_w_gate", "ffn2_w_up"):
        arrays[name] = column_blocks(i[name][0], CH * P)
    blocks = column_blocks(i["w_in"][0], P).reshape(2, 3, PAIRS, P, D)
    arrays["w_in"] = blocks[:, [2, 0, 1]].transpose(2, 0, 1, 3, 4).reshape(-1, D)
    arrays = {f"in_{k}": np.ascontiguousarray(v) for k, v in arrays.items()}
    a = {k[3:]: nc.dram_tensor(k, v.shape, F32, kind="ExternalInput").ap() for k, v in arrays.items()}
    out = nc.dram_tensor("out_dram", [SEQ, D], F32, kind="ExternalOutput").ap()
    build(nc, a, out)
    r = run(nc, [arrays], core_ids=[0])
    return r.results[0]["out_dram"].reshape(1, SEQ, D)
```

```python
from contextlib import ExitStack

import numpy as np

import concourse.bass as bass
from concourse import mybir

F32 = mybir.dt.float32
F32R = mybir.dt.float32r
ALU = mybir.AluOpType
ACT = mybir.ActivationFunctionType

P = 128
SEQ = 1024
D = 1024
DFF = 2816
HEAD = 64
HALF = 512
TT = SEQ // P
KT = D // P
CH = 2
NCH = DFF // (CH * P)
PAIRS = 4
GROUP = D // 2
EPS = 1e-6
SCALE = HEAD ** -0.5
NEG = -1e30



class Norm:

    def __init__(self, sem, tag, b, gain, xn_hi, xn_lo):
        self.b, self.gain, self.xn_hi, self.xn_lo = b, gain, xn_hi, xn_lo
        self.square = sem(f"{tag}_sum_of_squares")
        self.root = sem(f"{tag}_root")
        self.rstd = sem(f"{tag}_rstd")
        self.scaled = sem(f"{tag}_scaled")
        self.turned = sem(f"{tag}_turned")
        self.hi = sem(f"{tag}_hi_split")
        self.lo = sem(f"{tag}_lo_split")

    def row_root(self, act, x, t, squares):
        b = self.b
        if t >= 2:
            act.wait_ge(self.square, t - 1)
        act.activation(squares[t % 2], x[:, t, :], ACT.Square, accum_out=b.sumsq[:, t:t + 1]
                       ).then_inc(self.square, 1)
        act.wait_ge(self.square, t + 1)
        act.activation(b.root[:, t:t + 1], b.sumsq[:, t:t + 1], ACT.Sqrt, scale=1.0 / D,
                       bias=b.eps[:, 0:1]).then_inc(self.root, 1)

    def row_reciprocal(self, dve, t):
        b = self.b
        dve.wait_ge(self.root, t + 1)
        dve.reciprocal(b.rstd[:, t:t + 1], b.root[:, t:t + 1]).then_inc(self.rstd, 1)
        dve.wait_ge(self.rstd, t + 1)

    def row_scale(self, dve, x, t):
        self.row_reciprocal(dve, t)
        if t >= 4:
            dve.wait_ge(self.turned, 8)
        dve.tensor_scalar(self.b.scaled[:, t % 4, :], x[:, t, :], self.b.rstd[:, t:t + 1], None, ALU.mult
                          ).then_inc(self.scaled, 1)

    def turn(self, pe, r, bank, read=0):
        b, half, f = self.b, r // 2, 4 * (r % 2)
        if read:
            pe.wait_ge(self.lo, read)
        for i in range(4):
            pe.wait_ge(self.scaled, 4 * half + i + 1)
            for j in range(4):
                last = pe.transpose(b.ps[:, bank + j, i * P:(i + 1) * P],
                                    b.scaled[:, i, (f + j) * P:(f + j + 1) * P], b.ident[:, :])
                if i == 3:
                    last.then_inc(self.turned, 1)

    def hi_part(self, act, r, bank):
        half, f = r // 2, 4 * (r % 2)
        for j in range(4):
            act.wait_ge(self.turned, 4 * r + j + 1)
            act.activation(self.xn_hi[:, f + j, half * HALF:(half + 1) * HALF], self.b.ps[:, bank + j, :], ACT.Copy,
                           scale=self.gain[:, f + j:f + j + 1]).then_inc(self.hi, 1)

    def lo_part(self, dve, r, bank):
        half, f = r // 2, 4 * (r % 2)
        for j in range(4):
            cols = slice(half * HALF, (half + 1) * HALF)
            dve.wait_ge(self.hi, 4 * r + j + 1)
            dve.scalar_tensor_tensor(out=self.xn_lo[:, f + j, cols], in0=self.b.ps[:, bank + j, :],
                                     scalar=self.gain[:, f + j:f + j + 1],
                                     in1=self.xn_hi[:, f + j, cols].bitcast(F32),
                                     op0=ALU.mult, op1=ALU.subtract).then_inc(self.lo, 1)


def address(eng, value):
    return value if isinstance(value, int) else eng.snap(value)



def ffn_block(nc, b, sem, tag, weights, norm, next_norm, arena, store, x_from=None, next_weights=None,
              final_gain=None):
    with ExitStack() as ctx:
        def sb(name, shape, dt=F32):
            return ctx.enter_context(nc.sbuf_tensor(f"{tag}_{name}", shape, dt))

        w_gate, w_up, w_down = weights
        up_raw = sb("up_raw", [P, CH, KT, P])
        down_raw = sb("down_raw", [P, CH, D])
        h_hi = [arena[0][:, CH * k:CH * (k + 1), :] for k in range(2)]
        h_lo = [arena[0][:, CH * (k + 2):CH * (k + 3), :] for k in range(2)]
        down_hi, down_lo = arena[1][:, 0:CH, :], arena[1][:, CH:2 * CH, :]
        up_hi, up_lo = ([arena[1][:, 2 * CH + CH * part + t, :].rearrange("p (k c) -> p k c", k=KT)
                         for t in range(CH)] for part in range(2))
        gate_raw, gate_hi, gate_lo = b.w_raw, b.w_hi, b.w_lo
        gate_act = [b.scaled[:, 0, h * HALF:(h + 1) * HALF] for h in range(2)]
        h_full = [b.scaled[:, 1, h * HALF:(h + 1) * HALF] for h in range(2)]
        squares = [h_hi[1][:, i, :] for i in range(2)]
        x_loaded = [sem(f"{tag}_x_loaded{t}") for t in range(TT)]
        gain_loaded = sem(f"{tag}_final_gain_loaded")
        gate_loaded = [sem(f"{tag}_gate_loaded{t}") for t in range(CH)]
        up_loaded = [sem(f"{tag}_up_loaded{t}") for t in range(CH)]
        down_loaded = sem(f"{tag}_down_loaded")
        gate_hi_done = sem(f"{tag}_gate_hi_done")
        up_hi_done = sem(f"{tag}_up_hi_done")
        down_hi_done = sem(f"{tag}_down_hi_done")
        gate_split = sem(f"{tag}_gate_split")
        up_split = sem(f"{tag}_up_split")
        down_split = sem(f"{tag}_down_split")
        gate_ready = sem(f"{tag}_gate_ready")
        up_ready = sem(f"{tag}_up_ready")
        silu_done = sem(f"{tag}_silu_done")
        h_done = sem(f"{tag}_h_done")
        h_hi_done = sem(f"{tag}_h_hi_done")
        h_split = sem(f"{tag}_h_split")
        y_ready = sem(f"{tag}_y_ready")
        y_added = sem(f"{tag}_y_added")
        stored = sem(f"{tag}_stored")
        normed = sem(f"{tag}_normed")
        block = ctx.enter_context(nc.Block())

        BANK_Y = 4
        PAIRS_OF_CHUNKS = (NCH - 3) // 2

        @block.sync
        def _(sp):
            def load_columns(raw, w, first, t, loaded):
                sp.dma_start(raw[:, t, :, :], w[bass.ds(first, P), :].rearrange("p (k f) -> p k f", k=KT)
                             ).then_inc(loaded[t], 16)

            def load_down(first):
                sp.dma_start(down_raw[:, :, :], w_down[bass.ds(first, CH * P), :].rearrange(
                    "(t p) d -> p t d", p=P)).then_inc(down_loaded, 16)

            def chunk(c, first=False, last=False):
                here = address(sp, c * CH * P)
                ahead = [address(sp, (c + 1) * CH * P + t * P) for t in range(CH)]
                if not first:
                    sp.wait_ge(down_split, CH * c)
                load_down(here)
                if last and final_gain is not None:
                    return
                for t in range(CH):
                    sp.wait_ge(gate_split, CH * c + t + 1)
                    if last:
                        load_columns(gate_raw, next_weights, t * P, t, gate_loaded)
                        continue
                    load_columns(gate_raw, w_gate, ahead[t], t, gate_loaded)
                    sp.wait_ge(up_split, CH * c + t + 1)
                    load_columns(up_raw, w_up, ahead[t], t, up_loaded)

            def load_x(tiles):
                for t in tiles:
                    sp.dma_start(b.x[:, t, :], x_from[t * P:(t + 1) * P, :]).then_inc(x_loaded[t], 16)

            if x_from is None:
                sp.sem_inc(gate_loaded[0], 16)
                sp.sem_inc(gate_loaded[1], 16)
                sp.sem_inc(gate_hi_done, CH)
                sp.sem_inc(gate_split, CH)
            else:
                load_x(range(4))
                load_columns(gate_raw, w_gate, 0, 0, gate_loaded)
            load_columns(up_raw, w_up, 0, 0, up_loaded)
            if x_from is not None:
                load_x(range(4, TT))
                load_columns(gate_raw, w_gate, P, 1, gate_loaded)
            load_columns(up_raw, w_up, P, 1, up_loaded)
            chunk(0, first=True)
            if final_gain is not None:
                sp.dma_start(b.final_gain[:, :], final_gain.to_broadcast([P, D])).then_inc(gain_loaded, 16)
            with sp.Fori(0, PAIRS_OF_CHUNKS) as i:
                chunk(2 * i + 1)
                chunk(2 * i + 2)
            chunk(NCH - 2)
            chunk(NCH - 1, last=True)
            for t in range(TT):
                if final_gain is not None:
                    sp.wait_ge(normed, t + 1)
                else:
                    sp.wait_ge(y_added, 4 + 16 * (NCH - 1) + 2 * t + 2)
                sp.dma_start(store[t * P:(t + 1) * P, :], b.x[:, t, :]).then_inc(stored, 16)
            sp.wait_ge(stored, 16 * TT)

        @block.scalar
        def _(act):
            def split_gate(c, t):
                act.wait_ge(gate_loaded[t], 16 * (c + 1))
                act.activation(gate_hi[t][:, :, :], gate_raw[:, t, :, :], ACT.Copy).then_inc(gate_hi_done, 1)

            def split_up(c, t):
                act.wait_ge(up_loaded[t], 16 * (c + 1))
                act.activation(up_hi[t], up_raw[:, t, :, :], ACT.Copy).then_inc(up_hi_done, 1)

            def split_down(c):
                act.wait_ge(y_ready, 16 * c + 1)
                act.wait_ge(down_loaded, 16 * (c + 1))
                for t in range(CH):
                    act.activation(down_hi[:, t, :], down_raw[:, t, :], ACT.Copy).then_inc(down_hi_done, 1)

            def chunk(c, k, first=False, last=False):
                if not first:
                    split_down(c - 1)
                for t in range(CH):
                    for half in range(2):
                        n = 2 * CH * c + 2 * t + half
                        cols = slice(half * HALF, (half + 1) * HALF)
                        act.wait_ge(gate_ready, n + 1)
                        if not (first and t == 0):
                            act.wait_ge(h_done, n - 1)
                        act.activation(gate_act[half], b.ps[:, half, :], ACT.Silu).then_inc(silu_done, 1)
                        act.wait_ge(h_done, n + 1)
                        act.activation(h_hi[k][:, t, cols], h_full[half], ACT.Copy).then_inc(h_hi_done, 1)
                    if not last:
                        split_gate(c + 1, t)
                        split_up(c + 1, t)

            if x_from is not None:
                for t in range(4):
                    act.wait_ge(x_loaded[t], 16)
                    norm.row_root(act, b.x, t, squares)
                norm.hi_part(act, 0, BANK_Y)
                split_gate(0, 0)
                norm.hi_part(act, 1, 0)
                split_up(0, 0)
                for t in range(4, TT):
                    act.wait_ge(x_loaded[t], 16)
                    norm.row_root(act, b.x, t, squares)
                norm.hi_part(act, 2, BANK_Y)
            else:
                norm.hi_part(act, 2, BANK_Y)
                split_up(0, 0)
            norm.hi_part(act, 3, BANK_Y)
            if x_from is not None:
                split_gate(0, 1)
            split_up(0, 1)
            chunk(0, 0, first=True)
            with act.Fori(0, PAIRS_OF_CHUNKS) as i:
                chunk(2 * i + 1, 1)
                chunk(2 * i + 2, 0)
            chunk(NCH - 2, (NCH - 2) % 2)
            chunk(NCH - 1, (NCH - 1) % 2, last=True)
            split_down(NCH - 1)
            if final_gain is None:
                for t in range(CH):
                    split_gate(NCH, t)
            for t in range(TT):
                act.wait_ge(y_added, 4 + 16 * (NCH - 1) + 2 * t + 2)
                next_norm.row_root(act, b.x, t, squares)
                if final_gain is None and t in NORM_ROUNDS:
                    next_norm.hi_part(act, NORM_ROUNDS[t], 0)

        @block.vector
        def _(dve):
            def split_gate(c, t):
                dve.wait_ge(gate_hi_done, CH * c + t + 1)
                dve.tensor_tensor(gate_lo[t][:, :, :], gate_raw[:, t, :, :], gate_hi[t][:, :, :].bitcast(F32),
                                  ALU.subtract).then_inc(gate_split, 1)

            def split_up(c, t):
                dve.wait_ge(up_hi_done, CH * c + t + 1)
                dve.tensor_tensor(up_lo[t], up_raw[:, t, :, :], up_hi[t].bitcast(F32), ALU.subtract
                                  ).then_inc(up_split, 1)

            def split_down(c):
                for t in range(CH):
                    dve.wait_ge(down_hi_done, CH * c + t + 1)
                    dve.tensor_tensor(down_lo[:, t, :], down_raw[:, t, :], down_hi[:, t, :].bitcast(F32),
                                      ALU.subtract).then_inc(down_split, 1)

            def add_down(c, t):
                for half in range(2):
                    g = 2 * t + half
                    dve.wait_ge(y_ready, 1 + 16 * c + g + 1)
                    cols = slice(half * HALF, (half + 1) * HALF)
                    dve.scalar_tensor_tensor(out=b.x[:, t, cols], in0=b.ps[:, BANK_Y + g % 4, :], scalar=0.5,
                                             in1=b.x[:, t, cols], op0=ALU.mult, op1=ALU.add
                                             ).then_inc(y_added, 1)

            def chunk(c, k, first=False, last=False):
                if not first:
                    split_down(c - 1)
                for t in range(CH):
                    for half in range(2):
                        n = 2 * CH * c + 2 * t + half
                        cols = slice(half * HALF, (half + 1) * HALF)
                        dve.wait_ge(silu_done, n + 1)
                        dve.wait_ge(up_ready, n + 1)
                        if not (first and t == 0):
                            dve.wait_ge(h_split, n - 1)
                        dve.tensor_tensor(h_full[half], b.ps[:, 2 + half, :], gate_act[half], ALU.mult
                                          ).then_inc(h_done, 1)
                        dve.wait_ge(h_hi_done, n + 1)
                        dve.tensor_tensor(h_lo[k][:, t, cols], h_full[half], h_hi[k][:, t, cols].bitcast(F32),
                                          ALU.subtract).then_inc(h_split, 1)
                    if not last:
                        split_gate(c + 1, t)
                        split_up(c + 1, t)
                if not first:
                    for t in range(TT):
                        add_down(c - 1, t)

            def normed_result(t):
                next_norm.row_reciprocal(dve, t)
                dve.scalar_tensor_tensor(out=b.x[:, t, :], in0=b.x[:, t, :], scalar=b.rstd[:, t:t + 1],
                                         in1=b.final_gain[:, :], op0=ALU.mult, op1=ALU.mult).then_inc(normed, 1)

            if x_from is not None:
                for t in range(4):
                    norm.row_scale(dve, b.x, t)
                norm.lo_part(dve, 0, BANK_Y)
                split_gate(0, 0)
                norm.lo_part(dve, 1, 0)
                split_up(0, 0)
                for t in range(4, TT):
                    norm.row_scale(dve, b.x, t)
                norm.lo_part(dve, 2, BANK_Y)
            else:
                norm.lo_part(dve, 2, BANK_Y)
                split_up(0, 0)
            norm.lo_part(dve, 3, BANK_Y)
            if x_from is not None:
                split_gate(0, 1)
            split_up(0, 1)
            chunk(0, 0, first=True)
            with dve.Fori(0, PAIRS_OF_CHUNKS) as i:
                chunk(2 * i + 1, 1)
                chunk(2 * i + 2, 0)
            chunk(NCH - 2, (NCH - 2) % 2)
            chunk(NCH - 1, (NCH - 1) % 2, last=True)
            split_down(NCH - 1)
            if final_gain is None:
                for t in range(CH):
                    split_gate(NCH, t)
            else:
                dve.wait_ge(gain_loaded, 16)
            for t in range(TT):
                add_down(NCH - 1, t)
                if final_gain is None:
                    norm_vector_step(dve, next_norm, b.x, t, 0)
                elif t > 0:
                    normed_result(t - 1)
            if final_gain is not None:
                normed_result(TT - 1)

        @block.tensor
        def _(pe):
            def product(bank, hi, lo, half):
                cols = slice(half * HALF, (half + 1) * HALF)
                for k in range(KT):
                    pe.matmul(b.ps[:, bank, :], hi[:, k, :], norm.xn_hi[:, k, cols], start=(k == 0), stop=False)
                    pe.matmul(b.ps[:, bank, :], hi[:, k, :], norm.xn_lo[:, k, cols], start=False, stop=False)
                    last = pe.matmul(b.ps[:, bank, :], lo[:, k, :], norm.xn_hi[:, k, cols], start=False,
                                     stop=(k == KT - 1))
                return last

            def up_products(c, t, first=False):
                for half in range(2):
                    n = 2 * CH * c + 2 * t + half
                    if not first:
                        pe.wait_ge(silu_done, n - 1)
                    elif half == 1:
                        pe.wait_ge(norm.lo, 16)
                    elif x_from is None:
                        norm.turn(pe, 2, BANK_Y)
                    else:
                        pe.wait_ge(norm.lo, 8)
                    if half == 0:
                        pe.wait_ge(gate_split, CH * c + t + 1)
                    product(half, gate_hi[t], gate_lo[t], half).then_inc(gate_ready, 1)
                    if not first:
                        pe.wait_ge(h_done, n - 1)
                    elif half == 0 and x_from is None:
                        norm.turn(pe, 3, BANK_Y, 12)
                    elif half == 0:
                        norm.turn(pe, 2, BANK_Y)
                    if half == 0:
                        pe.wait_ge(up_split, CH * c + t + 1)
                    product(2 + half, up_hi[t], up_lo[t], half).then_inc(up_ready, 1)
                    if first and half == 0 and x_from is not None:
                        norm.turn(pe, 3, BANK_Y, 12)

            def down_products(c, k, t):
                for half in range(2):
                    g = 2 * t + half
                    pe.wait_ge(y_added, 16 * c + g + 1)
                    tok, cols = slice(t * P, (t + 1) * P), slice(half * HALF, (half + 1) * HALF)
                    for f in range(CH):
                        out = b.ps[:, BANK_Y + g % 4, :]
                        pe.matmul(out, h_hi[k][:, f, tok], down_hi[:, f, cols], start=(f == 0), stop=False)
                        pe.matmul(out, h_hi[k][:, f, tok], down_lo[:, f, cols], start=False, stop=False)
                        last = pe.matmul(out, h_lo[k][:, f, tok], down_hi[:, f, cols], start=False,
                                         stop=(f == CH - 1))
                    last.then_inc(y_ready, 1)

            def chunk(c, k, first=False):
                for t in range(CH):
                    up_products(c, t, first and t == 0)
                if not first:
                    pe.wait_ge(h_split, 2 * CH * c)
                    pe.wait_ge(down_split, CH * c)
                    for t in range(TT):
                        down_products(c - 1, 1 - k, t)

            pe.sem_inc(y_added, 4)
            pe.sem_inc(y_ready, 1)
            if x_from is not None:
                norm.turn(pe, 0, BANK_Y)
                norm.turn(pe, 1, 0)
            chunk(0, 0, first=True)
            with pe.Fori(0, PAIRS_OF_CHUNKS) as i:
                chunk(2 * i + 1, 1)
                chunk(2 * i + 2, 0)
            chunk(NCH - 2, (NCH - 2) % 2)
            chunk(NCH - 1, (NCH - 1) % 2)
            pe.wait_ge(h_split, 2 * CH * NCH)
            pe.wait_ge(down_split, CH * NCH)
            for t in range(TT):
                down_products(NCH - 1, (NCH - 1) % 2, t)
                if final_gain is None and t in TURN_ROUNDS:
                    next_norm.turn(pe, TURN_ROUNDS[t], 0, 4 * TURN_ROUNDS[t])


TURN_ROUNDS = {4: 0, 5: 1}
NORM_ROUNDS = {5: 0, 6: 1}


def norm_vector_step(dve, norm, x, t, bank):
    if t in NORM_ROUNDS:
        norm.lo_part(dve, NORM_ROUNDS[t], bank)
    elif 0 < t < 5:
        norm.row_scale(dve, x, t - 1)
    for row in {6: (4, 5), 7: (6, 7)}.get(t, ()):
        norm.row_scale(dve, x, row)



STEPS = 8
QG = 256
SB_KIND, DIL_KIND = 0, 1
HALVES = 6
Q, K, V = 0, 1, 2
PRODUCTS = ((Q, 0), (K, 0), (Q, 1), (K, 1), (V, 0), (V, 1))
ROTATED = 4
UNITS = ((2, 2), (1, 2, 1), (2, 2, 2, 2), (1, 2, 2, 2, 1), (4, 4), (1, 2, 1), (1, 1, 1, 1), (1, 1, 1, 2, 3))
ENDS = {1: 0, 2: 1, 3: 2, 4: 3, 6: 4, 7: 5}
TURNS = 22


def turn_index(s, j, v_turn):
    return 1 + sum(u % 4 + 1 for u in range(s)) + j + (v_turn and s == STEPS - 1)


def v_turned_in(it, kind, s, project):
    if s == 0:
        return it, kind, 1
    if s == STEPS - 1 and project:
        return it + (kind + 1) // 2, (kind + 1) % 2, 0
    return None


def units_between(s, j):
    start = sum(map(sum, UNITS[:s])) + sum(UNITS[s][:j])
    return start, start + UNITS[s][j]


def heads_block(nc, b, sem, norm, w_in, neg_mask, log_count, cos, sin, o_dram):
    with ExitStack() as ctx:
        def sb(name, shape, dt=F32):
            return ctx.enter_context(nc.sbuf_tensor(f"heads_{name}", shape, dt))

        w_raw, w_hi, w_lo = [b.w_raw[:, i, :, :] for i in range(2)], b.w_hi, b.w_lo
        qk_hi = [[sb(f"{n}_hi{kind}", [P, SEQ], F32R) for n in "qk"] for kind in range(2)]
        qk_lo = [[sb(f"{n}_lo{kind}", [P, SEQ], F32R) for n in "qk"] for kind in range(2)]
        v_both = [sb(f"v_both{kind}", [P, TT, 2, P], F32R) for kind in range(2)]
        o_low = sb("o_low", [HEAD, QG])
        v_turned = sb("v_feature_major", [P, HALF])
        weight = [[b.scaled[:, 2 * s + a, :] for a in range(2)] for s in range(2)]
        stay = [[sb(f"stay{s}{a}", [P, SEQ + 1]) for a in range(2)] for s in range(2)]
        wt_hi = sb("wt_hi", [P, TT, QG], F32R)
        wt_lo = sb("wt_lo", [P, TT, QG], F32R)
        o_stage = sb("o_stage", [P, SEQ])
        cos_sb, sin_sb = sb("cos", [P, SEQ]), sb("sin", [P, SEQ])
        log_count_sb = sb("log_count", [P, SEQ])
        rot_in, rot_swap, rot_out = sb("rot_in", [P, HALF]), sb("rot_swap", [P, HALF]), sb("rot_out", [P, HALF])
        neg_f = sb("neg_f", [P, P])
        neg_r, ident_r = sb("neg_r", [P, P], F32R), sb("ident_r", [P, P], F32R)
        row_max, neg_max, row_sum, row_inv = (sb(n, [P, 4]) for n in ("row_max", "neg_max", "row_sum", "row_inv"))

        tables_loaded = sem("tables_loaded")
        tables_ready = sem("tables_ready")
        w_loaded = [sem(f"w_loaded{i}") for i in range(2)]
        w_hi_done, w_split = sem("w_hi_done"), sem("w_split")
        proj_ready, proj_free = sem("proj_ready"), sem("proj_free")
        sb_hi_done = sem("sb_qk_hi_done")
        rot_swapped, rot_cos, rot_sin, rot_sum = (sem(f"rot_{n}") for n in ("swapped", "cos", "sin", "sum"))
        rot_hi_done, rot_split = sem("rot_hi_done"), sem("rot_split")
        z_ready = sem("z_ready")
        gates_ready, products_ready, sb_weights = sem("gates_ready"), sem("products_ready"), sem("sb_weights")
        dil_max, dil_negmax, dil_exp, dil_inv, dil_weights = (
            sem(f"dil_{n}") for n in ("max", "negmax", "exp", "inv", "weights"))
        scores_seen = sem("dil_scores_seen")
        turned, turn_hi_done, turn_split = sem("turned"), sem("turn_hi_done"), sem("turn_split")
        pv_ready, o_low_done, o_copied = sem("pv_ready"), sem("o_low_done"), sem("o_copied")
        o_stored = [sem(f"o_stored{h}") for h in range(2)]
        block = ctx.enter_context(nc.Block())

        BANK_PV, BANK_TURN, BANK_PROJ = 4, 5, 7
        z = [b.ps[:, 2 * a:2 * a + 2, :].rearrange("p a c -> p (a c)") for a in range(2)]

        def pair_of(it, kind, ahead):
            k = kind + ahead
            return it + k // 2, k % 2

        def run(it, kind):
            return 2 * it + kind

        @block.sync
        def _(sp):
            def load_weights(it, kind, piece):
                n = 3 * kind + piece
                slot = n % 2
                first = address(sp, (6 * it + n) * P)
                sp.wait_ge(w_split, 2 + 6 * it + n - 1)
                sp.dma_start(w_raw[slot][:, :, :], w_in[bass.ds(first, P), :].rearrange(
                    "p (k c) -> p k c", k=KT)).then_inc(w_loaded[slot], 16)

            def store_head(it, kind, head):
                rows = slice(head * HEAD, (head + 1) * HEAD)
                first = address(sp, kind * GROUP + it * P + head * HEAD)
                sp.wait_ge(o_copied, 1 + STEPS * run(it, kind) + 4 * head + 4)
                sp.dma_start(o_dram[bass.ds(first, HEAD), :], o_stage[rows, :]
                             ).then_inc(o_stored[head], 16)

            def one_run(it, kind, project=True, more=True):
                it1, kind1 = pair_of(it, kind, 1)
                it2, kind2 = pair_of(it, kind, 2)
                if project:
                    load_weights(it1, kind1, V)
                if more:
                    load_weights(it2, kind2, Q)
                store_head(it, kind, 0)
                if more:
                    load_weights(it2, kind2, K)
                store_head(it, kind, 1)

            sp.sem_inc(w_split, 4)
            sp.sem_inc(w_hi_done, 2)
            sp.sem_inc(w_loaded[0], 16)
            sp.sem_inc(w_loaded[1], 16)
            load_weights(0, 0, V)
            for dst, src in ((neg_f, neg_mask), (log_count_sb, log_count), (cos_sb, cos), (sin_sb, sin)):
                sp.dma_start(dst[:, :], src[:, :]).then_inc(tables_loaded, 16)
            load_weights(0, 1, Q)
            load_weights(0, 1, K)
            sp.sem_inc(o_stored[0], 16)
            sp.sem_inc(o_stored[1], 16)
            with sp.Fori(0, PAIRS - 1) as it:
                one_run(it, SB_KIND)
                one_run(it, DIL_KIND)
            one_run(PAIRS - 1, SB_KIND, more=False)
            one_run(PAIRS - 1, DIL_KIND, project=False, more=False)
            for h in range(2):
                sp.wait_ge(o_stored[h], 16 * (2 * PAIRS + 1))

        @block.gpsimd
        def _(pool):
            def products(it, s):
                for a in range(2):
                    nk = P * (2 * (s % 4) + a + 1)
                    beta = weight[s % 2][a][:, SEQ - nk:SEQ]
                    pool.wait_ge(products_ready, 2 * STEPS * it + 2 * s + a + 1)
                    pool.tensor_tensor(beta, beta, stay[s % 2][a][:, SEQ - nk + 1:SEQ + 1], ALU.mult
                                       ).then_inc(sb_weights, 1)

            def rotate_cos(it, j):
                half = PRODUCTS[j][1]
                n = ROTATED * it + j
                pool.wait_ge(proj_free, 1 + HALVES * run(it, DIL_KIND) + j + 1)
                pool.wait_ge(rot_split, 1 + n)
                pool.tensor_tensor(rot_out[:, :], rot_in[:, :], cos_sb[:, half * HALF:(half + 1) * HALF],
                                   ALU.mult).then_inc(rot_cos, 1)

            def step(it, kind, s, project=True, last=False):
                it1, kind1 = pair_of(it, kind, 1)
                if s < STEPS - 1:
                    if kind == SB_KIND:
                        products(it, s + 1)
                elif not last and kind1 == SB_KIND:
                    products(it1, 0)
                if project and kind1 == DIL_KIND and ENDS.get(s, HALVES) < ROTATED:
                    rotate_cos(it1, ENDS[s])

            def one_run(it, kind, project=True, last=False):
                for s in range(STEPS):
                    step(it, kind, s, project, last)

            pool.wait_ge(tables_ready, 1)
            products(0, 0)
            with pool.Fori(0, PAIRS - 1) as it:
                one_run(it, SB_KIND)
                one_run(it, DIL_KIND)
            one_run(PAIRS - 1, SB_KIND)
            one_run(PAIRS - 1, DIL_KIND, project=False, last=True)

        @block.scalar
        def _(act):
            def split_weights(it, kind, piece):
                n = 3 * kind + piece
                slot = n % 2
                act.wait_ge(w_loaded[slot], 16 * (3 * it + n // 2 + 1))
                done = {Q: -2, K: 0, V: 3}[piece]
                if not (piece != V and isinstance(it, int) and run(it, kind) == 0):
                    act.wait_ge(proj_ready, 1 + HALVES * run(it, kind) + done)
                act.activation(w_hi[slot][:, :, :], w_raw[slot][:, :, :], ACT.Copy).then_inc(w_hi_done, 1)

            def gates(it, s, a):
                nk = P * (2 * (s % 4) + a + 1)
                keys = slice(SEQ - nk, SEQ)
                act.wait_ge(z_ready, 1 + 2 * STEPS * run(it, SB_KIND) + 2 * s + a + 1)
                if not (isinstance(it, int) and it == 0 and s == 0):
                    act.wait_ge(turned, stage_free(it, SB_KIND, s))
                act.activation(weight[s % 2][a][:, keys], z[a][:, 0:nk], ACT.Sigmoid, scale=SCALE)
                act.activation(stay[s % 2][a][:, keys], z[a][:, 0:nk], ACT.Sigmoid, scale=-SCALE
                               ).then_inc(gates_ready, 1)

            def exponentials(it, s, a):
                nk = P * (2 * (s % 4) + a + 1)
                keys = slice(SEQ - nk, SEQ)
                c = 2 * (s % 2) + a
                act.wait_ge(dil_negmax, 2 * STEPS * it + 2 * s + a + 1)
                act.activation(weight[s % 2][a][:, keys], weight[s % 2][a][:, keys], ACT.Exp, scale=SCALE,
                               bias=neg_max[:, c:c + 1], accum_out=row_sum[:, c:c + 1]).then_inc(dil_exp, 1)

            def elementwise(it, kind, s, a):
                if kind == SB_KIND:
                    gates(it, s, a)
                else:
                    exponentials(it, s, a)

            def weights_hi(it, kind, s, j, v_turn):
                n = 1 + TURNS * run(it, kind) + turn_index(s, j, v_turn)
                bank = BANK_TURN + turn_index(s, j, v_turn) % 2
                if j == 0:
                    act.wait_ge(pv_ready, 1 + STEPS * run(it, kind) + s)
                act.wait_ge(turned, n + 1)
                for dst, cols in turn_parts(wt_hi, s, j):
                    last = act.activation(dst, b.ps[:, bank, cols], ACT.Copy)
                last.then_inc(turn_hi_done, 1)

            def v_hi_part(it, kind, half, n, bank):
                act.wait_ge(turned, n + 1)
                act.activation(v_both[kind][:, 4 * half:4 * half + 4, :, 0:HEAD],
                               b.ps[:, bank, :].rearrange("p (t h c) -> p t h c", h=2, c=HEAD), ACT.Copy
                               ).then_inc(turn_hi_done, 1)

            def projected(it, kind, j):
                piece, half = PRODUCTS[j]
                cols = slice(half * HALF, (half + 1) * HALF)
                act.wait_ge(proj_ready, 1 + HALVES * run(it, kind) + j + 1)
                if piece == V:
                    act.activation(v_turned[:, :], b.ps[:, BANK_PROJ, :], ACT.Copy).then_inc(proj_free, 1)
                elif kind == SB_KIND:
                    act.activation(qk_hi[kind][piece][:, cols], b.ps[:, BANK_PROJ, :], ACT.Copy
                                   ).then_inc(sb_hi_done, 1)
                else:
                    act.wait_ge(rot_split, 1 + ROTATED * it + j)
                    act.activation(rot_in[:, :], b.ps[:, BANK_PROJ, :], ACT.Copy).then_inc(proj_free, 1)
                    act.wait_ge(proj_free, 1 + HALVES * run(it, kind) + j + 1)
                    for head in range(2):
                        for part in range(2):
                            src = head * HEAD + part * 32
                            dst = head * HEAD + (1 - part) * 32
                            act.dma_start(rot_swap[dst:dst + 32, :], rot_in[src:src + 32, :]
                                          ).then_inc(rot_swapped, 16)

            def rotated_hi(it, j):
                piece, half = PRODUCTS[j]
                act.wait_ge(rot_sum, ROTATED * it + j + 1)
                act.activation(qk_hi[DIL_KIND][piece][:, half * HALF:(half + 1) * HALF], rot_out[:, :],
                               ACT.Copy).then_inc(rot_hi_done, 1)

            def values_low(it, kind, s):
                act.wait_ge(pv_ready, 1 + STEPS * run(it, kind) + s + 1)
                act.activation(o_low[:, :], b.ps[HEAD:P, BANK_PV, 0:QG], ACT.Copy).then_inc(o_low_done, 1)

            def step(it, kind, s, project=True, last=False):
                it1, kind1 = pair_of(it, kind, 1)
                it2, kind2 = pair_of(it, kind, 2)
                nit, nkind, ns = (it, kind, s + 1) if s < STEPS - 1 else (it1, kind1, 0)
                ahead = not (last and s == STEPS - 1)
                if ahead:
                    elementwise(nit, nkind, ns, 0)
                if s > 0:
                    values_low(it, kind, s - 1)
                if project and s == 4:
                    split_weights(it1, kind1, V)
                if v_turned_in(it, kind, s, project):
                    i = turn_index(s, -1, True)
                    v_hi_part(*v_turned_in(it, kind, s, project), 1 + TURNS * run(it, kind) + i, BANK_TURN + i % 2)
                for j in range(s % 4 + 1):
                    weights_hi(it, kind, s, j, project)
                    if j == 0 and ahead:
                        elementwise(nit, nkind, ns, 1)
                    if j == 1 and s == 7 and more_after(it, project):
                        split_weights(it2, kind2, Q)
                if project and kind1 == DIL_KIND and ENDS.get(s - 1, HALVES) < ROTATED:
                    rotated_hi(it1, ENDS[s - 1])
                if project and s == 0:
                    split_weights(it1, kind1, K)
                if project and s in ENDS:
                    projected(it1, kind1, ENDS[s])
                if s == STEPS - 1:
                    values_low(it, kind, s)

            def one_run(it, kind, project=True, last=False):
                for s in range(STEPS):
                    step(it, kind, s, project, last)

            norm.hi_part(act, 2, 0)
            for j in range(HALVES):
                projected(0, 0, j)
                if j == 0:
                    norm.hi_part(act, 3, 0)
                if j == 2:
                    split_weights(0, 0, V)
                if j == 3:
                    split_weights(0, 1, Q)
                if j == 4:
                    v_hi_part(0, 0, 0, 0, BANK_TURN + 1)
            elementwise(0, SB_KIND, 0, 0)
            elementwise(0, SB_KIND, 0, 1)
            with act.Fori(0, PAIRS - 1) as it:
                one_run(it, SB_KIND)
                one_run(it, DIL_KIND)
            one_run(PAIRS - 1, SB_KIND)
            one_run(PAIRS - 1, DIL_KIND, project=False, last=True)

        @block.vector
        def _(dve):
            def split_weights(it, kind, piece):
                n = 3 * kind + piece
                slot = n % 2
                dve.wait_ge(w_hi_done, 6 * it + n + 1)
                dve.tensor_tensor(w_lo[slot][:, :, :], w_raw[slot][:, :, :], w_hi[slot][:, :, :].bitcast(F32),
                                  ALU.subtract).then_inc(w_split, 1)

            def scan(it, s, a):
                nk = P * (2 * (s % 4) + a + 1)
                dve.wait_ge(gates_ready, 2 * STEPS * it + 2 * s + a + 1)
                back = stay[s % 2][a][:, SEQ - nk:SEQ][:, ::-1]
                dve.tensor_tensor_scan(back, back, back, 1.0, ALU.mult, ALU.min).then_inc(products_ready, 1)

            def masked_max(it, s, a):
                i = 2 * (s % 4) + a
                nk = P * (i + 1)
                keys = slice(SEQ - nk, SEQ)
                c = 2 * (s % 2) + a
                dve.wait_ge(z_ready, 1 + 2 * STEPS * run(it, DIL_KIND) + 2 * s + a + 1)
                dve.wait_ge(turned, stage_free(it, DIL_KIND, s))
                dve.wait_ge(tables_loaded, 16 * 4)
                dve.sem_inc(scores_seen, 1)
                dve.tensor_tensor_reduce(weight[s % 2][a][:, keys], z[a][:, 0:nk], log_count_sb[:, keys], 1.0,
                                         -3e38, ALU.add, ALU.max, row_max[:, c:c + 1]).then_inc(dil_max, 1)
                dve.wait_ge(dil_max, 2 * STEPS * it + 2 * s + a + 1)
                dve.tensor_scalar(neg_max[:, c:c + 1], row_max[:, c:c + 1], -SCALE, None, ALU.mult
                                  ).then_inc(dil_negmax, 1)

            def normalize(it, s, a):
                nk = P * (2 * (s % 4) + a + 1)
                keys = slice(SEQ - nk, SEQ)
                c = 2 * (s % 2) + a
                n = 2 * STEPS * it + 2 * s + a + 1
                dve.wait_ge(dil_exp, n)
                dve.reciprocal(row_inv[:, c:c + 1], row_sum[:, c:c + 1]).then_inc(dil_inv, 1)
                dve.wait_ge(dil_inv, n)
                dve.tensor_scalar(weight[s % 2][a][:, keys], weight[s % 2][a][:, keys], row_inv[:, c:c + 1], None,
                                  ALU.mult).then_inc(dil_weights, 1)

            def elementwise(it, kind, s, a):
                if kind == SB_KIND:
                    scan(it, s, a)
                else:
                    masked_max(it, s, a)

            def weights_lo(it, kind, s, j, v_turn):
                n = 1 + TURNS * run(it, kind) + turn_index(s, j, v_turn)
                bank = BANK_TURN + turn_index(s, j, v_turn) % 2
                dve.wait_ge(turn_hi_done, n + 1)
                for (dst, cols), (hi, _) in zip(turn_parts(wt_lo, s, j), turn_parts(wt_hi, s, j)):
                    last = dve.tensor_tensor(dst, b.ps[:, bank, cols], hi.bitcast(F32), ALU.subtract)
                last.then_inc(turn_split, 1)

            def v_lo_part(it, kind, half, n, bank):
                dve.wait_ge(turn_hi_done, n + 1)
                part = slice(4 * half, 4 * half + 4)
                dve.tensor_tensor(v_both[kind][:, part, :, HEAD:P],
                                  b.ps[:, bank, :].rearrange("p (t h c) -> p t h c", h=2, c=HEAD),
                                  v_both[kind][:, part, :, 0:HEAD].bitcast(F32), ALU.subtract
                                  ).then_inc(turn_split, 1)

            def values_out(it, kind, s):
                head, g = s // 4, s % 4
                rows = slice(head * HEAD, (head + 1) * HEAD)
                if g == 0:
                    dve.wait_ge(o_stored[head], 16 * (run(it, kind) + 1))
                dve.wait_ge(o_low_done, STEPS * run(it, kind) + s + 1)
                dve.tensor_tensor(o_stage[rows, g * QG:(g + 1) * QG], b.ps[0:HEAD, BANK_PV, 0:QG], o_low[:, :],
                                  ALU.add).then_inc(o_copied, 1)

            def projected_lo(it, j):
                piece, half = PRODUCTS[j]
                cols = slice(half * HALF, (half + 1) * HALF)
                dve.wait_ge(sb_hi_done, ROTATED * it + j + 1)
                dve.tensor_tensor(qk_lo[SB_KIND][piece][:, cols], b.ps[:, BANK_PROJ, :],
                                  qk_hi[SB_KIND][piece][:, cols].bitcast(F32), ALU.subtract
                                  ).then_inc(proj_free, 1)

            def rotate(it, j):
                half = PRODUCTS[j][1]
                cols = slice(half * HALF, (half + 1) * HALF)
                n = ROTATED * it + j
                dve.wait_ge(rot_swapped, 64 * (n + 1))
                dve.tensor_tensor(rot_swap[:, :], rot_swap[:, :], sin_sb[:, cols], ALU.mult).then_inc(rot_sin, 1)
                dve.wait_ge(rot_sin, n + 1)
                dve.wait_ge(rot_cos, n + 1)
                dve.tensor_tensor(rot_out[:, :], rot_out[:, :], rot_swap[:, :], ALU.add).then_inc(rot_sum, 1)

            def rotated_lo(it, j):
                piece, half = PRODUCTS[j]
                cols = slice(half * HALF, (half + 1) * HALF)
                dve.wait_ge(rot_hi_done, ROTATED * it + j + 1)
                dve.tensor_tensor(qk_lo[DIL_KIND][piece][:, cols], rot_out[:, :],
                                  qk_hi[DIL_KIND][piece][:, cols].bitcast(F32), ALU.subtract
                                  ).then_inc(rot_split, 1)

            def step(it, kind, s, project=True, last=False):
                it1, kind1 = pair_of(it, kind, 1)
                it2, kind2 = pair_of(it, kind, 2)
                nit, nkind, ns = (it, kind, s + 1) if s < STEPS - 1 else (it1, kind1, 0)
                ahead = not (last and s == STEPS - 1)
                rot = None
                if project and kind1 == DIL_KIND and ENDS.get(s - 1, HALVES) < ROTATED:
                    rot = (it1, ENDS[s - 1])
                if ahead:
                    elementwise(nit, nkind, ns, 0)
                if s > 0:
                    values_out(it, kind, s - 1)
                if project and s == 4:
                    split_weights(it1, kind1, V)
                if v_turned_in(it, kind, s, project):
                    i = turn_index(s, -1, True)
                    v_lo_part(*v_turned_in(it, kind, s, project), 1 + TURNS * run(it, kind) + i, BANK_TURN + i % 2)
                for j in range(s % 4 + 1):
                    weights_lo(it, kind, s, j, project)
                    if j == 0 and ahead:
                        elementwise(nit, nkind, ns, 1)
                    if j == 1 and s == 7 and more_after(it, project):
                        split_weights(it2, kind2, Q)
                if ahead and nkind == DIL_KIND:
                    normalize(nit, ns, 0)
                if rot:
                    rotate(*rot)
                if ahead and nkind == DIL_KIND:
                    normalize(nit, ns, 1)
                if rot:
                    rotated_lo(*rot)
                if project and s == 0:
                    split_weights(it1, kind1, K)
                if project and kind1 == SB_KIND and ENDS.get(s, HALVES) < ROTATED:
                    projected_lo(it1, ENDS[s])
                if s == STEPS - 1:
                    values_out(it, kind, s)

            def one_run(it, kind, project=True, last=False):
                for s in range(STEPS):
                    step(it, kind, s, project, last)

            norm.lo_part(dve, 2, 0)
            for j in range(HALVES):
                if j < ROTATED:
                    projected_lo(0, j)
                if j == 0:
                    norm.lo_part(dve, 3, 0)
                if j == 2:
                    split_weights(0, 0, V)
                if j == 3:
                    split_weights(0, 1, Q)
                if j == 4:
                    v_lo_part(0, 0, 0, 0, BANK_TURN + 1)
            dve.wait_ge(tables_loaded, 16 * 4)
            dve.tensor_copy(neg_r[:, :], neg_f[:, :])
            dve.tensor_copy(ident_r[:, :], b.ident[:, :])
            for s in range(2):
                for a in range(2):
                    ones = dve.memset(stay[s][a][:, SEQ:SEQ + 1], 1.0)
            ones.then_inc(tables_ready, 1)
            elementwise(0, SB_KIND, 0, 0)
            elementwise(0, SB_KIND, 0, 1)
            with dve.Fori(0, PAIRS - 1) as it:
                one_run(it, SB_KIND)
                one_run(it, DIL_KIND)
            one_run(PAIRS - 1, SB_KIND)
            one_run(PAIRS - 1, DIL_KIND, project=False, last=True)

        @block.tensor
        def _(pe):
            def project(it, kind, u0, u1):
                for u in range(u0, u1):
                    j, k = u // KT, u % KT
                    piece, half = PRODUCTS[j]
                    n = 3 * kind + piece
                    hi, lo = w_hi[n % 2], w_lo[n % 2]
                    cols = slice(half * HALF, (half + 1) * HALF)
                    out = b.ps[:, BANK_PROJ, :]
                    if k == 0:
                        pe.wait_ge(w_split, 2 + 6 * it + n + 1)
                        pe.wait_ge(proj_free, 1 + HALVES * run(it, kind) + j)
                    pe.matmul(out, hi[:, k, :], b.xn_hi[:, k, cols], start=(k == 0), stop=False)
                    pe.matmul(out, hi[:, k, :], b.xn_lo[:, k, cols], start=False, stop=False)
                    last = pe.matmul(out, lo[:, k, :], b.xn_hi[:, k, cols], start=False, stop=(k == KT - 1))
                    if k == KT - 1:
                        last.then_inc(proj_ready, 1)

            def scores(it, kind, s):
                head, g = s // 4, s % 4
                rows = slice(head * HEAD, (head + 1) * HEAD)
                (q_hi, k_hi), (q_lo, k_lo) = qk_hi[kind], qk_lo[kind]
                if s in (0, 2):
                    if kind == SB_KIND:
                        pe.wait_ge(proj_free, 1 + HALVES * run(it, kind) + (2 if s == 0 else 4))
                    else:
                        pe.wait_ge(rot_split, 1 + ROTATED * it + (2 if s == 0 else 4))
                for a in range(2):
                    i = 2 * g + a
                    nk = P * (i + 1)
                    if s > 0 or kind == DIL_KIND:
                        before = (it, kind, s - 1) if s > 0 else (it, SB_KIND, STEPS - 1)
                        if before[1] == SB_KIND:
                            pe.wait_ge(gates_ready, 2 * STEPS * before[0] + 2 * before[2] + a + 1)
                        else:
                            pe.wait_ge(dil_max, 2 * STEPS * before[0] + 2 * before[2] + a + 1)
                    elif not (isinstance(it, int) and it == 0):
                        pe.wait_ge(dil_max, 2 * STEPS * it - 2 + a + 1)
                    qt = slice(i * P, (i + 1) * P)
                    for c0 in range(0, nk, HALF):
                        c1 = min(nk, c0 + HALF)
                        out = z[a][:, c0:c1]
                        pe.matmul(out, q_hi[rows, qt], k_hi[rows, c0:c1], start=True, stop=False)
                        if kind == SB_KIND and c1 == nk:
                            pe.matmul(z[a][:, nk - P:nk], ident_r[:, :], neg_r[:, :], start=False, stop=False)
                        pe.matmul(out, q_hi[rows, qt], k_lo[rows, c0:c1], start=False, stop=False)
                        last = pe.matmul(out, q_lo[rows, qt], k_hi[rows, c0:c1], start=False, stop=True)
                    last.then_inc(z_ready, 1)

            def turn_weights(it, kind, s, j, v_turn):
                g = s % 4
                n = turn_index(s, j, v_turn)
                if j == 0:
                    if kind == SB_KIND:
                        pe.wait_ge(sb_weights, 2 * STEPS * it + 2 * s + 2)
                    else:
                        pe.wait_ge(dil_weights, 2 * STEPS * it + 2 * s + 2)
                pe.wait_ge(turn_split, 1 + TURNS * run(it, kind) + n - 1)
                for kk in range(2):
                    for a in range(2):
                        key, i = 2 * j + kk, 2 * g + a
                        if key > i:
                            continue
                        col = SEQ - P * (i + 1) + key * P
                        c = (2 * kk + a) * P
                        last = pe.transpose(b.ps[:, BANK_TURN + n % 2, c:c + P],
                                            weight[s % 2][a][:, col:col + P], b.ident[:, :])
                last.then_inc(turned, 1)

            def turn_v(it, kind, half, bank, before):
                pe.wait_ge(proj_free, 1 + HALVES * run(it, kind) + ROTATED + half + 1)
                if before is not None:
                    pe.wait_ge(turn_split, before)
                for t in range(4):
                    last = pe.transpose(b.ps[:, bank, t * P:(t + 1) * P], v_turned[:, t * P:(t + 1) * P],
                                        b.ident[:, :])
                last.then_inc(turned, 1)

            def weighted_values(it, kind, s, j, v_turn):
                head, g = s // 4, s % 4
                pe.wait_ge(turn_split, 1 + TURNS * run(it, kind) + turn_index(s, j, v_turn) + 1)
                if j == 0:
                    pe.wait_ge(o_copied, 1 + STEPS * run(it, kind) + s)
                for k in (2 * j, 2 * j + 1):
                    end = k == 2 * g + 1
                    cols = slice(P, QG) if end else slice(0, QG)
                    out, v = b.ps[:, BANK_PV, cols], v_both[kind][:, k, head, :]
                    pe.matmul(out, v, wt_hi[:, k, cols], start=(k == 0), stop=False)
                    last = pe.matmul(out, v, wt_lo[:, k, cols], start=False, stop=end)
                if end:
                    last.then_inc(pv_ready, 1)

            def step(it, kind, s, proj=True, last=False):
                it1, kind1 = pair_of(it, kind, 1)
                nit, nkind, ns = (it, kind, s + 1) if s < STEPS - 1 else (it1, kind1, 0)
                if not (last and s == STEPS - 1):
                    scores(nit, nkind, ns)
                if s > 0:
                    weighted_values(it, kind, s - 1, (s - 1) % 4, proj)
                if v_turned_in(it, kind, s, proj):
                    i = turn_index(s, -1, True)
                    turn_v(*v_turned_in(it, kind, s, proj), BANK_TURN + i % 2, 1 + TURNS * run(it, kind) + i - 1)
                for j in range(s % 4 + 1):
                    if proj:
                        project(it1, kind1, *units_between(s, j))
                    turn_weights(it, kind, s, j, proj)
                    if j > 0:
                        weighted_values(it, kind, s, j - 1, proj)
                if proj:
                    project(it1, kind1, *units_between(s, s % 4 + 1))
                if s == STEPS - 1:
                    weighted_values(it, kind, s, s % 4, proj)

            def one_run(it, kind, proj=True, last=False):
                for s in range(STEPS):
                    step(it, kind, s, proj, last)

            pe.sem_inc(proj_free, 1)
            pe.sem_inc(proj_ready, 1)
            pe.sem_inc(pv_ready, 1)
            pe.sem_inc(o_copied, 1)
            pe.sem_inc(rot_split, 1)
            pe.sem_inc(z_ready, 1)
            norm.turn(pe, 2, 0)
            for j in range(HALVES):
                if j == 2:
                    pe.wait_ge(norm.lo, 16)
                project(0, 0, KT * j, KT * (j + 1))
                if j == 0:
                    norm.turn(pe, 3, 0, 12)
                if j == ROTATED:
                    turn_v(0, 0, 0, BANK_TURN + 1, None)
            pe.wait_ge(tables_ready, 1)
            scores(0, SB_KIND, 0)
            with pe.Fori(0, PAIRS - 1) as it:
                one_run(it, SB_KIND)
                one_run(it, DIL_KIND)
            one_run(PAIRS - 1, SB_KIND)
            one_run(PAIRS - 1, DIL_KIND, proj=False, last=True)


def stage_free(it, kind, s):
    v_turn = not (isinstance(it, int) and it == PAIRS - 1 and kind == DIL_KIND)
    if s < 2:
        n = turn_index(s + STEPS - 2, (s - 2) % 4, True) + 1 - TURNS
    else:
        n = turn_index(s - 2, (s - 2) % 4, v_turn) + 1
    return 1 + TURNS * (2 * it + kind) + n


def more_after(it, project):
    return project and not (isinstance(it, int) and it == PAIRS - 1)


def turn_parts(dst, s, j):
    if j < s % 4:
        return [(dst[:, 2 * j:2 * j + 2, :], slice(0, 2 * QG))]
    return [(dst[:, 2 * j, :], slice(0, QG)), (dst[:, 2 * j + 1, P:QG], slice(QG + P, 2 * QG))]



OQ = 256


def output_block(nc, b, sem, next_norm, w_split_buffers, o_split_buffers, o_dram, x_dram, w_out, group_gain,
                 next_weights):
    with ExitStack() as ctx:
        def sb(name, shape, dt=F32):
            return ctx.enter_context(nc.sbuf_tensor(f"out_{name}", shape, dt))

        (w_hi, w_lo), (o_hi, o_lo) = w_split_buffers, o_split_buffers
        o_raw = [b.scaled[:, 2 * i:2 * i + 2, :].rearrange("p a (f c) -> p (a f) c", c=OQ) for i in range(2)]
        o_sq = sb("o_sq", [P, KT, OQ])
        squares = [sb(f"squares{i}", [P, D])[:, :] for i in range(2)]
        ones = sb("ones", [P, 1])
        root, rstd = sb("root", [P, 2 * TT]), sb("rstd", [P, 2 * TT])
        o_loaded = [sem(f"out_o_loaded{i}") for i in range(2)]
        w_loaded = [sem(f"out_w_loaded{i}") for i in range(2)]
        x_loaded = [sem(f"out_x_loaded{t}") for t in range(TT)]
        o_hi_done, o_split, o_squared = sem("out_o_hi_done"), sem("out_o_split"), sem("out_o_squared")
        w_hi_done, w_split = sem("out_w_hi_done"), sem("out_w_split")
        ones_set, sums_ready, root_done, rstd_done = (sem(f"out_{n}") for n in ("ones", "sums", "root", "rstd"))
        y_ready, y_added = sem("out_y_ready"), sem("out_y_added")
        block = ctx.enter_context(nc.Block())
        BANK_SUM, BANK_NORM = 7, 3
        QUARTERS = SEQ // OQ
        PIECES = KT + CH

        @block.sync
        def _(sp):
            def load_o(q):
                if q >= 2:
                    sp.wait_ge(o_split, q - 1)
                    sp.wait_ge(o_squared, q - 1)
                sp.dma_start(o_raw[q % 2], o_dram.rearrange("(f p) c -> p f c", p=P)[:, :, q * OQ:(q + 1) * OQ]
                             ).then_inc(o_loaded[q % 2], 16)

            load_o(0)
            for f in range(PIECES):
                if f >= 2:
                    sp.wait_ge(w_split, f - 1)
                src = w_out[f * P:(f + 1) * P, :] if f < KT else next_weights[(f - KT) * P:(f - KT + 1) * P, :]
                sp.dma_start(b.w_raw[:, f % 2, :, :], src.rearrange("p (k c) -> p k c", k=KT)
                             ).then_inc(w_loaded[f % 2], 16)
                if f == 1:
                    load_o(1)
                if f == KT - 1:
                    for t in range(3):
                        sp.dma_start(b.x[:, t, :], x_dram[t * P:(t + 1) * P, :]).then_inc(x_loaded[t], 16)
            for q in range(2, QUARTERS):
                load_o(q)
            for t in range(3, TT):
                sp.dma_start(b.x[:, t, :], x_dram[t * P:(t + 1) * P, :]).then_inc(x_loaded[t], 16)

        def weight_piece(f):
            if f < KT:
                return w_hi[:, f, :], w_lo[:, f, :]
            return tuple(w[f - KT][:, :, :].rearrange("p k c -> p (k c)") for w in (b.w_hi, b.w_lo))

        def raw_piece(f):
            return b.w_raw[:, f % 2, :, :].rearrange("p k c -> p (k c)")

        @block.scalar
        def _(act):
            def split_weights(f):
                act.wait_ge(w_loaded[f % 2], 16 * (f // 2 + 1))
                act.activation(weight_piece(f)[0], raw_piece(f), ACT.Copy,
                               scale=group_gain[:, f:f + 1] if f < KT else 1.0).then_inc(w_hi_done, 1)

            def quarter(q):
                act.wait_ge(o_loaded[q % 2], 16 * (q // 2 + 1))
                act.activation(o_hi[:, :, q * OQ:(q + 1) * OQ], o_raw[q % 2], ACT.Copy).then_inc(o_hi_done, 1)
                if q > 0:
                    act.wait_ge(sums_ready, q)
                act.activation(o_sq[:, :, :], o_raw[q % 2], ACT.Square).then_inc(o_squared, 1)

            quarter(0)
            for f in range(KT):
                split_weights(f)
            for q in range(1, QUARTERS):
                quarter(q)
            act.wait_ge(sums_ready, QUARTERS)
            act.activation(root[:, :], b.ps[:, BANK_SUM, 0:2 * TT], ACT.Sqrt, scale=1.0 / GROUP,
                           bias=b.eps[:, 0:1]).then_inc(root_done, 1)
            for f in range(KT, PIECES):
                split_weights(f)
            for t in range(TT):
                act.wait_ge(y_added, 4 * t + 4)
                next_norm.row_root(act, b.x, t, squares)
                if t in NORM_ROUNDS:
                    next_norm.hi_part(act, NORM_ROUNDS[t], BANK_NORM)

        @block.vector
        def _(dve):
            def split_weights(f):
                hi, lo = weight_piece(f)
                dve.wait_ge(w_hi_done, f + 1)
                if f < KT:
                    dve.scalar_tensor_tensor(out=lo, in0=raw_piece(f), scalar=group_gain[:, f:f + 1],
                                             in1=hi.bitcast(F32), op0=ALU.mult, op1=ALU.subtract
                                             ).then_inc(w_split, 1)
                else:
                    dve.tensor_tensor(lo, raw_piece(f), hi.bitcast(F32), ALU.subtract).then_inc(w_split, 1)

            def quarter(q):
                tok = slice(q * OQ, (q + 1) * OQ)
                dve.wait_ge(o_hi_done, q + 1)
                dve.tensor_tensor(o_lo[:, :, tok], o_raw[q % 2], o_hi[:, :, tok].bitcast(F32), ALU.subtract
                                  ).then_inc(o_split, 1)

            dve.memset(ones[:, :], 1.0).then_inc(ones_set, 1)
            quarter(0)
            for f in range(KT):
                split_weights(f)
            for q in range(1, QUARTERS):
                quarter(q)
            dve.wait_ge(root_done, 1)
            dve.reciprocal(rstd[:, :], root[:, :]).then_inc(rstd_done, 1)
            dve.wait_ge(rstd_done, 1)
            for f in range(KT, PIECES):
                split_weights(f)
            for t in range(TT):
                dve.wait_ge(x_loaded[t], 16)
                for half in range(2):
                    cols = slice(half * HALF, (half + 1) * HALF)
                    for group in range(2):
                        m = 4 * t + 2 * half + group
                        dve.wait_ge(y_ready, m + 1)
                        if group == 1:
                            dve.wait_ge(y_added, m)
                        dve.scalar_tensor_tensor(out=b.x[:, t, cols], in0=b.ps[:, m % 3, :],
                                                 scalar=rstd[:, group * TT + t:group * TT + t + 1],
                                                 in1=b.x[:, t, cols], op0=ALU.mult, op1=ALU.add
                                                 ).then_inc(y_added, 1)
                norm_vector_step(dve, next_norm, b.x, t, BANK_NORM)

        @block.tensor
        def _(pe):
            def sums(q):
                pe.wait_ge(o_squared, q + 1)
                for group in range(2):
                    for tt in range(OQ // P):
                        c = group * TT + q * (OQ // P) + tt
                        for i in range(KT // 2):
                            last = pe.matmul(b.ps[:, BANK_SUM, c:c + 1],
                                             o_sq[:, group * (KT // 2) + i, tt * P:(tt + 1) * P], ones[:, :],
                                             start=(q == 0 and c == 0 and i == 0), stop=(i == KT // 2 - 1),
                                             skip_group_check=True)
                last.then_inc(sums_ready, 1)

            pe.wait_ge(ones_set, 1)
            sums(0)
            for t in range(TT):
                tok = slice(t * P, (t + 1) * P)
                pe.wait_ge(o_split, t // 2 + 1)
                for half in range(2):
                    cols = slice(half * HALF, (half + 1) * HALF)
                    for group in range(2):
                        m = 4 * t + 2 * half + group
                        out = b.ps[:, m % 3, :]
                        if m == 3:
                            for q in range(1, QUARTERS):
                                sums(q)
                        if m >= 3:
                            pe.wait_ge(y_added, m - 2)
                        for i in range(KT // 2):
                            f = group * (KT // 2) + i
                            if t == 0 and half == 0:
                                pe.wait_ge(w_split, f + 1)
                            pe.matmul(out, o_hi[:, f, tok], w_hi[:, f, cols], start=(i == 0), stop=False)
                            pe.matmul(out, o_hi[:, f, tok], w_lo[:, f, cols], start=False, stop=False)
                            last = pe.matmul(out, o_lo[:, f, tok], w_hi[:, f, cols], start=False,
                                             stop=(i == KT // 2 - 1))
                        last.then_inc(y_ready, 1)
                if t in TURN_ROUNDS:
                    next_norm.turn(pe, TURN_ROUNDS[t], BANK_NORM, 4 * TURN_ROUNDS[t])



class Buffers:
    pass


def constants():
    half = HEAD // 2
    inv_freq = np.float32(10000.0) ** (-np.arange(half, dtype=np.float32) / np.float32(half))
    ang = (np.arange(SEQ, dtype=np.float32)[None, :] * inv_freq[:, None]).astype(np.float32).astype(np.float64)
    cos, sin = np.cos(ang).astype(np.float32), np.sin(ang).astype(np.float32)
    cos_rows = np.concatenate([cos] * 4)
    sin_rows = np.concatenate([-sin, sin] * 2)
    ident = np.eye(P, dtype=np.float32)
    neg = np.where(np.arange(P)[None, :] < np.arange(P)[:, None], 0.0, NEG).astype(np.float32)
    dist = (SEQ - P) + np.arange(P)[:, None] - np.arange(SEQ)[None, :]
    count = np.zeros((P, SEQ))
    for window, dilation in ((128, 1), (512, 4), (2048, 16)):
        count += (dist >= 0) & (dist <= window) & (dist % dilation == 0)
    log_count = np.where(count > 0, np.log(np.maximum(count, 1.0)) / SCALE, NEG).astype(np.float32)
    return {"ident_c": ident, "neg_c": neg, "log_count_c": log_count, "cos_c": cos_rows, "sin_c": sin_rows}


def build(nc, a, out):
    x_dram = nc.dram_tensor("x_between", [SEQ, D], F32, kind="Internal").ap()
    o_dram = nc.dram_tensor("o_between", [D, SEQ], F32, kind="Internal").ap()
    with ExitStack() as ctx:
        def sem(name):
            return ctx.enter_context(nc.semaphore(name))

        def sb(name, shape, dt=F32):
            return ctx.enter_context(nc.sbuf_tensor(name, shape, dt))

        b = Buffers()
        b.ps = ctx.enter_context(nc.psum_tensor("banks", [P, 8, HALF], F32))
        b.ident = sb("ident_sb", [P, P])
        gains = sb("gains_sb", [P, 4, KT])
        b.eps, b.sumsq, b.root, b.rstd = sb("eps", [P, 1]), sb("sumsq", [P, TT]), sb("root", [P, TT]), sb("rstd", [P, TT])
        b.scaled = sb("scaled_rows", [P, 4, D])
        b.w_raw = sb("w_raw", [P, CH, KT, P])
        b.w_hi = [sb(f"w_hi{t}", [P, KT, P], F32R) for t in range(CH)]
        b.w_lo = [sb(f"w_lo{t}", [P, KT, P], F32R) for t in range(CH)]
        first_pair = [sb(f"first_{n}", [P, KT, SEQ], F32R) for n in ("hi", "lo")]
        loaded, eps_set = sem("constants_loaded"), sem("eps_set")
        with nc.Block() as block:
            @block.sync
            def _(sp):
                sp.dma_start(b.ident[:, :], a["ident_c"]).then_inc(loaded, 16)
                for i, name in enumerate(("ffn1_norm", "mix_norm", "group_norm", "ffn2_norm")):
                    sp.dma_start(gains[:, i, :], a[name]).then_inc(loaded, 16)
                sp.wait_ge(loaded, 16 * 5)

            @block.vector
            def _(dve):
                dve.memset(b.eps[:, :], EPS).then_inc(eps_set, 1)

        ffn1_norm = Norm(sem, "ffn1_norm", b, gains[:, 0, :], *first_pair)
        mix_norm = Norm(sem, "mix_norm", b, gains[:, 1, :], *first_pair)
        with (nc.sbuf_tensor("x_first", [P, TT, D], F32) as x_first,
              nc.sbuf_tensor("ffn1_hi", [P, KT, SEQ], F32R) as arena_hi,
              nc.sbuf_tensor("ffn1_lo", [P, KT, SEQ], F32R) as arena_lo):
            b.x = x_first
            ffn_block(nc, b, sem, "ffn1", (a["ffn1_w_gate"], a["ffn1_w_up"], a["ffn1_w_down"]), ffn1_norm, mix_norm,
                      (arena_hi, arena_lo), x_dram, x_from=a["x"], next_weights=a["w_in"])
        b.xn_hi, b.xn_lo = first_pair
        heads_block(nc, b, sem, mix_norm, a["w_in"], a["neg_c"], a["log_count_c"], a["cos_c"], a["sin_c"], o_dram)
        with (nc.sbuf_tensor("x_second", [P, TT, D], F32) as x_second,
              nc.sbuf_tensor("second_hi", [P, KT, SEQ], F32R) as second_hi,
              nc.sbuf_tensor("second_lo", [P, KT, SEQ], F32R) as second_lo):
            b.x = x_second
            ffn2_norm = Norm(sem, "ffn2_norm", b, gains[:, 3, :], second_hi, second_lo)
            final_norm = Norm(sem, "final_norm", b, None, None, None)
            output_block(nc, b, sem, ffn2_norm, first_pair, (second_hi, second_lo), o_dram, x_dram, a["w_out"],
                         gains[:, 2, :], a["ffn2_w_gate"])
            with nc.sbuf_tensor("final_gain_sb", [P, D], F32) as b.final_gain:
                ffn_block(nc, b, sem, "ffn2", (a["ffn2_w_gate"], a["ffn2_w_up"], a["ffn2_w_down"]), ffn2_norm,
                          final_norm, first_pair, out, final_gain=a["final_norm"])


def kernel(**inputs):
    import concourse.bacc as bacc
    from concourse.bass_utils import run_bass_kernel_spmd as run

    nc = bacc.Bacc("TRN2", target_bir_lowering=False, num_devices=1, dynamic_dma_scratch_size=1024)

    def feature_tiles(v):
        return np.ascontiguousarray(v.reshape(-1, P).T)

    def column_blocks(w, width):
        return w.reshape(KT, P, -1, width).transpose(2, 1, 0, 3).reshape(-1, KT * width)

    i = {k: np.asarray(v) for k, v in inputs.items()}
    arrays = {
        "x": i["x"].reshape(SEQ, D),
        "ffn1_norm": feature_tiles(i["ffn1_norm"]),
        "mix_norm": feature_tiles(i["mix_norm"]),
        "group_norm": feature_tiles(np.concatenate([i["sb_out_norm"][0], i["dil_out_norm"][0]])),
        "ffn2_norm": feature_tiles(i["ffn2_norm"]),
        "final_norm": i["final_norm"].reshape(1, D),
        **constants(),
    }
    for name in ("ffn1_w_down", "w_out", "ffn2_w_down"):
        arrays[name] = i[name][0]
    for name in ("ffn1_w_gate", "ffn1_w_up", "ffn2_w_gate", "ffn2_w_up"):
        arrays[name] = column_blocks(i[name][0], P)
    blocks = column_blocks(i["w_in"][0], P).reshape(2, 3, PAIRS, P, D)
    arrays["w_in"] = blocks.transpose(2, 0, 1, 3, 4).reshape(-1, D)
    arrays = {f"in_{k}": np.ascontiguousarray(v) for k, v in arrays.items()}
    a = {k[3:]: nc.dram_tensor(k, v.shape, F32, kind="ExternalInput").ap() for k, v in arrays.items()}
    out = nc.dram_tensor("out_dram", [SEQ, D], F32, kind="ExternalOutput").ap()
    build(nc, a, out)
    r = run(nc, [arrays], core_ids=[0])
    return r.results[0]["out_dram"].reshape(1, SEQ, D)
```

```python
from contextlib import ExitStack

import numpy as np

import concourse.bass as bass
from concourse import mybir

F32 = mybir.dt.float32
F32R = mybir.dt.float32r
ALU = mybir.AluOpType
ACT = mybir.ActivationFunctionType

P = 128
SEQ = 1024
D = 1024
DFF = 2816
HEAD = 64
HALF = 512
TT = SEQ // P
KT = D // P
CH = 2
NCH = DFF // (CH * P)
PAIRS = 4
GROUP = D // 2
EPS = 1e-6
SCALE = HEAD ** -0.5
NEG = -1e30



class Norm:

    def __init__(self, sem, tag, b, gain, xn_hi, xn_lo):
        self.b, self.gain, self.xn_hi, self.xn_lo = b, gain, xn_hi, xn_lo
        self.square = sem(f"{tag}_sum_of_squares")
        self.root = sem(f"{tag}_root")
        self.rstd = sem(f"{tag}_rstd")
        self.scaled = sem(f"{tag}_scaled")
        self.turned = sem(f"{tag}_turned")
        self.hi = sem(f"{tag}_hi_split")
        self.lo = sem(f"{tag}_lo_split")

    def row_root(self, act, x, t, squares):
        b = self.b
        if t >= 2:
            act.wait_ge(self.square, t - 1)
        act.activation(squares[t % 2], x[:, t, :], ACT.Square, accum_out=b.sumsq[:, t:t + 1]
                       ).then_inc(self.square, 1)
        act.wait_ge(self.square, t + 1)
        act.activation(b.root[:, t:t + 1], b.sumsq[:, t:t + 1], ACT.Sqrt, scale=1.0 / D,
                       bias=b.eps[:, 0:1]).then_inc(self.root, 1)

    def row_reciprocal(self, dve, t):
        b = self.b
        dve.wait_ge(self.root, t + 1)
        dve.reciprocal(b.rstd[:, t:t + 1], b.root[:, t:t + 1]).then_inc(self.rstd, 1)
        dve.wait_ge(self.rstd, t + 1)

    def row_scale(self, dve, x, t):
        self.row_reciprocal(dve, t)
        if t >= 4:
            dve.wait_ge(self.turned, 8)
        dve.tensor_scalar(self.b.scaled[:, t % 4, :], x[:, t, :], self.b.rstd[:, t:t + 1], None, ALU.mult
                          ).then_inc(self.scaled, 1)

    def turn(self, pe, r, bank, read=0):
        b, half, f = self.b, r // 2, 4 * (r % 2)
        if read:
            pe.wait_ge(self.lo, read)
        for i in range(4):
            pe.wait_ge(self.scaled, 4 * half + i + 1)
            for j in range(4):
                last = pe.transpose(b.ps[:, bank + j, i * P:(i + 1) * P],
                                    b.scaled[:, i, (f + j) * P:(f + j + 1) * P], b.ident[:, :])
                if i == 3:
                    last.then_inc(self.turned, 1)

    def hi_part(self, act, r, bank):
        half, f = r // 2, 4 * (r % 2)
        for j in range(4):
            act.wait_ge(self.turned, 4 * r + j + 1)
            act.activation(self.xn_hi[:, f + j, half * HALF:(half + 1) * HALF], self.b.ps[:, bank + j, :], ACT.Copy,
                           scale=self.gain[:, f + j:f + j + 1]).then_inc(self.hi, 1)

    def lo_part(self, dve, r, bank):
        half, f = r // 2, 4 * (r % 2)
        for j in range(4):
            cols = slice(half * HALF, (half + 1) * HALF)
            dve.wait_ge(self.hi, 4 * r + j + 1)
            dve.scalar_tensor_tensor(out=self.xn_lo[:, f + j, cols], in0=self.b.ps[:, bank + j, :],
                                     scalar=self.gain[:, f + j:f + j + 1],
                                     in1=self.xn_hi[:, f + j, cols].bitcast(F32),
                                     op0=ALU.mult, op1=ALU.subtract).then_inc(self.lo, 1)


def address(eng, value):
    return value if isinstance(value, int) else eng.snap(value)



def ffn_block(nc, b, sem, tag, weights, norm, next_norm, arena, store, x_from=None, next_weights=None,
              final_gain=None):
    with ExitStack() as ctx:
        def sb(name, shape, dt=F32):
            return ctx.enter_context(nc.sbuf_tensor(f"{tag}_{name}", shape, dt))

        w_gate, w_up, w_down = weights
        up_raw = sb("up_raw", [P, CH, KT, P])
        down_raw = sb("down_raw", [P, CH, D])
        h_hi = [arena[0][:, CH * k:CH * (k + 1), :] for k in range(2)]
        h_lo = [arena[0][:, CH * (k + 2):CH * (k + 3), :] for k in range(2)]
        down_hi, down_lo = arena[1][:, 0:CH, :], arena[1][:, CH:2 * CH, :]
        up_hi, up_lo = ([arena[1][:, 2 * CH + CH * part + t, :].rearrange("p (k c) -> p k c", k=KT)
                         for t in range(CH)] for part in range(2))
        last_down_hi, last_down_lo = arena[1][:, 2 * CH:3 * CH, :], arena[1][:, 3 * CH:4 * CH, :]
        gate_raw, gate_hi, gate_lo = b.w_raw, b.w_hi, b.w_lo
        gate_act = [b.scaled[:, 0, h * HALF:(h + 1) * HALF] for h in range(2)]
        h_full = [b.scaled[:, 1, h * HALF:(h + 1) * HALF] for h in range(2)]
        squares = [h_hi[1][:, i, :] for i in range(2)]
        x_loaded = [sem(f"{tag}_x_loaded{t}") for t in range(TT)]
        gain_loaded = sem(f"{tag}_final_gain_loaded")
        gate_loaded = [sem(f"{tag}_gate_loaded{t}") for t in range(CH)]
        up_loaded = [sem(f"{tag}_up_loaded{t}") for t in range(CH)]
        down_loaded = sem(f"{tag}_down_loaded")
        gate_hi_done = sem(f"{tag}_gate_hi_done")
        up_hi_done = sem(f"{tag}_up_hi_done")
        down_hi_done = sem(f"{tag}_down_hi_done")
        gate_split = sem(f"{tag}_gate_split")
        up_split = sem(f"{tag}_up_split")
        down_split = sem(f"{tag}_down_split")
        gate_ready = sem(f"{tag}_gate_ready")
        up_ready = sem(f"{tag}_up_ready")
        silu_done = sem(f"{tag}_silu_done")
        h_done = sem(f"{tag}_h_done")
        h_hi_done = sem(f"{tag}_h_hi_done")
        h_split = sem(f"{tag}_h_split")
        y_ready = sem(f"{tag}_y_ready")
        y_added = sem(f"{tag}_y_added")
        stored = sem(f"{tag}_stored")
        normed = sem(f"{tag}_normed")
        block = ctx.enter_context(nc.Block())

        BANK_Y = 4
        PAIRS_OF_CHUNKS = (NCH - 3) // 2

        @block.sync
        def _(sp):
            def load_columns(raw, w, first, t, loaded):
                sp.dma_start(raw[:, t, :, :], w[bass.ds(first, P), :].rearrange("p (k f) -> p k f", k=KT)
                             ).then_inc(loaded[t], 16)

            def load_down(first):
                sp.dma_start(down_raw[:, :, :], w_down[bass.ds(first, CH * P), :].rearrange(
                    "(t p) d -> p t d", p=P)).then_inc(down_loaded, 16)

            def chunk(c, first=False, last=False):
                here = address(sp, c * CH * P)
                ahead = [address(sp, (c + 1) * CH * P + t * P) for t in range(CH)]
                if not first:
                    sp.wait_ge(down_split, CH * c)
                load_down(here)
                if last and final_gain is not None:
                    return
                for t in range(CH):
                    sp.wait_ge(gate_split, CH * c + t + 1)
                    if last:
                        load_columns(gate_raw, next_weights, t * P, t, gate_loaded)
                        continue
                    load_columns(gate_raw, w_gate, ahead[t], t, gate_loaded)
                    sp.wait_ge(up_split, CH * c + t + 1)
                    load_columns(up_raw, w_up, ahead[t], t, up_loaded)

            def load_x(tiles):
                for t in tiles:
                    sp.dma_start(b.x[:, t, :], x_from[t * P:(t + 1) * P, :]).then_inc(x_loaded[t], 16)

            if x_from is None:
                sp.sem_inc(gate_loaded[0], 16)
                sp.sem_inc(gate_loaded[1], 16)
                sp.sem_inc(gate_hi_done, CH)
                sp.sem_inc(gate_split, CH)
            else:
                load_x(range(1))
                for dst, src in b.constants:
                    sp.dma_start(dst, src).then_inc(b.constants_loaded, 16)
                load_x(range(1, 4))
                load_columns(gate_raw, w_gate, 0, 0, gate_loaded)
            load_columns(up_raw, w_up, 0, 0, up_loaded)
            if x_from is not None:
                load_x(range(4, TT))
                load_columns(gate_raw, w_gate, P, 1, gate_loaded)
            load_columns(up_raw, w_up, P, 1, up_loaded)
            chunk(0, first=True)
            if final_gain is not None:
                sp.dma_start(b.final_gain[:, :], final_gain.to_broadcast([P, D])).then_inc(gain_loaded, 16)
            with sp.Fori(0, PAIRS_OF_CHUNKS) as i:
                chunk(2 * i + 1)
                chunk(2 * i + 2)
            chunk(NCH - 2)
            chunk(NCH - 1, last=True)
            for t in range(TT):
                if final_gain is not None:
                    sp.wait_ge(normed, t + 1)
                else:
                    sp.wait_ge(y_added, 4 + 16 * (NCH - 1) + 2 * t + 2)
                sp.dma_start(store[t * P:(t + 1) * P, :], b.x[:, t, :]).then_inc(stored, 16)
            if final_gain is not None:
                sp.wait_ge(stored, 16 * TT)
            else:
                b.x_stored = stored

        @block.scalar
        def _(act):
            def split_gate(c, t):
                act.wait_ge(gate_loaded[t], 16 * (c + 1))
                act.activation(gate_hi[t][:, :, :], gate_raw[:, t, :, :], ACT.Copy).then_inc(gate_hi_done, 1)

            def split_up(c, t):
                act.wait_ge(up_loaded[t], 16 * (c + 1))
                act.activation(up_hi[t], up_raw[:, t, :, :], ACT.Copy).then_inc(up_hi_done, 1)

            def split_down(c, last=False):
                if not last:
                    act.wait_ge(y_ready, 16 * c + 1)
                act.wait_ge(down_loaded, 16 * (c + 1))
                for t in range(CH):
                    act.activation((last_down_hi if last else down_hi)[:, t, :], down_raw[:, t, :], ACT.Copy).then_inc(down_hi_done, 1)

            def chunk(c, k, first=False, last=False):
                if not first:
                    split_down(c - 1)
                for t in range(CH):
                    for half in range(2):
                        n = 2 * CH * c + 2 * t + half
                        cols = slice(half * HALF, (half + 1) * HALF)
                        act.wait_ge(gate_ready, n + 1)
                        if not (first and t == 0):
                            act.wait_ge(h_done, n - 1)
                        act.activation(gate_act[half], b.ps[:, half, :], ACT.Silu).then_inc(silu_done, 1)
                        act.wait_ge(h_done, n + 1)
                        act.activation(h_hi[k][:, t, cols], h_full[half], ACT.Copy).then_inc(h_hi_done, 1)
                    if not last:
                        split_gate(c + 1, t)
                        split_up(c + 1, t)

            if x_from is not None:
                act.wait_ge(b.eps_set, 1)
                for t in range(4):
                    act.wait_ge(x_loaded[t], 16)
                    norm.row_root(act, b.x, t, squares)
                act.wait_ge(b.constants_loaded, 16 * len(b.constants))
                norm.hi_part(act, 0, 0)
                split_gate(0, 0)
                norm.hi_part(act, 1, BANK_Y)
                split_up(0, 0)
                for t in range(4, TT):
                    act.wait_ge(x_loaded[t], 16)
                    norm.row_root(act, b.x, t, squares)
                norm.hi_part(act, 2, BANK_Y)
            else:
                norm.hi_part(act, 2, BANK_Y)
                split_up(0, 0)
            norm.hi_part(act, 3, BANK_Y)
            if x_from is not None:
                split_gate(0, 1)
            split_up(0, 1)
            chunk(0, 0, first=True)
            with act.Fori(0, PAIRS_OF_CHUNKS) as i:
                chunk(2 * i + 1, 1)
                chunk(2 * i + 2, 0)
            chunk(NCH - 2, (NCH - 2) % 2)
            chunk(NCH - 1, (NCH - 1) % 2, last=True)
            split_down(NCH - 1, last=True)
            if final_gain is None:
                for t in range(CH):
                    split_gate(NCH, t)
            for t in range(TT):
                act.wait_ge(y_added, 4 + 16 * (NCH - 1) + 2 * t + 2)
                next_norm.row_root(act, b.x, t, squares)
                if final_gain is None and t in NORM_ROUNDS:
                    next_norm.hi_part(act, NORM_ROUNDS[t], 0)

        @block.vector
        def _(dve):
            def split_gate(c, t):
                dve.wait_ge(gate_hi_done, CH * c + t + 1)
                dve.tensor_tensor(gate_lo[t][:, :, :], gate_raw[:, t, :, :], gate_hi[t][:, :, :].bitcast(F32),
                                  ALU.subtract).then_inc(gate_split, 1)

            def split_up(c, t):
                dve.wait_ge(up_hi_done, CH * c + t + 1)
                dve.tensor_tensor(up_lo[t], up_raw[:, t, :, :], up_hi[t].bitcast(F32), ALU.subtract
                                  ).then_inc(up_split, 1)

            def split_down(c, hi=down_hi, lo=down_lo):
                for t in range(CH):
                    dve.wait_ge(down_hi_done, CH * c + t + 1)
                    dve.tensor_tensor(lo[:, t, :], down_raw[:, t, :], hi[:, t, :].bitcast(F32), ALU.subtract
                                      ).then_inc(down_split, 1)

            def add_down(c, t):
                for half in range(2):
                    g = 2 * t + half
                    dve.wait_ge(y_ready, 1 + 16 * c + g + 1)
                    cols = slice(half * HALF, (half + 1) * HALF)
                    dve.scalar_tensor_tensor(out=b.x[:, t, cols], in0=b.ps[:, BANK_Y + g % 4, :], scalar=0.5,
                                             in1=b.x[:, t, cols], op0=ALU.mult, op1=ALU.add
                                             ).then_inc(y_added, 1)

            def chunk(c, k, first=False, last=False):
                if not first:
                    split_down(c - 1)
                for t in range(CH):
                    for half in range(2):
                        n = 2 * CH * c + 2 * t + half
                        cols = slice(half * HALF, (half + 1) * HALF)
                        dve.wait_ge(silu_done, n + 1)
                        dve.wait_ge(up_ready, n + 1)
                        if not (first and t == 0):
                            dve.wait_ge(h_split, n - 1)
                        dve.tensor_tensor(h_full[half], b.ps[:, 2 + half, :], gate_act[half], ALU.mult
                                          ).then_inc(h_done, 1)
                        dve.wait_ge(h_hi_done, n + 1)
                        dve.tensor_tensor(h_lo[k][:, t, cols], h_full[half], h_hi[k][:, t, cols].bitcast(F32),
                                          ALU.subtract).then_inc(h_split, 1)
                    if not last:
                        split_gate(c + 1, t)
                        if t == CH - 1 and not first:
                            add_down(c - 1, 0)
                        split_up(c + 1, t)
                if last:
                    split_down(c, last_down_hi, last_down_lo)
                if not first:
                    for t in range(0 if last else 1, TT):
                        add_down(c - 1, t)

            def normed_result(t):
                next_norm.row_reciprocal(dve, t)
                dve.scalar_tensor_tensor(out=b.x[:, t, :], in0=b.x[:, t, :], scalar=b.rstd[:, t:t + 1],
                                         in1=b.final_gain[:, :], op0=ALU.mult, op1=ALU.mult).then_inc(normed, 1)

            if x_from is not None:
                dve.memset(b.eps[:, :], EPS).then_inc(b.eps_set, 1)
                for t in range(4):
                    norm.row_scale(dve, b.x, t)
                dve.wait_ge(b.constants_loaded, 16 * len(b.constants))
                norm.lo_part(dve, 0, 0)
                split_gate(0, 0)
                norm.lo_part(dve, 1, BANK_Y)
                split_up(0, 0)
                for t in range(4, TT):
                    norm.row_scale(dve, b.x, t)
                norm.lo_part(dve, 2, BANK_Y)
            else:
                norm.lo_part(dve, 2, BANK_Y)
                split_up(0, 0)
            norm.lo_part(dve, 3, BANK_Y)
            if x_from is not None:
                split_gate(0, 1)
            split_up(0, 1)
            chunk(0, 0, first=True)
            with dve.Fori(0, PAIRS_OF_CHUNKS) as i:
                chunk(2 * i + 1, 1)
                chunk(2 * i + 2, 0)
            chunk(NCH - 2, (NCH - 2) % 2)
            chunk(NCH - 1, (NCH - 1) % 2, last=True)
            if final_gain is None:
                for t in range(CH):
                    split_gate(NCH, t)
            else:
                dve.wait_ge(gain_loaded, 16)
            for t in range(TT):
                if final_gain is None:
                    rows_before(next_norm, dve, b.x, t)
                add_down(NCH - 1, t)
                if final_gain is not None and t > 0:
                    normed_result(t - 1)
                if final_gain is None and t in NORM_ROUNDS:
                    next_norm.lo_part(dve, NORM_ROUNDS[t], 0)
            if final_gain is None:
                rows_before(next_norm, dve, b.x, TT)
            else:
                normed_result(TT - 1)

        @block.tensor
        def _(pe):
            def product(bank, hi, lo, half, first=False):
                cols = slice(half * HALF, (half + 1) * HALF)
                for k in range(KT):
                    if first:
                        pe.wait_ge(norm.lo, KT * half + k + 1)
                    pe.matmul(b.ps[:, bank, :], hi[:, k, :], norm.xn_hi[:, k, cols], start=(k == 0), stop=False)
                    pe.matmul(b.ps[:, bank, :], hi[:, k, :], norm.xn_lo[:, k, cols], start=False, stop=False)
                    last = pe.matmul(b.ps[:, bank, :], lo[:, k, :], norm.xn_hi[:, k, cols], start=False,
                                     stop=(k == KT - 1))
                return last

            def up_products(c, t, first=False):
                for half in range(2):
                    n = 2 * CH * c + 2 * t + half
                    if not first:
                        pe.wait_ge(silu_done, n - 1)
                    elif half == 0 and x_from is None:
                        norm.turn(pe, 2, BANK_Y)
                    if half == 0:
                        pe.wait_ge(gate_split, CH * c + t + 1)
                    product(half, gate_hi[t], gate_lo[t], half, first).then_inc(gate_ready, 1)
                    if not first:
                        pe.wait_ge(h_done, n - 1)
                    elif half == 0 and x_from is None:
                        norm.turn(pe, 3, BANK_Y, 12)
                    elif half == 0:
                        norm.turn(pe, 2, BANK_Y)
                    if half == 0:
                        pe.wait_ge(up_split, CH * c + t + 1)
                    product(2 + half, up_hi[t], up_lo[t], half).then_inc(up_ready, 1)
                    if first and half == 0 and x_from is not None:
                        norm.turn(pe, 3, BANK_Y, 12)

            def down_products(c, k, t, w_hi=down_hi, w_lo=down_lo):
                for half in range(2):
                    g = 2 * t + half
                    pe.wait_ge(y_added, 16 * c + g + 1)
                    tok, cols = slice(t * P, (t + 1) * P), slice(half * HALF, (half + 1) * HALF)
                    for f in range(CH):
                        out = b.ps[:, BANK_Y + g % 4, :]
                        pe.matmul(out, h_hi[k][:, f, tok], w_hi[:, f, cols], start=(f == 0), stop=False)
                        pe.matmul(out, h_hi[k][:, f, tok], w_lo[:, f, cols], start=False, stop=False)
                        last = pe.matmul(out, h_lo[k][:, f, tok], w_hi[:, f, cols], start=False,
                                         stop=(f == CH - 1))
                    last.then_inc(y_ready, 1)

            def chunk(c, k, first=False):
                for t in range(CH):
                    up_products(c, t, first and t == 0)
                if not first:
                    pe.wait_ge(h_split, 2 * CH * c)
                    pe.wait_ge(down_split, CH * c)
                    for t in range(TT):
                        down_products(c - 1, 1 - k, t)

            pe.sem_inc(y_added, 4)
            pe.sem_inc(y_ready, 1)
            if x_from is not None:
                pe.wait_ge(b.constants_loaded, 16 * len(b.constants))
                norm.turn(pe, 0, 0)
                norm.turn(pe, 1, BANK_Y)
            chunk(0, 0, first=True)
            with pe.Fori(0, PAIRS_OF_CHUNKS) as i:
                chunk(2 * i + 1, 1)
                chunk(2 * i + 2, 0)
            chunk(NCH - 2, (NCH - 2) % 2)
            chunk(NCH - 1, (NCH - 1) % 2)
            pe.wait_ge(h_split, 2 * CH * NCH)
            pe.wait_ge(down_split, CH * NCH)
            for t in range(TT):
                down_products(NCH - 1, (NCH - 1) % 2, t, last_down_hi, last_down_lo)
                if final_gain is None and t in NORM_ROUNDS:
                    next_norm.turn(pe, NORM_ROUNDS[t], 0, 4 * NORM_ROUNDS[t])


NORM_ROUNDS = {4: 0, 5: 1}


def rows_before(norm, dve, x, t):
    for row in {1: (0,), 2: (1,), 3: (2,), 4: (3,), 6: (4, 5), 8: (6, 7)}.get(t, ()):
        norm.row_scale(dve, x, row)



STEPS = 8
QG = 256
SB_KIND, DIL_KIND = 0, 1
HALVES = 6
Q, K, V = 0, 1, 2
PRODUCTS = ((Q, 0), (K, 0), (Q, 1), (K, 1), (V, 0), (V, 1))
ROTATED = 4
ROTATE_BEHIND = 1
UNITS = ((1, 3), (0, 2, 2), (1, 0, 4, 3), (0, 3, 3, 0, 2), (2, 6), (0, 2, 2), (0, 3, 1, 1), (0, 2, 2, 2, 1))
ENDS = {next(s for s in range(STEPS) if sum(map(sum, UNITS[:s + 1])) >= KT * (j + 1)): j for j in range(HALVES)}
TURNS = 22


def turn_index(s, j, v_turn):
    return 1 + sum(u % 4 + 1 for u in range(s)) + j + (v_turn and s == STEPS - 1)


def bank_count(s):
    return sum(u % 4 + 1 for u in range(s))


BANKS = bank_count(STEPS)


def wt_part(s, j):
    return 2 * ((bank_count(s) + j) % 4)


def banks_back(it, kind, s, j, n):
    while j < n:
        n -= j + 1
        s -= 1
        if s < 0:
            if isinstance(it, int) and it == 0 and kind == 0:
                return None
            it, kind, s = (it, 0, STEPS - 1) if kind == 1 else (it - 1, 1, STEPS - 1)
        j = s % 4
    return it, kind, s, j - n


def values_done(it, kind, s, j):
    bank = banks_back(it, kind, s, j, 2)
    return bank[:3] if bank and bank[3] == bank[2] % 4 else None


def v_turned_in(it, kind, s, project):
    if s == 0:
        return it, kind, 1
    if s == STEPS - 1 and project:
        return it + (kind + 1) // 2, (kind + 1) % 2, 0
    return None


def units_between(s, j):
    start = sum(map(sum, UNITS[:s])) + sum(UNITS[s][:j])
    return start, start + UNITS[s][j]


def heads_block(nc, b, sem, norm, w_in, neg_mask, log_count, cos, sin, o_dram, w_out, group_gain):
    with ExitStack() as ctx:
        def sb(name, shape, dt=F32):
            return ctx.enter_context(nc.sbuf_tensor(f"heads_{name}", shape, dt))

        cos_sb, sin_sb = sb("cos", [P, SEQ]), sb("sin", [P, SEQ])
        log_count_sb = sb("log_count", [P, SEQ])
        neg_f = sb("neg_f", [P, P])
        wt_hi = sb("wt_hi", [P, TT, QG], F32R)
        wt_lo = sb("wt_lo", [P, TT, QG], F32R)
        o_stage = sb("o_stage", [P, SEQ])
        w_raw, w_hi, w_lo = [b.w_raw[:, i, :, :] for i in range(2)], b.w_hi, b.w_lo
        qk_hi = [[sb(f"{n}_hi{kind}", [P, SEQ], F32R) for n in "qk"] for kind in range(2)]
        qk_lo = [[sb(f"{n}_lo{kind}", [P, SEQ], F32R) for n in "qk"] for kind in range(2)]
        v_both = [sb(f"v_both{kind}", [P, TT, 2, P], F32R) for kind in range(2)]
        o_low = sb("o_low", [HEAD, QG])
        v_turned = sb("v_feature_major", [P, HALF])
        weight = [[b.scaled[:, 2 * s + a, :] for a in range(2)] for s in range(2)]
        stay = [[sb(f"stay{s}{a}", [P, SEQ + 1]) for a in range(2)] for s in range(2)]
        rot_in, rot_swap, rot_out = sb("rot_in", [P, HALF]), sb("rot_swap", [P, HALF]), sb("rot_out", [P, HALF])
        neg_r, ident_r = sb("neg_r", [P, P], F32R), sb("ident_r", [P, P], F32R)
        row_max, neg_max, row_sum, row_inv = (sb(n, [P, 4]) for n in ("row_max", "neg_max", "row_sum", "row_inv"))

        tables_loaded = sem("tables_loaded")
        tables_ready = sem("tables_ready")
        w_loaded = [sem(f"w_loaded{i}") for i in range(2)]
        w_hi_done, w_split = sem("w_hi_done"), sem("w_split")
        proj_ready, proj_free = sem("proj_ready"), sem("proj_free")
        sb_hi_done = sem("sb_qk_hi_done")
        rot_swapped, rot_cos, rot_sin, rot_sum = (sem(f"rot_{n}") for n in ("swapped", "cos", "sin", "sum"))
        rot_hi_done, rot_split = sem("rot_hi_done"), sem("rot_split")
        z_ready = sem("z_ready")
        gates_ready, products_ready, sb_weights = sem("gates_ready"), sem("products_ready"), sem("sb_weights")
        dil_max, dil_negmax, dil_exp, dil_inv, dil_weights = (
            sem(f"dil_{n}") for n in ("max", "negmax", "exp", "inv", "weights"))
        scores_seen = sem("dil_scores_seen")
        turned, turn_hi_done, turn_split = sem("turned"), sem("turn_hi_done"), sem("turn_split")
        out_w_loaded = [sem(f"out_w_loaded{i}") for i in range(2)]
        out_w_hi_done, out_w_gained, out_w_split = (sem(f"out_w_{n}") for n in ("hi_done", "gained", "split"))
        pv_ready, o_low_done, o_copied = sem("pv_ready"), sem("o_low_done"), sem("o_copied")
        o_stored = [sem(f"o_stored{h}") for h in range(2)]
        block = ctx.enter_context(nc.Block())

        BANK_PV, BANK_TURN, BANK_PROJ = 4, 5, 7
        z = [b.ps[:, 2 * a:2 * a + 2, :].rearrange("p a c -> p (a c)") for a in range(2)]

        def first_bank(j):
            return (BANK_PV, BANK_PROJ)[j % 2]

        def pair_of(it, kind, ahead):
            k = kind + ahead
            return it + k // 2, k % 2

        def run(it, kind):
            return 2 * it + kind

        @block.sync
        def _(sp):
            def load_weights(it, kind, piece):
                n = 3 * kind + piece
                slot = n % 2
                first = address(sp, (6 * it + n) * P)
                sp.wait_ge(w_split, 2 + 6 * it + n - 1)
                sp.dma_start(w_raw[slot][:, :, :], w_in[bass.ds(first, P), :].rearrange(
                    "p (k c) -> p k c", k=KT)).then_inc(w_loaded[slot], 16)

            def load_out_weights(f):
                sp.dma_start(b.w_raw[:, f % 2, :, :], w_out[f * P:(f + 1) * P, :].rearrange(
                    "p (k c) -> p k c", k=KT)).then_inc(out_w_loaded[f % 2], 16)

            def swap_halves(it, kind, j):
                sp.wait_ge(proj_free, 1 + HALVES * run(it, kind) + j + 1)
                for head in range(2):
                    for part in range(2):
                        src = head * HEAD + part * 32
                        dst = head * HEAD + (1 - part) * 32
                        sp.dma_start(rot_swap[dst:dst + 32, :], rot_in[src:src + 32, :]
                                     ).then_inc(rot_swapped, 16)

            def store_head(it, kind, head):
                rows = slice(head * HEAD, (head + 1) * HEAD)
                first = address(sp, kind * GROUP + it * P + head * HEAD)
                sp.wait_ge(o_copied, 1 + STEPS * run(it, kind) + 4 * head + 4)
                sp.dma_start(o_dram[bass.ds(first, HEAD), :], o_stage[rows, :]
                             ).then_inc(o_stored[head], 16)

            def one_run(it, kind, project=True, more=True):
                it1, kind1 = pair_of(it, kind, 1)
                it2, kind2 = pair_of(it, kind, 2)
                if project:
                    load_weights(it1, kind1, V)
                if kind1 == DIL_KIND:
                    swap_halves(it1, kind1, 0)
                    swap_halves(it1, kind1, 1)
                if more:
                    load_weights(it2, kind2, Q)
                if kind1 == DIL_KIND:
                    swap_halves(it1, kind1, 2)
                    swap_halves(it1, kind1, 3)
                if not project:
                    for f in range(2, KT):
                        sp.wait_ge(out_w_split, f - 1)
                        load_out_weights(f)
                store_head(it, kind, 0)
                if more:
                    load_weights(it2, kind2, K)
                elif project:
                    sp.wait_ge(w_split, 2 + 6 * PAIRS)
                    load_out_weights(0)
                    load_out_weights(1)
                store_head(it, kind, 1)

            sp.sem_inc(w_split, 4)
            sp.sem_inc(w_hi_done, 2)
            sp.sem_inc(w_loaded[0], 16)
            sp.sem_inc(w_loaded[1], 16)
            load_weights(0, 0, V)
            sp.wait_ge(b.x_stored, 16 * TT)
            for dst, src in ((neg_f, neg_mask), (log_count_sb, log_count), (cos_sb, cos), (sin_sb, sin)):
                sp.dma_start(dst[:, :], src[:, :]).then_inc(tables_loaded, 16)
            load_weights(0, 1, Q)
            load_weights(0, 1, K)
            sp.sem_inc(o_stored[0], 16)
            sp.sem_inc(o_stored[1], 16)
            with sp.Fori(0, PAIRS - 1) as it:
                one_run(it, SB_KIND)
                one_run(it, DIL_KIND)
            one_run(PAIRS - 1, SB_KIND, more=False)
            one_run(PAIRS - 1, DIL_KIND, project=False, more=False)
            for h in range(2):
                sp.wait_ge(o_stored[h], 16 * (2 * PAIRS + 1))

        @block.gpsimd
        def _(pool):
            def products(it, s):
                for a in range(2):
                    nk = P * (2 * (s % 4) + a + 1)
                    beta = weight[s % 2][a][:, SEQ - nk:SEQ]
                    pool.wait_ge(products_ready, 2 * STEPS * it + 2 * s + a + 1)
                    pool.tensor_tensor(beta, beta, stay[s % 2][a][:, SEQ - nk + 1:SEQ + 1], ALU.mult
                                       ).then_inc(sb_weights, 1)

            def split_weights(it, kind, piece):
                n = 3 * kind + piece
                slot = n % 2
                pool.wait_ge(w_hi_done, 6 * it + n + 1)
                pool.tensor_tensor(w_lo[slot][:, :, :], w_raw[slot][:, :, :], w_hi[slot][:, :, :].bitcast(F32),
                                   ALU.subtract).then_inc(w_split, 1)

            def rotate_cos(it, j):
                half = PRODUCTS[j][1]
                n = ROTATED * it + j
                pool.wait_ge(proj_free, 1 + HALVES * run(it, DIL_KIND) + j + 1)
                pool.wait_ge(rot_split, 1 + n)
                pool.tensor_tensor(rot_out[:, :], rot_in[:, :], cos_sb[:, half * HALF:(half + 1) * HALF],
                                   ALU.mult).then_inc(rot_cos, 1)

            def step(it, kind, s, project=True, last=False):
                it1, kind1 = pair_of(it, kind, 1)
                if s < STEPS - 1:
                    if kind == SB_KIND:
                        products(it, s + 1)
                elif not last and kind1 == SB_KIND:
                    products(it1, 0)
                if project and kind1 == DIL_KIND and ENDS.get(s, HALVES) < ROTATED:
                    rotate_cos(it1, ENDS[s])
                if project and s == 0:
                    split_weights(it1, kind1, K)
                if project and ENDS.get(s) == 2:
                    split_weights(it1, kind1, V)
                if more_after(it, project) and ENDS.get(s) == 3:
                    split_weights(*pair_of(it, kind, 2), Q)

            def split_out_weights(f):
                raw = b.w_raw[:, f % 2, :, :].rearrange("p k c -> p (k c)")
                pool.wait_ge(out_w_hi_done, f + 1)
                pool.tensor_tensor(raw, raw, group_gain[:, f:f + 1].to_broadcast([P, D]), ALU.mult
                                   ).then_inc(out_w_gained, 1)
                pool.wait_ge(out_w_gained, f + 1)
                pool.tensor_tensor(norm.xn_lo[:, f, :], raw, norm.xn_hi[:, f, :].bitcast(F32), ALU.subtract
                                   ).then_inc(out_w_split, 1)

            def one_run(it, kind, project=True, last=False):
                for s in range(STEPS):
                    step(it, kind, s, project, last)
                    if last:
                        split_out_weights(s)

            split_weights(0, 0, V)
            split_weights(0, 1, Q)
            pool.wait_ge(tables_ready, 1)
            products(0, 0)
            with pool.Fori(0, PAIRS - 1) as it:
                one_run(it, SB_KIND)
                one_run(it, DIL_KIND)
            one_run(PAIRS - 1, SB_KIND)
            one_run(PAIRS - 1, DIL_KIND, project=False, last=True)

        @block.scalar
        def _(act):
            def split_weights(it, kind, piece):
                n = 3 * kind + piece
                slot = n % 2
                act.wait_ge(w_loaded[slot], 16 * (3 * it + n // 2 + 1))
                done = {Q: -2, K: 0, V: 3}[piece]
                if not (piece != V and isinstance(it, int) and run(it, kind) == 0):
                    act.wait_ge(proj_ready, 1 + HALVES * run(it, kind) + done)
                act.activation(w_hi[slot][:, :, :], w_raw[slot][:, :, :], ACT.Copy).then_inc(w_hi_done, 1)

            def gates(it, s, a):
                nk = P * (2 * (s % 4) + a + 1)
                keys = slice(SEQ - nk, SEQ)
                act.wait_ge(z_ready, 1 + 2 * STEPS * run(it, SB_KIND) + 2 * s + a + 1)
                if not (isinstance(it, int) and it == 0 and s == 0):
                    act.wait_ge(turned, stage_free(it, SB_KIND, s))
                act.activation(weight[s % 2][a][:, keys], z[a][:, 0:nk], ACT.Sigmoid, scale=SCALE)
                act.activation(stay[s % 2][a][:, keys], z[a][:, 0:nk], ACT.Sigmoid, scale=-SCALE
                               ).then_inc(gates_ready, 1)

            def exponentials(it, s, a):
                nk = P * (2 * (s % 4) + a + 1)
                keys = slice(SEQ - nk, SEQ)
                c = 2 * (s % 2) + a
                act.wait_ge(dil_negmax, 2 * STEPS * it + 2 * s + a + 1)
                act.activation(weight[s % 2][a][:, keys], weight[s % 2][a][:, keys], ACT.Exp, scale=SCALE,
                               bias=neg_max[:, c:c + 1], accum_out=row_sum[:, c:c + 1]).then_inc(dil_exp, 1)

            def elementwise(it, kind, s, a):
                if kind == SB_KIND:
                    gates(it, s, a)
                else:
                    exponentials(it, s, a)

            def weights_hi(it, kind, s, j, v_turn):
                n = 1 + TURNS * run(it, kind) + turn_index(s, j, v_turn)
                bank = BANK_TURN + turn_index(s, j, v_turn) % 2
                act.wait_ge(pv_ready, BANKS * run(it, kind) + bank_count(s) + j + 1)
                act.wait_ge(turned, n + 1)
                for dst, cols in turn_parts(wt_hi, s, j):
                    last = act.activation(dst, b.ps[:, bank, cols], ACT.Copy)
                last.then_inc(turn_hi_done, 1)

            def v_hi_part(it, kind, half, n, bank):
                act.wait_ge(turned, n + 1)
                act.activation(v_both[kind][:, 4 * half:4 * half + 4, :, 0:HEAD],
                               b.ps[:, bank, :].rearrange("p (t h c) -> p t h c", h=2, c=HEAD), ACT.Copy
                               ).then_inc(turn_hi_done, 1)

            def projected(it, kind, j, bank=BANK_PROJ):
                piece, half = PRODUCTS[j]
                cols = slice(half * HALF, (half + 1) * HALF)
                act.wait_ge(proj_ready, 1 + HALVES * run(it, kind) + j + 1)
                if piece == V:
                    act.activation(v_turned[:, :], b.ps[:, bank, :], ACT.Copy).then_inc(proj_free, 1)
                elif kind == SB_KIND:
                    act.activation(qk_hi[kind][piece][:, cols], b.ps[:, bank, :], ACT.Copy
                                   ).then_inc(sb_hi_done, 1)
                else:
                    act.wait_ge(rot_split, 1 + ROTATED * it + j)
                    act.activation(rot_in[:, :], b.ps[:, bank, :], ACT.Copy).then_inc(proj_free, 1)

            def split_out_weights(f):
                if f == 0:
                    act.wait_ge(proj_ready, 1 + HALVES * 2 * PAIRS)
                act.wait_ge(out_w_loaded[f % 2], 16 * (f // 2 + 1))
                act.activation(norm.xn_hi[:, f, :], b.w_raw[:, f % 2, :, :].rearrange("p k c -> p (k c)"), ACT.Copy,
                               scale=group_gain[:, f:f + 1]).then_inc(out_w_hi_done, 1)

            def rotated_hi(it, j):
                piece, half = PRODUCTS[j]
                act.wait_ge(rot_sum, ROTATED * it + j + 1)
                act.activation(qk_hi[DIL_KIND][piece][:, half * HALF:(half + 1) * HALF], rot_out[:, :],
                               ACT.Copy).then_inc(rot_hi_done, 1)

            def values_low(it, kind, s):
                act.wait_ge(pv_ready, 4 + BANKS * run(it, kind) + bank_count(s + 1))
                act.activation(o_low[:, :], b.ps[HEAD:P, BANK_PV, 0:QG], ACT.Copy
                               ).then_inc(o_low_done, 1)

            def step(it, kind, s, project=True, last=False):
                it1, kind1 = pair_of(it, kind, 1)
                nit, nkind, ns = (it, kind, s + 1) if s < STEPS - 1 else (it1, kind1, 0)
                ahead = not (last and s == STEPS - 1)
                leads = nkind == SB_KIND
                if ahead and leads:
                    elementwise(nit, nkind, ns, 0)
                if v_turned_in(it, kind, s, project):
                    i = turn_index(s, -1, True)
                    v_hi_part(*v_turned_in(it, kind, s, project), 1 + TURNS * run(it, kind) + i, BANK_TURN + i % 2)
                for j in range(s % 4 + 1):
                    weights_hi(it, kind, s, j, project)
                    if values_done(it, kind, s, j):
                        values_low(*values_done(it, kind, s, j))
                    if ahead and not leads and j == 0:
                        elementwise(nit, nkind, ns, 0)
                    if ahead and j == (0 if leads else min(1, s % 4)):
                        elementwise(nit, nkind, ns, 1)
                if project and kind1 == DIL_KIND and ENDS.get(s - 1, HALVES) < ROTATED:
                    rotated_hi(it1, ENDS[s - 1])
                if project and s in ENDS:
                    projected(it1, kind1, ENDS[s])
                if project and s == 0:
                    split_weights(it1, kind1, K)
                if project and ENDS.get(s) == 2:
                    split_weights(it1, kind1, V)
                if more_after(it, project) and ENDS.get(s) == 3:
                    split_weights(*pair_of(it, kind, 2), Q)
                if last:
                    split_out_weights(s)
                if last and s == STEPS - 1:
                    values_low(it, kind, s)

            def one_run(it, kind, first=0, end=STEPS, project=True, last=False):
                for s in range(first, end):
                    step(it, kind, s, project, last)

            norm.hi_part(act, 2, 0)
            for j in range(HALVES):
                projected(0, 0, j, first_bank(j))
                if j == 0:
                    norm.hi_part(act, 3, 0)
                if j == 2:
                    split_weights(0, 0, V)
                if j == 3:
                    split_weights(0, 1, Q)
                if j == 4:
                    v_hi_part(0, 0, 0, 0, BANK_TURN + 1)
            elementwise(0, SB_KIND, 0, 0)
            elementwise(0, SB_KIND, 0, 1)
            one_run(0, SB_KIND, 0, 2)
            with act.Fori(0, PAIRS - 1) as it:
                one_run(it, SB_KIND, 2)
                one_run(it, DIL_KIND)
                one_run(it + 1, SB_KIND, 0, 2)
            one_run(PAIRS - 1, SB_KIND, 2)
            one_run(PAIRS - 1, DIL_KIND, project=False, last=True)

        @block.vector
        def _(dve):
            def scan(it, s, a):
                nk = P * (2 * (s % 4) + a + 1)
                dve.wait_ge(gates_ready, 2 * STEPS * it + 2 * s + a + 1)
                back = stay[s % 2][a][:, SEQ - nk:SEQ][:, ::-1]
                dve.tensor_tensor_scan(back, back, back, 1.0, ALU.mult, ALU.min).then_inc(products_ready, 1)

            def masked_max(it, s, a):
                i = 2 * (s % 4) + a
                nk = P * (i + 1)
                keys = slice(SEQ - nk, SEQ)
                c = 2 * (s % 2) + a
                dve.wait_ge(z_ready, 1 + 2 * STEPS * run(it, DIL_KIND) + 2 * s + a + 1)
                dve.wait_ge(turned, stage_free(it, DIL_KIND, s))
                dve.wait_ge(tables_loaded, 16 * 4)
                dve.sem_inc(scores_seen, 1)
                dve.tensor_tensor_reduce(weight[s % 2][a][:, keys], z[a][:, 0:nk], log_count_sb[:, keys], 1.0,
                                         -3e38, ALU.add, ALU.max, row_max[:, c:c + 1]).then_inc(dil_max, 1)
                dve.wait_ge(dil_max, 2 * STEPS * it + 2 * s + a + 1)
                dve.tensor_scalar(neg_max[:, c:c + 1], row_max[:, c:c + 1], -SCALE, None, ALU.mult
                                  ).then_inc(dil_negmax, 1)

            def normalize(it, s, a):
                nk = P * (2 * (s % 4) + a + 1)
                keys = slice(SEQ - nk, SEQ)
                c = 2 * (s % 2) + a
                n = 2 * STEPS * it + 2 * s + a + 1
                dve.wait_ge(dil_exp, n)
                dve.reciprocal(row_inv[:, c:c + 1], row_sum[:, c:c + 1]).then_inc(dil_inv, 1)
                dve.wait_ge(dil_inv, n)
                dve.tensor_scalar(weight[s % 2][a][:, keys], weight[s % 2][a][:, keys], row_inv[:, c:c + 1], None,
                                  ALU.mult).then_inc(dil_weights, 1)

            def elementwise(it, kind, s, a):
                if kind == SB_KIND:
                    scan(it, s, a)
                else:
                    masked_max(it, s, a)

            def weights_lo(it, kind, s, j, v_turn):
                n = 1 + TURNS * run(it, kind) + turn_index(s, j, v_turn)
                bank = BANK_TURN + turn_index(s, j, v_turn) % 2
                dve.wait_ge(turn_hi_done, n + 1)
                for (dst, cols), (hi, _) in zip(turn_parts(wt_lo, s, j), turn_parts(wt_hi, s, j)):
                    last = dve.tensor_tensor(dst, b.ps[:, bank, cols], hi.bitcast(F32), ALU.subtract)
                last.then_inc(turn_split, 1)

            def v_lo_part(it, kind, half, n, bank):
                dve.wait_ge(turn_hi_done, n + 1)
                part = slice(4 * half, 4 * half + 4)
                dve.tensor_tensor(v_both[kind][:, part, :, HEAD:P],
                                  b.ps[:, bank, :].rearrange("p (t h c) -> p t h c", h=2, c=HEAD),
                                  v_both[kind][:, part, :, 0:HEAD].bitcast(F32), ALU.subtract
                                  ).then_inc(turn_split, 1)

            def values_out(it, kind, s):
                head, g = s // 4, s % 4
                rows = slice(head * HEAD, (head + 1) * HEAD)
                if g == 0:
                    dve.wait_ge(o_stored[head], 16 * (run(it, kind) + 1))
                dve.wait_ge(o_low_done, STEPS * run(it, kind) + s + 1)
                dve.tensor_tensor(o_stage[rows, g * QG:(g + 1) * QG], b.ps[0:HEAD, BANK_PV, 0:QG], o_low[:, :],
                                  ALU.add).then_inc(o_copied, 1)

            def projected_lo(it, j, bank=BANK_PROJ):
                piece, half = PRODUCTS[j]
                cols = slice(half * HALF, (half + 1) * HALF)
                dve.wait_ge(sb_hi_done, ROTATED * it + j + 1)
                dve.tensor_tensor(qk_lo[SB_KIND][piece][:, cols], b.ps[:, bank, :],
                                  qk_hi[SB_KIND][piece][:, cols].bitcast(F32), ALU.subtract
                                  ).then_inc(proj_free, 1)

            def rotate(it, j):
                half = PRODUCTS[j][1]
                cols = slice(half * HALF, (half + 1) * HALF)
                n = ROTATED * it + j
                dve.wait_ge(rot_swapped, 64 * (n + 1))
                dve.tensor_tensor(rot_swap[:, :], rot_swap[:, :], sin_sb[:, cols], ALU.mult).then_inc(rot_sin, 1)
                dve.wait_ge(rot_sin, n + 1)
                dve.wait_ge(rot_cos, n + 1)
                dve.tensor_tensor(rot_out[:, :], rot_out[:, :], rot_swap[:, :], ALU.add).then_inc(rot_sum, 1)

            def rotated_lo(it, j):
                piece, half = PRODUCTS[j]
                cols = slice(half * HALF, (half + 1) * HALF)
                dve.wait_ge(rot_hi_done, ROTATED * it + j + 1)
                dve.tensor_tensor(qk_lo[DIL_KIND][piece][:, cols], rot_out[:, :],
                                  qk_hi[DIL_KIND][piece][:, cols].bitcast(F32), ALU.subtract
                                  ).then_inc(rot_split, 1)

            def step(it, kind, s, project=True, last=False):
                it1, kind1 = pair_of(it, kind, 1)
                nit, nkind, ns = (it, kind, s + 1) if s < STEPS - 1 else (it1, kind1, 0)
                ahead = not (last and s == STEPS - 1)
                rot = None
                if project and kind1 == DIL_KIND and ENDS.get(s - 1, HALVES) < ROTATED:
                    rot = (it1, ENDS[s - 1])
                leads = nkind == DIL_KIND
                if ahead and leads:
                    elementwise(nit, nkind, ns, 0)
                if v_turned_in(it, kind, s, project):
                    i = turn_index(s, -1, True)
                    v_lo_part(*v_turned_in(it, kind, s, project), 1 + TURNS * run(it, kind) + i, BANK_TURN + i % 2)
                for j in range(s % 4 + 1):
                    weights_lo(it, kind, s, j, project)
                    if values_done(it, kind, s, j):
                        values_out(*values_done(it, kind, s, j))
                    if ahead and not leads and j == 0:
                        elementwise(nit, nkind, ns, 0)
                    if ahead and j == (0 if leads else min(1, s % 4)):
                        elementwise(nit, nkind, ns, 1)
                    if j == min(ROTATE_BEHIND, s % 4) and rot:
                        rotate(*rot)
                if ahead and nkind == DIL_KIND:
                    normalize(nit, ns, 0)
                    normalize(nit, ns, 1)
                if rot:
                    rotated_lo(*rot)
                if project and kind1 == SB_KIND and ENDS.get(s, HALVES) < ROTATED:
                    projected_lo(it1, ENDS[s])
                if last and s == STEPS - 1:
                    values_out(it, kind, s)

            def one_run(it, kind, first=0, end=STEPS, project=True, last=False):
                for s in range(first, end):
                    step(it, kind, s, project, last)

            norm.lo_part(dve, 2, 0)
            for j in range(HALVES):
                if j < ROTATED:
                    projected_lo(0, j, first_bank(j))
                if j == 0:
                    norm.lo_part(dve, 3, 0)
                if j == 4:
                    v_lo_part(0, 0, 0, 0, BANK_TURN + 1)
            dve.wait_ge(tables_loaded, 16 * 4)
            dve.tensor_copy(neg_r[:, :], neg_f[:, :])
            dve.tensor_copy(ident_r[:, :], b.ident[:, :])
            for s in range(2):
                for a in range(2):
                    ones = dve.memset(stay[s][a][:, SEQ:SEQ + 1], 1.0)
            ones.then_inc(tables_ready, 1)
            elementwise(0, SB_KIND, 0, 0)
            elementwise(0, SB_KIND, 0, 1)
            one_run(0, SB_KIND, 0, 2)
            with dve.Fori(0, PAIRS - 1) as it:
                one_run(it, SB_KIND, 2)
                one_run(it, DIL_KIND)
                one_run(it + 1, SB_KIND, 0, 2)
            one_run(PAIRS - 1, SB_KIND, 2)
            one_run(PAIRS - 1, DIL_KIND, project=False, last=True)

        @block.tensor
        def _(pe):
            def project(it, kind, u0, u1, bank=BANK_PROJ, ahead=0):
                for u in range(u0, u1):
                    j, k = u // KT, u % KT
                    piece, half = PRODUCTS[j]
                    n = 3 * kind + piece
                    hi, lo = w_hi[n % 2], w_lo[n % 2]
                    cols = slice(half * HALF, (half + 1) * HALF)
                    out = b.ps[:, bank, :]
                    if k == 0:
                        pe.wait_ge(w_split, 2 + 6 * it + n + 1)
                        if not (ahead and j == 0):
                            pe.wait_ge(proj_free, 1 + HALVES * run(it, kind) + j - ahead)
                    pe.matmul(out, hi[:, k, :], norm.xn_hi[:, k, cols], start=(k == 0), stop=False)
                    pe.matmul(out, hi[:, k, :], norm.xn_lo[:, k, cols], start=False, stop=False)
                    last = pe.matmul(out, lo[:, k, :], norm.xn_hi[:, k, cols], start=False, stop=(k == KT - 1))
                    if k == KT - 1:
                        last.then_inc(proj_ready, 1)

            def scores(it, kind, s):
                head, g = s // 4, s % 4
                rows = slice(head * HEAD, (head + 1) * HEAD)
                (q_hi, k_hi), (q_lo, k_lo) = qk_hi[kind], qk_lo[kind]
                if s in (0, 2):
                    if kind == SB_KIND:
                        pe.wait_ge(proj_free, 1 + HALVES * run(it, kind) + (2 if s == 0 else 4))
                    else:
                        pe.wait_ge(rot_split, 1 + ROTATED * it + (2 if s == 0 else 4))
                for a in range(2):
                    i = 2 * g + a
                    nk = P * (i + 1)
                    if s > 0 or kind == DIL_KIND:
                        before = (it, kind, s - 1) if s > 0 else (it, SB_KIND, STEPS - 1)
                        if before[1] == SB_KIND:
                            pe.wait_ge(gates_ready, 2 * STEPS * before[0] + 2 * before[2] + a + 1)
                        else:
                            pe.wait_ge(dil_max, 2 * STEPS * before[0] + 2 * before[2] + a + 1)
                    elif not (isinstance(it, int) and it == 0):
                        pe.wait_ge(dil_max, 2 * STEPS * it - 2 + a + 1)
                    qt = slice(i * P, (i + 1) * P)
                    for c0 in range(0, nk, HALF):
                        c1 = min(nk, c0 + HALF)
                        out = z[a][:, c0:c1]
                        pe.matmul(out, q_hi[rows, qt], k_hi[rows, c0:c1], start=True, stop=False)
                        if kind == SB_KIND and c1 == nk:
                            pe.matmul(z[a][:, nk - P:nk], ident_r[:, :], neg_r[:, :], start=False, stop=False)
                        pe.matmul(out, q_hi[rows, qt], k_lo[rows, c0:c1], start=False, stop=False)
                        last = pe.matmul(out, q_lo[rows, qt], k_hi[rows, c0:c1], start=False, stop=True)
                    last.then_inc(z_ready, 1)

            def turn_weights(it, kind, s, j, v_turn):
                g = s % 4
                n = turn_index(s, j, v_turn)
                if j == 0:
                    if kind == SB_KIND:
                        pe.wait_ge(sb_weights, 2 * STEPS * it + 2 * s + 2)
                    else:
                        pe.wait_ge(dil_weights, 2 * STEPS * it + 2 * s + 2)
                pe.wait_ge(turn_split, 1 + TURNS * run(it, kind) + n - 1)
                for kk in range(2):
                    for a in range(2):
                        key, i = 2 * j + kk, 2 * g + a
                        if key > i:
                            continue
                        col = SEQ - P * (i + 1) + key * P
                        c = (2 * kk + a) * P
                        last = pe.transpose(b.ps[:, BANK_TURN + n % 2, c:c + P],
                                            weight[s % 2][a][:, col:col + P], b.ident[:, :])
                last.then_inc(turned, 1)

            def turn_v(it, kind, half, bank, before):
                pe.wait_ge(proj_free, 1 + HALVES * run(it, kind) + ROTATED + half + 1)
                if before is not None:
                    pe.wait_ge(turn_split, before)
                for t in range(4):
                    last = pe.transpose(b.ps[:, bank, t * P:(t + 1) * P], v_turned[:, t * P:(t + 1) * P],
                                        b.ident[:, :])
                last.then_inc(turned, 1)

            def weighted_values(it, kind, s, j, v_turn):
                head, g = s // 4, s % 4
                pe.wait_ge(turn_split, 1 + TURNS * run(it, kind) + turn_index(s, j, v_turn) + 1)
                if j == 0:
                    pe.wait_ge(o_copied, 1 + STEPS * run(it, kind) + s)
                for kk in range(2):
                    k, part = 2 * j + kk, wt_part(s, j) + kk
                    end = k == 2 * g + 1
                    cols = slice(P, QG) if end else slice(0, QG)
                    out, v = b.ps[:, BANK_PV, cols], v_both[kind][:, k, head, :]
                    pe.matmul(out, v, wt_hi[:, part, cols], start=(k == 0), stop=False)
                    last = pe.matmul(out, v, wt_lo[:, part, cols], start=False, stop=end)
                last.then_inc(pv_ready, 1)

            def values_behind(it, kind, s, j, n):
                bank = banks_back(it, kind, s, j, n)
                if bank:
                    it0, kind0, s0, _ = bank
                    weighted_values(*bank, not (isinstance(it0, int) and it0 == PAIRS - 1 and kind0 == DIL_KIND))

            def step(it, kind, s, proj=True, last=False):
                it1, kind1 = pair_of(it, kind, 1)
                nit, nkind, ns = (it, kind, s + 1) if s < STEPS - 1 else (it1, kind1, 0)
                if not (last and s == STEPS - 1):
                    scores(nit, nkind, ns)
                if v_turned_in(it, kind, s, proj):
                    i = turn_index(s, -1, True)
                    turn_v(*v_turned_in(it, kind, s, proj), BANK_TURN + i % 2, 1 + TURNS * run(it, kind) + i - 1)
                for j in range(s % 4 + 1):
                    if proj:
                        project(it1, kind1, *units_between(s, j))
                    turn_weights(it, kind, s, j, proj)
                    values_behind(it, kind, s, j, 2)
                if proj:
                    project(it1, kind1, *units_between(s, s % 4 + 1))
                if last and s == STEPS - 1:
                    values_behind(it, kind, s, s % 4, 1)
                    values_behind(it, kind, s, s % 4, 0)

            def one_run(it, kind, first=0, end=STEPS, proj=True, last=False):
                for s in range(first, end):
                    step(it, kind, s, proj, last)

            pe.sem_inc(proj_free, 1)
            pe.sem_inc(proj_ready, 1)
            pe.sem_inc(pv_ready, 4)
            pe.sem_inc(o_copied, 1)
            pe.sem_inc(rot_split, 1)
            pe.sem_inc(z_ready, 1)
            norm.turn(pe, 2, 0)
            for j in range(HALVES):
                if j == 2:
                    pe.wait_ge(norm.lo, 16)
                project(0, 0, KT * j, KT * (j + 1), first_bank(j), 1)
                if j == 0:
                    norm.turn(pe, 3, 0, 12)
                if j == ROTATED:
                    turn_v(0, 0, 0, BANK_TURN + 1, None)
            pe.wait_ge(tables_ready, 1)
            scores(0, SB_KIND, 0)
            one_run(0, SB_KIND, 0, 2)
            with pe.Fori(0, PAIRS - 1) as it:
                one_run(it, SB_KIND, 2)
                one_run(it, DIL_KIND)
                one_run(it + 1, SB_KIND, 0, 2)
            one_run(PAIRS - 1, SB_KIND, 2)
            one_run(PAIRS - 1, DIL_KIND, proj=False, last=True)


def stage_free(it, kind, s):
    v_turn = not (isinstance(it, int) and it == PAIRS - 1 and kind == DIL_KIND)
    if s < 2:
        n = turn_index(s + STEPS - 2, (s - 2) % 4, True) + 1 - TURNS
    else:
        n = turn_index(s - 2, (s - 2) % 4, v_turn) + 1
    return 1 + TURNS * (2 * it + kind) + n


def more_after(it, project):
    return project and not (isinstance(it, int) and it == PAIRS - 1)


def turn_parts(dst, s, j):
    part = wt_part(s, j)
    if j < s % 4:
        return [(dst[:, part:part + 2, :], slice(0, 2 * QG))]
    return [(dst[:, part, :], slice(0, QG)), (dst[:, part + 1, P:QG], slice(QG + P, 2 * QG))]



OQ = 256


def output_block(nc, b, sem, next_norm, w_split_buffers, o_split_buffers, o_dram, x_dram, next_weights):
    with ExitStack() as ctx:
        def sb(name, shape, dt=F32):
            return ctx.enter_context(nc.sbuf_tensor(f"out_{name}", shape, dt))

        (w_hi, w_lo), (o_hi, o_lo) = w_split_buffers, o_split_buffers
        o_raw = [b.scaled[:, i, :].rearrange("p (f c) -> p f c", c=OQ) for i in range(4)]
        o_sq = sb("o_sq", [P, KT, OQ])
        squares = [sb(f"squares{i}", [P, D])[:, :] for i in range(2)]
        ones = sb("ones", [P, 1])
        root, rstd = sb("root", [P, 2 * TT]), sb("rstd", [P, 2 * TT])
        o_loaded = [sem(f"out_o_loaded{i}") for i in range(4)]
        w_loaded = [sem(f"out_next_w_loaded{i}") for i in range(CH)]
        x_loaded = [sem(f"out_x_loaded{t}") for t in range(TT)]
        o_hi_done, o_split, o_squared = sem("out_o_hi_done"), sem("out_o_split"), sem("out_o_squared")
        w_hi_done, o_halved, o_folded = sem("out_next_w_hi_done"), sem("out_o_halved"), sem("out_o_folded")
        ones_set, sums_ready, root_done, rstd_done = (sem(f"out_{n}") for n in ("ones", "sums", "root", "rstd"))
        y_ready, y_added = sem("out_y_ready"), sem("out_y_added")
        block = ctx.enter_context(nc.Block())
        BANK_NORM = 3
        QUARTERS = SEQ // OQ
        BANK_SUM = (7, 4, 5, 6)
        SUMS_BEHIND = {1: 0, 3: 1, 9: 2, 15: 3}

        def features(group):
            return slice(group * (KT // 2), (group + 1) * (KT // 2))

        COLS = 2 * OQ // P

        @block.sync
        def _(sp):
            def load_o(q):
                for group in range(2):
                    n = 2 * q + group
                    if n >= 4:
                        sp.wait_ge(o_split, n - 3)
                        sp.wait_ge(o_squared, n - 3)
                    sp.dma_start(o_raw[n % 4], o_dram[group * GROUP:(group + 1) * GROUP, q * OQ:(q + 1) * OQ]
                                 .rearrange("(f p) c -> p f c", p=P)).then_inc(o_loaded[n % 4], 16)

            def load_x(tiles):
                for t in tiles:
                    sp.dma_start(b.x[:, t, :], x_dram[t * P:(t + 1) * P, :]).then_inc(x_loaded[t], 16)

            load_o(0)
            load_x(range(2))
            load_o(1)
            load_x(range(2, 4))
            load_o(2)
            load_o(3)
            load_x(range(4, TT))
            for t in range(CH):
                sp.dma_start(b.w_raw[:, t, :, :], next_weights[t * P:(t + 1) * P, :].rearrange(
                    "p (k c) -> p k c", k=KT)).then_inc(w_loaded[t], 16)

        @block.gpsimd
        def _(pool):
            for n in range(2 * QUARTERS):
                first = n % 2 * (KT // 2)
                pool.wait_ge(o_squared, n + 1)
                pool.tensor_tensor(o_sq[:, first:first + 2, :], o_sq[:, first:first + 2, :],
                                   o_sq[:, first + 2:first + 4, :], ALU.add).then_inc(o_halved, 1)
                pool.wait_ge(o_halved, n + 1)
                pool.tensor_tensor(o_sq[:, first, :], o_sq[:, first, :], o_sq[:, first + 1, :], ALU.add
                                   ).then_inc(o_folded, 1)

        @block.scalar
        def _(act):
            def quarter(q):
                for group in range(2):
                    n = 2 * q + group
                    act.wait_ge(o_loaded[n % 4], 16 * (q // 2 + 1))
                    act.activation(o_hi[:, features(group), q * OQ:(q + 1) * OQ], o_raw[n % 4], ACT.Copy
                                   ).then_inc(o_hi_done, 1)
                for group in range(2):
                    n = 2 * q + group
                    if q > 0:
                        act.wait_ge(sums_ready, q)
                    act.activation(o_sq[:, features(group), :], o_raw[n % 4], ACT.Square).then_inc(o_squared, 1)

            def roots(q):
                act.wait_ge(sums_ready, q + 1)
                act.activation(root[:, q * COLS:(q + 1) * COLS], b.ps[:, BANK_SUM[q], 0:COLS], ACT.Sqrt,
                               scale=1.0 / GROUP, bias=b.eps[:, 0:1]).then_inc(root_done, 1)

            quarter(0)
            roots(0)
            quarter(1)
            for t in range(TT):
                if t in (1, 3):
                    roots(t // 2 + 1)
                    quarter(t // 2 + 2)
                if t == 4:
                    roots(3)
                    for i in range(CH):
                        act.wait_ge(w_loaded[i], 16)
                        act.activation(b.w_hi[i][:, :, :], b.w_raw[:, i, :, :], ACT.Copy).then_inc(w_hi_done, 1)
                act.wait_ge(y_added, 4 * t + 4)
                next_norm.row_root(act, b.x, t, squares)
                if t in NORM_ROUNDS:
                    next_norm.hi_part(act, NORM_ROUNDS[t], BANK_NORM)

        @block.vector
        def _(dve):
            def quarter(q):
                tok = slice(q * OQ, (q + 1) * OQ)
                for group in range(2):
                    n = 2 * q + group
                    dve.wait_ge(o_hi_done, n + 1)
                    dve.tensor_tensor(o_lo[:, features(group), tok], o_raw[n % 4],
                                      o_hi[:, features(group), tok].bitcast(F32), ALU.subtract
                                      ).then_inc(o_split, 1)

            def reciprocals(q):
                cols = slice(q * COLS, (q + 1) * COLS)
                dve.wait_ge(root_done, q + 1)
                dve.reciprocal(rstd[:, cols], root[:, cols]).then_inc(rstd_done, 1)

            dve.memset(ones[:, :], 1.0).then_inc(ones_set, 1)
            quarter(0)
            reciprocals(0)
            quarter(1)
            for t in range(TT):
                if t in (1, 3):
                    reciprocals(t // 2 + 1)
                    quarter(t // 2 + 2)
                    dve.wait_ge(o_squared, 2 * (t // 2 + 3))
                if t == 5:
                    reciprocals(3)
                if t == 4:
                    for i in range(CH):
                        dve.wait_ge(w_hi_done, i + 1)
                        dve.tensor_tensor(b.w_lo[i][:, :, :], b.w_raw[:, i, :, :], b.w_hi[i][:, :, :].bitcast(F32),
                                          ALU.subtract)
                rows_before(next_norm, dve, b.x, t)
                dve.wait_ge(x_loaded[t], 16)
                if t % 2 == 0:
                    dve.wait_ge(rstd_done, t // 2 + 1)
                for half in range(2):
                    cols = slice(half * HALF, (half + 1) * HALF)
                    for group in range(2):
                        m = 4 * t + 2 * half + group
                        dve.wait_ge(y_ready, m + 1)
                        if group == 1:
                            dve.wait_ge(y_added, m)
                        dve.scalar_tensor_tensor(out=b.x[:, t, cols], in0=b.ps[:, m % 3, :],
                                                 scalar=rstd[:, 2 * t + group:2 * t + group + 1],
                                                 in1=b.x[:, t, cols], op0=ALU.mult, op1=ALU.add
                                                 ).then_inc(y_added, 1)
                if t in NORM_ROUNDS:
                    next_norm.lo_part(dve, NORM_ROUNDS[t], BANK_NORM)
            rows_before(next_norm, dve, b.x, TT)

        @block.tensor
        def _(pe):
            def sums(q):
                pe.wait_ge(o_folded, 2 * q + 2)
                for tt in range(OQ // P):
                    for group in range(2):
                        c = 2 * tt + group
                        last = pe.matmul(b.ps[:, BANK_SUM[q], c:c + 1],
                                         o_sq[:, group * (KT // 2), tt * P:(tt + 1) * P], ones[:, :],
                                         start=(c == 0), stop=True, skip_group_check=True)
                last.then_inc(sums_ready, 1)

            pe.wait_ge(ones_set, 1)
            for t in range(TT):
                tok = slice(t * P, (t + 1) * P)
                for half in range(2):
                    cols = slice(half * HALF, (half + 1) * HALF)
                    for group in range(2):
                        m = 4 * t + 2 * half + group
                        out = b.ps[:, m % 3, :]
                        pe.wait_ge(o_split, 2 * (t // 2) + group + 1)
                        if m >= 3:
                            pe.wait_ge(y_added, m - 2)
                        for i in range(KT // 2):
                            f = group * (KT // 2) + i
                            pe.matmul(out, o_hi[:, f, tok], w_hi[:, f, cols], start=(i == 0), stop=False)
                            pe.matmul(out, o_hi[:, f, tok], w_lo[:, f, cols], start=False, stop=False)
                            last = pe.matmul(out, o_lo[:, f, tok], w_hi[:, f, cols], start=False,
                                             stop=(i == KT // 2 - 1))
                        last.then_inc(y_ready, 1)
                        if m in SUMS_BEHIND:
                            sums(SUMS_BEHIND[m])
                if t in NORM_ROUNDS:
                    if NORM_ROUNDS[t] == 0:
                        pe.wait_ge(root_done, QUARTERS)
                    next_norm.turn(pe, NORM_ROUNDS[t], BANK_NORM, 4 * NORM_ROUNDS[t])



class Buffers:
    pass


def constants():
    half = HEAD // 2
    inv_freq = np.float32(10000.0) ** (-np.arange(half, dtype=np.float32) / np.float32(half))
    ang = (np.arange(SEQ, dtype=np.float32)[None, :] * inv_freq[:, None]).astype(np.float32).astype(np.float64)
    cos, sin = np.cos(ang).astype(np.float32), np.sin(ang).astype(np.float32)
    cos_rows = np.concatenate([cos] * 4)
    sin_rows = np.concatenate([-sin, sin] * 2)
    ident = np.eye(P, dtype=np.float32)
    neg = np.where(np.arange(P)[None, :] < np.arange(P)[:, None], 0.0, NEG).astype(np.float32)
    dist = (SEQ - P) + np.arange(P)[:, None] - np.arange(SEQ)[None, :]
    count = np.zeros((P, SEQ))
    for window, dilation in ((128, 1), (512, 4), (2048, 16)):
        count += (dist >= 0) & (dist <= window) & (dist % dilation == 0)
    log_count = np.where(count > 0, np.log(np.maximum(count, 1.0)) / SCALE, NEG).astype(np.float32)
    return {"ident_c": ident, "neg_c": neg, "log_count_c": log_count, "cos_c": cos_rows, "sin_c": sin_rows}


def build(nc, a, out):
    x_dram = nc.dram_tensor("x_between", [SEQ, D], F32, kind="Internal").ap()
    o_dram = nc.dram_tensor("o_between", [D, SEQ], F32, kind="Internal").ap()
    with ExitStack() as ctx:
        def sem(name):
            return ctx.enter_context(nc.semaphore(name))

        def sb(name, shape, dt=F32):
            return ctx.enter_context(nc.sbuf_tensor(name, shape, dt))

        b = Buffers()
        b.ps = ctx.enter_context(nc.psum_tensor("banks", [P, 8, HALF], F32))
        b.ident = sb("ident_sb", [P, P])
        gains = sb("gains_sb", [P, 4, KT])
        b.eps, b.sumsq, b.root, b.rstd = sb("eps", [P, 1]), sb("sumsq", [P, TT]), sb("root", [P, TT]), sb("rstd", [P, TT])
        b.scaled = sb("scaled_rows", [P, 4, D])
        b.w_raw = sb("w_raw", [P, CH, KT, P])
        b.w_hi = [sb(f"w_hi{t}", [P, KT, P], F32R) for t in range(CH)]
        b.w_lo = [sb(f"w_lo{t}", [P, KT, P], F32R) for t in range(CH)]
        first_pair = [sb(f"first_{n}", [P, KT, SEQ], F32R) for n in ("hi", "lo")]
        b.constants_loaded, b.eps_set = sem("constants_loaded"), sem("eps_set")
        b.constants = [(b.ident[:, :], a["ident_c"])] + [
            (gains[:, i, :], a[name]) for i, name in enumerate(("ffn1_norm", "mix_norm", "group_norm", "ffn2_norm"))]
        ffn1_norm = Norm(sem, "ffn1_norm", b, gains[:, 0, :], *first_pair)
        mix_norm = Norm(sem, "mix_norm", b, gains[:, 1, :], *first_pair)
        with (nc.sbuf_tensor("x_first", [P, TT, D], F32) as x_first,
              nc.sbuf_tensor("ffn1_hi", [P, KT, SEQ], F32R) as arena_hi,
              nc.sbuf_tensor("ffn1_lo", [P, KT, SEQ], F32R) as arena_lo):
            b.x = x_first
            ffn_block(nc, b, sem, "ffn1", (a["ffn1_w_gate"], a["ffn1_w_up"], a["ffn1_w_down"]), ffn1_norm, mix_norm,
                      (arena_hi, arena_lo), x_dram, x_from=a["x"], next_weights=a["w_in"])
        heads_block(nc, b, sem, mix_norm, a["w_in"], a["neg_c"], a["log_count_c"], a["cos_c"], a["sin_c"], o_dram,
                    a["w_out"], gains[:, 2, :])
        with (nc.sbuf_tensor("x_second", [P, TT, D], F32) as x_second,
              nc.sbuf_tensor("second_hi", [P, KT, SEQ], F32R) as second_hi,
              nc.sbuf_tensor("second_lo", [P, KT, SEQ], F32R) as second_lo):
            b.x = x_second
            ffn2_norm = Norm(sem, "ffn2_norm", b, gains[:, 3, :], second_hi, second_lo)
            final_norm = Norm(sem, "final_norm", b, None, None, None)
            output_block(nc, b, sem, ffn2_norm, first_pair, (second_hi, second_lo), o_dram, x_dram,
                         a["ffn2_w_gate"])
            with nc.sbuf_tensor("final_gain_sb", [P, D], F32) as b.final_gain:
                ffn_block(nc, b, sem, "ffn2", (a["ffn2_w_gate"], a["ffn2_w_up"], a["ffn2_w_down"]), ffn2_norm,
                          final_norm, first_pair, out, final_gain=a["final_norm"])


def kernel(**inputs):
    import concourse.bacc as bacc
    from concourse.bass_utils import run_bass_kernel_spmd as run

    nc = bacc.Bacc("TRN2", target_bir_lowering=False, num_devices=1, dynamic_dma_scratch_size=1024)

    def feature_tiles(v):
        return np.ascontiguousarray(v.reshape(-1, P).T)

    def column_blocks(w, width):
        return w.reshape(KT, P, -1, width).transpose(2, 1, 0, 3).reshape(-1, KT * width)

    i = {k: np.asarray(v) for k, v in inputs.items()}
    arrays = {
        "x": i["x"].reshape(SEQ, D),
        "ffn1_norm": feature_tiles(i["ffn1_norm"]),
        "mix_norm": feature_tiles(i["mix_norm"]),
        "group_norm": feature_tiles(np.concatenate([i["sb_out_norm"][0], i["dil_out_norm"][0]])),
        "ffn2_norm": feature_tiles(i["ffn2_norm"]),
        "final_norm": i["final_norm"].reshape(1, D),
        **constants(),
    }
    for name in ("ffn1_w_down", "w_out", "ffn2_w_down"):
        arrays[name] = i[name][0]
    for name in ("ffn1_w_gate", "ffn1_w_up", "ffn2_w_gate", "ffn2_w_up"):
        arrays[name] = column_blocks(i[name][0], P)
    blocks = column_blocks(i["w_in"][0], P).reshape(2, 3, PAIRS, P, D)
    arrays["w_in"] = blocks.transpose(2, 0, 1, 3, 4).reshape(-1, D)
    arrays = {f"in_{k}": np.ascontiguousarray(v) for k, v in arrays.items()}
    a = {k[3:]: nc.dram_tensor(k, v.shape, F32, kind="ExternalInput").ap() for k, v in arrays.items()}
    out = nc.dram_tensor("out_dram", [SEQ, D], F32, kind="ExternalOutput").ap()
    build(nc, a, out)
    r = run(nc, [arrays], core_ids=[0])
    return r.results[0]["out_dram"].reshape(1, SEQ, D)
```
